# Optimizing a Trainium2 kernel written in Bass

```python
import jax, jax.numpy as jnp
from jax import lax
import numpy as np
import math
import jax
import jax.numpy as jnp

D_MODEL = 1024
BATCH = 1
SEQ = 256
DEPTH = 2

MLA_HEADS = 8
MLA_NOPE = 64
MLA_ROPE = 32
MLA_V = 64
MLA_Q_RANK = 768
MLA_KV_RANK = 256
DSA_HEADS = 4
DSA_DIM = 64
IDX_HEADS = 8
IDX_DIM = 32
DSA_TOPK_MAX = 256
RET_HEADS = 4
RET_DK = 64
RET_DV = 64
RET_CHUNK = 128
D_FF = 4 * D_MODEL
ROPE_THETA = 10000.0
EPS = 1e-6
Q_BLOCK = 128

MIX_WIDTH = MLA_HEADS * MLA_V + DSA_HEADS * DSA_DIM + RET_HEADS * RET_DV
MLA_COLS = (MLA_Q_RANK, MLA_KV_RANK, MLA_ROPE)
DSA_COLS = (DSA_HEADS * DSA_DIM, DSA_DIM, DSA_DIM, IDX_HEADS * IDX_DIM, IDX_DIM, IDX_HEADS)
RET_COLS = (RET_HEADS * RET_DK, RET_HEADS * RET_DK, RET_HEADS * RET_DV, RET_HEADS * RET_DV)
SPLITS = MLA_COLS + DSA_COLS + RET_COLS
IN_WIDTH = sum(SPLITS)


def rmsnorm(x, g):
    xf = x.astype(jnp.float32)
    y = xf * lax.rsqrt(jnp.mean(xf * xf, axis=-1, keepdims=True) + EPS)
    return (y * g.astype(jnp.float32)).astype(x.dtype)

def rope_tables(seq, dim):
    pos = jnp.arange(seq, dtype=jnp.float32)
    inv = ROPE_THETA ** (-jnp.arange(0, dim, 2, dtype=jnp.float32) / dim)
    ang = pos[:, None] * inv[None, :]
    return jnp.cos(ang), jnp.sin(ang)

def apply_rope(x, cos, sin):
    d2 = x.shape[-1] // 2
    x1, x2 = x[..., :d2], x[..., d2:]
    c = cos[:, None, :].astype(x.dtype)
    s = sin[:, None, :].astype(x.dtype)
    return jnp.concatenate([x1 * c - x2 * s, x1 * s + x2 * c], axis=-1)

def to_blocks(t):
    b, s = t.shape[0], t.shape[1]
    return t.reshape((b, s // Q_BLOCK, Q_BLOCK) + t.shape[2:]).swapaxes(0, 1)

def from_blocks(t):
    t = t.swapaxes(0, 1)
    return t.reshape(t.shape[0], t.shape[1] * t.shape[2], -1)

def mla_attention(q_nope, q_rope, k_nope, k_rope, v):
    S = q_nope.shape[1]
    nb = S // Q_BLOCK
    scale = (MLA_NOPE + MLA_ROPE) ** -0.5
    key_pos = jnp.arange(S)
    neg = jnp.finfo(jnp.float32).min

    def block(args):
        qn, qr, start = args
        s = jnp.einsum('bqhd,bkhd->bhqk', qn, k_nope) + jnp.einsum('bqhd,bkd->bhqk', qr, k_rope)
        s = s.astype(jnp.float32) * scale
        qpos = start + jnp.arange(Q_BLOCK)
        causal = key_pos[None, :] <= qpos[:, None]
        p = jax.nn.softmax(jnp.where(causal, s, neg), axis=-1).astype(v.dtype)
        return jnp.einsum('bhqk,bkhd->bqhd', p, v)

    starts = jnp.arange(nb, dtype=jnp.int32) * Q_BLOCK
    out = lax.map(block, (to_blocks(q_nope), to_blocks(q_rope), starts))
    return from_blocks(out)

def dsa_attention(q, k, v, q_idx, k_idx, w_idx, topk):
    S = q.shape[1]
    nb = S // Q_BLOCK
    scale = DSA_DIM ** -0.5
    key_pos = jnp.arange(S)
    neg = jnp.finfo(jnp.float32).min
    gather = jax.vmap(lambda table, idx: table[idx])

    def block(args):
        qb, qib, wb, start = args
        qpos = start + jnp.arange(Q_BLOCK)
        causal = key_pos[None, :] <= qpos[:, None]
        rel = jax.nn.relu(jnp.einsum('bqhd,bkd->bqhk', qib, k_idx))
        score = jnp.einsum('bqh,bqhk->bqk', wb, rel).astype(jnp.float32)
        score = jnp.where(causal[None], score, -jnp.inf)
        _, sel = lax.top_k(score, topk)
        valid = sel <= qpos[None, :, None]
        k_sel = gather(k, sel)
        v_sel = gather(v, sel)
        s = jnp.einsum('bqhd,bqjd->bhqj', qb, k_sel).astype(jnp.float32) * scale
        p = jax.nn.softmax(jnp.where(valid[:, None], s, neg), axis=-1).astype(v.dtype)
        return jnp.einsum('bhqj,bqjd->bqhd', p, v_sel)

    starts = jnp.arange(nb, dtype=jnp.int32) * Q_BLOCK
    out = lax.map(block, (to_blocks(q), to_blocks(q_idx), to_blocks(w_idx), starts))
    return from_blocks(out)

def retention(q, k, v, log_gamma):
    B, S, H, dk = q.shape
    dv = v.shape[-1]
    C = RET_CHUNK
    n = S // C
    qc = q.astype(jnp.float32).reshape(B, n, C, H, dk)
    kc = k.astype(jnp.float32).reshape(B, n, C, H, dk)
    vc = v.astype(jnp.float32).reshape(B, n, C, H, dv)
    pos = jnp.arange(C, dtype=jnp.float32)
    rel = pos[:, None] - pos[None, :]
    decay = jnp.where(rel[None] >= 0, jnp.exp(jnp.maximum(rel, 0.0)[None] * log_gamma[:, None, None]), 0.0)
    inner = jnp.einsum('bnqhd,bnchd->bnhqc', qc, kc) * decay[None, None]
    inner_out = jnp.einsum('bnhqc,bnche->bnqhe', inner, vc)
    zeta = jnp.exp((C - 1.0 - pos)[None, :] * log_gamma[:, None])
    chunk_state = jnp.einsum('bnchd,hc,bnche->bnhde', kc, zeta, vc)
    chunk_decay = jnp.exp(C * log_gamma)[None, :, None, None]

    def step(R, s_i):
        return R * chunk_decay + s_i, R

    R0 = jnp.zeros((B, H, dk, dv), jnp.float32)
    _, R_prev = lax.scan(step, R0, chunk_state.swapaxes(0, 1))
    R_prev = R_prev.swapaxes(0, 1)
    xi = jnp.exp((pos + 1.0)[None, :] * log_gamma[:, None])
    cross = jnp.einsum('bnqhd,bnhde,hq->bnqhe', qc, R_prev, xi)
    return (inner_out + cross).reshape(B, S, H, dv)

def head_groupnorm(x, g):
    mu = jnp.mean(x, axis=-1, keepdims=True)
    xc = x - mu
    var = jnp.mean(xc * xc, axis=-1, keepdims=True)
    return xc * lax.rsqrt(var + EPS) * g

def first_inputs(seed: int = 0) -> dict:
    key = jax.random.key(seed)
    ks = jax.random.split(key, 16)

    def nrm(k, shape, scale):
        return jax.random.normal(k, shape, jnp.float32) * scale

    def gain(k, shape):
        return 1.0 + 0.05 * jax.random.normal(k, shape, jnp.float32)

    return {
        'x': nrm(ks[0], (BATCH, SEQ, D_MODEL), 1.0),
        'g_mix': gain(ks[1], (DEPTH, D_MODEL)),
        'w_in': nrm(ks[2], (DEPTH, D_MODEL, IN_WIDTH), D_MODEL ** -0.5),
        'g_q': gain(ks[3], (DEPTH, MLA_Q_RANK)),
        'w_uq': nrm(ks[4], (DEPTH, MLA_Q_RANK, MLA_HEADS * (MLA_NOPE + MLA_ROPE)), MLA_Q_RANK ** -0.5),
        'g_kv': gain(ks[5], (DEPTH, MLA_KV_RANK)),
        'w_ukv': nrm(ks[6], (DEPTH, MLA_KV_RANK, MLA_HEADS * (MLA_NOPE + MLA_V)), MLA_KV_RANK ** -0.5),
        'g_ret': gain(ks[7], (DEPTH, RET_HEADS * RET_DV)),
        'w_out': nrm(ks[8], (DEPTH, MIX_WIDTH, D_MODEL), MIX_WIDTH ** -0.5),
        'g_mlp': gain(ks[9], (DEPTH, D_MODEL)),
        'w_ff1': nrm(ks[10], (DEPTH, D_MODEL, D_FF), D_MODEL ** -0.5),
        'w_ff2': nrm(ks[11], (DEPTH, D_FF, D_MODEL), D_FF ** -0.5),
        'g_final': gain(ks[12], (D_MODEL,)),
    }

def first_block(x, g_mix, w_in, g_q, w_uq, g_kv, w_ukv, g_ret, w_out, g_mlp, w_ff1, w_ff2, g_final):
    B, S, _ = x.shape
    topk = min(DSA_TOPK_MAX, S // 4)
    cos_r, sin_r = rope_tables(S, MLA_ROPE)
    cos_a, sin_a = rope_tables(S, DSA_DIM)
    cos_i, sin_i = rope_tables(S, IDX_DIM)
    cos_t, sin_t = rope_tables(S, RET_DK)
    log_gamma = jnp.log1p(-jnp.exp2(-5.0 - jnp.arange(RET_HEADS, dtype=jnp.float32)))
    split_at = np.cumsum(SPLITS)[:-1].tolist()
    idx_scale = (IDX_HEADS ** -0.5) * (IDX_DIM ** -0.5)

    for l in range(DEPTH):
        h = rmsnorm(x, g_mix[l])
        (cq, ckv, kr, aq, ak, av, qi, ki, wi, rq, rk, rv, rg) = jnp.split(h @ w_in[l], split_at, axis=-1)

        q = (rmsnorm(cq, g_q[l]) @ w_uq[l]).reshape(B, S, MLA_HEADS, MLA_NOPE + MLA_ROPE)
        q_nope = q[..., :MLA_NOPE]
        q_rope = apply_rope(q[..., MLA_NOPE:], cos_r, sin_r)
        kv = (rmsnorm(ckv, g_kv[l]) @ w_ukv[l]).reshape(B, S, MLA_HEADS, MLA_NOPE + MLA_V)
        k_nope, v_mla = kv[..., :MLA_NOPE], kv[..., MLA_NOPE:]
        k_rope = apply_rope(kr[:, :, None, :], cos_r, sin_r)[:, :, 0]
        o_a = mla_attention(q_nope, q_rope, k_nope, k_rope, v_mla)

        q_b = apply_rope(aq.reshape(B, S, DSA_HEADS, DSA_DIM), cos_a, sin_a)
        k_b = apply_rope(ak[:, :, None, :], cos_a, sin_a)[:, :, 0]
        q_i = apply_rope(qi.reshape(B, S, IDX_HEADS, IDX_DIM), cos_i, sin_i)
        k_i = apply_rope(ki[:, :, None, :], cos_i, sin_i)[:, :, 0]
        o_b = dsa_attention(q_b, k_b, av, q_i, k_i, wi * idx_scale, topk)

        q_c = apply_rope(rq.reshape(B, S, RET_HEADS, RET_DK), cos_t, sin_t)
        k_c = apply_rope(rk.reshape(B, S, RET_HEADS, RET_DK), cos_t, sin_t) * (RET_DK ** -0.5)
        ret = retention(q_c, k_c, rv.reshape(B, S, RET_HEADS, RET_DV), log_gamma)
        ret = head_groupnorm(ret, g_ret[l].reshape(RET_HEADS, RET_DV).astype(jnp.float32))
        o_c = (jax.nn.silu(rg.astype(jnp.float32)) * ret.reshape(B, S, RET_HEADS * RET_DV)).astype(x.dtype)

        x = x + jnp.concatenate([o_a, o_b, o_c], axis=-1) @ w_out[l]

        hf = rmsnorm(x, g_mlp[l])
        x = x + jnp.square(jax.nn.relu(hf @ w_ff1[l])) @ w_ff2[l]

    return rmsnorm(x, g_final)


DEPTH_2 = 1

ATT_PATTERNS = ((128, 1), (512, 4), (2048, 16))
N_ATT_GROUPS = 3
HEADS_PER_GROUP = 4
ATT_HEADS = N_ATT_GROUPS * HEADS_PER_GROUP
HEAD_DIM = 64
ATT_WIDTH = ATT_HEADS * HEAD_DIM
ATT_OUT_WIDTH = HEADS_PER_GROUP * HEAD_DIM
REL_BUCKETS = 32
REL_MAX_DIST = 2048
RWKV_HEADS = 8
RWKV_HEAD_DIM = 64
RWKV_WIDTH = RWKV_HEADS * RWKV_HEAD_DIM
DECAY_LORA = 64
ICLR_LORA = 64
GATE_LORA = 160
RWKV_SHIFT_WIDTH = 3 * RWKV_WIDTH + DECAY_LORA + ICLR_LORA + GATE_LORA
GN_EPS = 64e-5
N_BRANCHES = 2
IN_WIDTH_2 = 3 * ATT_WIDTH + RWKV_SHIFT_WIDTH + N_BRANCHES * D_MODEL
N_EXPERT_GROUPS = 4
EXPERTS_PER_GROUP = 8
N_EXPERTS = N_EXPERT_GROUPS * EXPERTS_PER_GROUP
TOP_K = 2
D_EXPERT = 512
ROW_BLOCK = 256
NORM_EPS = 1e-6
NEG_INF = -1e30


def rms_norm(x, gain, eps=NORM_EPS):
    xf = x.astype(jnp.float32)
    y = xf * lax.rsqrt(jnp.mean(xf * xf, axis=-1, keepdims=True) + eps)
    return (y * gain.astype(jnp.float32)).astype(x.dtype)

def t5_causal_bucket(dist):
    max_exact = REL_BUCKETS // 2
    d = jnp.maximum(dist.astype(jnp.float32), 1.0)
    large = max_exact + (jnp.log(d / max_exact) / math.log(REL_MAX_DIST / max_exact)
                         * (REL_BUCKETS - max_exact)).astype(jnp.int32)
    large = jnp.minimum(large, REL_BUCKETS - 1)
    return jnp.where(dist < max_exact, dist, large)

def dilated_window_attention(q, k, v, bias_table, window, dilation):
    B, S, H, E = q.shape
    L = S // dilation
    W = window // dilation
    n_blk = -(-L // W)
    Lp = n_blk * W

    def to_sub(t):
        return t.reshape(B, L, dilation, H, E).transpose(0, 2, 3, 1, 4)

    qb = jnp.pad(to_sub(q), ((0, 0),) * 3 + ((0, Lp - L), (0, 0))).reshape(B, dilation, H, n_blk, W, E)
    kv_pad = ((0, 0),) * 3 + ((W, Lp - L), (0, 0))

    def band(t):
        t = jnp.pad(to_sub(t), kv_pad)
        prev = t[:, :, :, :Lp].reshape(B, dilation, H, n_blk, W, E)
        cur = t[:, :, :, W:].reshape(B, dilation, H, n_blk, W, E)
        return jnp.concatenate([prev, cur], axis=4)

    kb, vb = band(k), band(v)
    qi = jnp.arange(W)[:, None]
    kj = jnp.arange(2 * W)[None, :]
    rel = qi + W - kj
    key_pos = (jnp.arange(n_blk) * W - W)[:, None, None] + kj[None]
    valid = (rel >= 0)[None] & (rel <= W)[None] & (key_pos >= 0)
    bias = bias_table[t5_causal_bucket(jnp.clip(rel, 0, W) * dilation)]
    bias = jnp.transpose(bias, (2, 0, 1)).astype(jnp.float32)[:, None]
    s = jnp.einsum('bdhnqe,bdhnke->bdhnqk', qb, kb).astype(jnp.float32) * (E ** -0.5) + bias
    s = jnp.where(valid, s, NEG_INF)
    lse = jax.nn.logsumexp(s, axis=-1)
    p = jnp.exp(s - lse[..., None])
    o = jnp.einsum('bdhnqk,bdhnke->bdhnqe', p.astype(v.dtype), vb)

    def from_sub(t):
        t = t.reshape((B, dilation, H, Lp) + t.shape[5:])[:, :, :, :L]
        t = jnp.moveaxis(t, 3, 1)
        return t.reshape((B, S, H) + t.shape[4:])

    return from_sub(o), from_sub(lse)

def wkv7_scan(r, decay, k, v, kk, a):
    B, S, H, N = r.shape

    def step(state, inp):
        r_t, w_t, k_t, v_t, kk_t, b_t = inp
        sa = jnp.einsum('bhvk,bhk->bhv', state, -kk_t)
        state = (state * w_t[:, :, None, :] + sa[..., None] * b_t[:, :, None, :]
                 + v_t[..., None] * k_t[:, :, None, :])
        return state, jnp.einsum('bhvk,bhk->bhv', state, r_t)

    xs = tuple(jnp.moveaxis(t, 1, 0) for t in (r, decay, k, v, kk, kk * a))
    _, out = lax.scan(step, jnp.zeros((B, H, N, N), jnp.float32), xs)
    return jnp.moveaxis(out, 0, 1)

def rwkv7_time_mix(p, shift_mu, w0, w_up, a0, a_up, g_up, k_k, k_a, r_k, ln_w, ln_b, w_rwkv_out):
    B, S, _ = p.shape
    H, N, C = RWKV_HEADS, RWKV_HEAD_DIM, RWKV_WIDTH
    pf = p.astype(jnp.float32)
    prev = jnp.pad(pf, ((0, 0), (1, 0), (0, 0)))[:, :-1]
    pm = pf + (prev - pf) * shift_mu
    r, k, v, xw, xa, xg = jnp.split(pm, [C, 2 * C, 3 * C, 3 * C + DECAY_LORA,
                                          3 * C + DECAY_LORA + ICLR_LORA], axis=-1)
    w_log = -jax.nn.softplus(-(w0 + jnp.tanh(xw) @ w_up)) - 0.5
    decay = jnp.exp(-jnp.exp(w_log))
    a = jax.nn.sigmoid(a0 + xa @ a_up)
    g = jax.nn.sigmoid(xg) @ g_up
    hd = lambda t: t.reshape(B, S, H, N)
    kk = hd(k * k_k)
    kk = kk / jnp.maximum(jnp.sqrt(jnp.sum(kk * kk, axis=-1, keepdims=True)), 1e-12)
    k = k * (1.0 + (a - 1.0) * k_a)
    o = wkv7_scan(hd(r), hd(decay), hd(k), hd(v), kk, hd(a))
    mu = jnp.mean(o, axis=-1, keepdims=True)
    var = jnp.mean(jnp.square(o - mu), axis=-1, keepdims=True)
    o = ((o - mu) * lax.rsqrt(var + GN_EPS)).reshape(B, S, C) * ln_w + ln_b
    bonus = jnp.sum(hd(r) * hd(k) * r_k, axis=-1, keepdims=True) * hd(v)
    o = (o + bonus.reshape(B, S, C)) * g
    return o.astype(p.dtype) @ w_rwkv_out

def hierarchical_moe(h, w_group_router, b_group_router, w_expert_router, b_expert_router,
                     w_expert_gate, w_expert_up, w_expert_down):
    B, S, D = h.shape
    T = B * S
    hf = h.reshape(T, D)
    grp_prob = jax.nn.softmax((hf @ w_group_router).astype(jnp.float32) + b_group_router, axis=-1)
    grp_p, grp_idx = lax.top_k(grp_prob, 1)
    exp_logits = ((hf @ w_expert_router).astype(jnp.float32) + b_expert_router).reshape(
        T, N_EXPERT_GROUPS, EXPERTS_PER_GROUP)
    sel_logits = jnp.take_along_axis(exp_logits, grp_idx[:, :, None], axis=1)[:, 0]
    top_p, top_i = lax.top_k(jax.nn.softmax(sel_logits, axis=-1), TOP_K)
    gates = grp_p * top_p / jnp.sum(top_p, axis=-1, keepdims=True)
    expert_id = grp_idx * EXPERTS_PER_GROUP + top_i

    A = T * TOP_K
    eid = expert_id.reshape(A).astype(jnp.int32)
    tok = jnp.arange(A, dtype=jnp.int32) // TOP_K
    gate = gates.reshape(A)
    order = jnp.argsort(eid)
    se = eid[order]
    counts = jnp.bincount(eid, length=N_EXPERTS)
    starts = jnp.cumsum(counts) - counts
    pcounts = (counts + ROW_BLOCK - 1) // ROW_BLOCK * ROW_BLOCK
    pends = jnp.cumsum(pcounts)
    pstarts = pends - pcounts
    dest = pstarts[se] + jnp.arange(A, dtype=jnp.int32) - starts[se]
    n_blocks = -(-A // ROW_BLOCK) + N_EXPERTS
    n_rows = n_blocks * ROW_BLOCK
    row_tok = jnp.full((n_rows,), T, jnp.int32).at[dest].set(tok[order])
    row_gate = jnp.zeros((n_rows,), jnp.float32).at[dest].set(gate[order])
    blk_expert = jnp.minimum(jnp.searchsorted(pends, jnp.arange(n_blocks) * ROW_BLOCK, side='right'),
                             N_EXPERTS - 1)
    h_pad = jnp.concatenate([hf, jnp.zeros((1, D), hf.dtype)], axis=0)
    xin = h_pad[row_tok].reshape(n_blocks, ROW_BLOCK, D)

    def expert_block(args):
        xb, e = args
        hid = jax.nn.silu(xb @ w_expert_gate[e]) * (xb @ w_expert_up[e])
        return hid @ w_expert_down[e]

    yb = lax.map(expert_block, (xin, blk_expert)).reshape(n_rows, D)
    y = jax.ops.segment_sum(yb.astype(jnp.float32) * row_gate[:, None], row_tok, num_segments=T + 1)[:T]
    return y.reshape(B, S, D).astype(h.dtype)

def hybrid_layer(x, norm1_gain, w_in, q_norm_gain, k_norm_gain, rel_bias_table, w_att_out,
                 shift_mu, w0, w_up, a0, a_up, g_up, k_k, k_a, r_k, ln_w, ln_b, w_rwkv_out,
                 w_out, norm2_gain, w_group_router, b_group_router, w_expert_router,
                 b_expert_router, w_expert_gate, w_expert_up, w_expert_down):
    B, S, D = x.shape
    h = rms_norm(x, norm1_gain)
    p = h @ w_in
    q, k, v, p_rwkv, p_gate = jnp.split(
        p, [ATT_WIDTH, 2 * ATT_WIDTH, 3 * ATT_WIDTH, 3 * ATT_WIDTH + RWKV_SHIFT_WIDTH], axis=-1)

    heads = lambda t: t.reshape(B, S, N_ATT_GROUPS, HEADS_PER_GROUP, HEAD_DIM)
    q = rms_norm(heads(q), q_norm_gain[:, None, :])
    k = rms_norm(heads(k), k_norm_gain[:, None, :])
    v = heads(v)
    outs, lses = [], []
    for g, (win, dil) in enumerate(ATT_PATTERNS):
        o_g, l_g = dilated_window_attention(
            q[:, :, g], k[:, :, g], v[:, :, g],
            rel_bias_table[:, g * HEADS_PER_GROUP:(g + 1) * HEADS_PER_GROUP], win, dil)
        outs.append(o_g)
        lses.append(l_g)
    wts = jax.nn.softmax(jnp.stack(lses, axis=0), axis=0)
    att = jnp.einsum('gbsh,gbshe->bshe', wts, jnp.stack(outs, axis=0).astype(jnp.float32))
    y_att = att.reshape(B, S, ATT_OUT_WIDTH).astype(x.dtype) @ w_att_out

    y_rwkv = rwkv7_time_mix(p_rwkv, shift_mu, w0, w_up, a0, a_up, g_up, k_k, k_a, r_k,
                            ln_w, ln_b, w_rwkv_out)

    gates = jax.nn.sigmoid(p_gate.astype(jnp.float32)).astype(x.dtype)
    mixed = gates[..., :D] * y_att + gates[..., D:] * y_rwkv
    x = x + mixed @ w_out

    x = x + hierarchical_moe(rms_norm(x, norm2_gain), w_group_router, b_group_router,
                             w_expert_router, b_expert_router, w_expert_gate, w_expert_up,
                             w_expert_down)
    return x

def second_inputs(seed: int = 0) -> dict:
    key = jax.random.key(seed)
    ks = jax.random.split(key, 28)
    f32 = jnp.float32
    L, D = DEPTH_2, D_MODEL
    nrm = lambda k, shape, scale: scale * jax.random.normal(k, shape, f32)
    return {
        'x': nrm(ks[0], (BATCH, SEQ, D), 1.0),
        'norm1_gain': 1.0 + nrm(ks[1], (L, D), 0.05),
        'w_in': nrm(ks[2], (L, D, IN_WIDTH_2), D ** -0.5),
        'q_norm_gain': 1.0 + nrm(ks[3], (L, N_ATT_GROUPS, HEAD_DIM), 0.05),
        'k_norm_gain': 1.0 + nrm(ks[4], (L, N_ATT_GROUPS, HEAD_DIM), 0.05),
        'rel_bias_table': nrm(ks[5], (REL_BUCKETS, ATT_HEADS), 0.5),
        'w_att_out': nrm(ks[6], (L, ATT_OUT_WIDTH, D), ATT_OUT_WIDTH ** -0.5),
        'rwkv_shift_mu': jax.random.uniform(ks[7], (L, RWKV_SHIFT_WIDTH), f32),
        'rwkv_w0': jax.random.uniform(ks[8], (L, RWKV_WIDTH), f32, -6.0, 1.0),
        'rwkv_w_up': nrm(ks[9], (L, DECAY_LORA, RWKV_WIDTH), 0.5 * DECAY_LORA ** -0.5),
        'rwkv_a0': nrm(ks[10], (L, RWKV_WIDTH), 0.1),
        'rwkv_a_up': nrm(ks[11], (L, ICLR_LORA, RWKV_WIDTH), ICLR_LORA ** -0.5),
        'rwkv_g_up': nrm(ks[12], (L, GATE_LORA, RWKV_WIDTH), GATE_LORA ** -0.5),
        'rwkv_k_k': 0.85 + nrm(ks[13], (L, RWKV_WIDTH), 0.05),
        'rwkv_k_a': 1.0 + nrm(ks[14], (L, RWKV_WIDTH), 0.05),
        'rwkv_r_k': nrm(ks[15], (L, RWKV_HEADS, RWKV_HEAD_DIM), 0.1),
        'rwkv_ln_w': 1.0 + nrm(ks[16], (L, RWKV_WIDTH), 0.05),
        'rwkv_ln_b': nrm(ks[17], (L, RWKV_WIDTH), 0.01),
        'w_rwkv_out': nrm(ks[18], (L, RWKV_WIDTH, D), RWKV_WIDTH ** -0.5),
        'w_out': nrm(ks[19], (L, D, D), D ** -0.5),
        'norm2_gain': 1.0 + nrm(ks[20], (L, D), 0.05),
        'w_group_router': nrm(ks[21], (L, D, N_EXPERT_GROUPS), D ** -0.5),
        'b_group_router': nrm(ks[22], (L, N_EXPERT_GROUPS), 0.01),
        'w_expert_router': nrm(ks[23], (L, D, N_EXPERTS), D ** -0.5),
        'b_expert_router': nrm(ks[24], (L, N_EXPERTS), 0.01),
        'w_expert_gate': nrm(ks[25], (L, N_EXPERTS, D, D_EXPERT), D ** -0.5),
        'w_expert_up': nrm(ks[26], (L, N_EXPERTS, D, D_EXPERT), D ** -0.5),
        'w_expert_down': nrm(ks[27], (L, N_EXPERTS, D_EXPERT, D), D_EXPERT ** -0.5),
    }

def second_block(x, norm1_gain, w_in, q_norm_gain, k_norm_gain, rel_bias_table, w_att_out,
              rwkv_shift_mu, rwkv_w0, rwkv_w_up, rwkv_a0, rwkv_a_up, rwkv_g_up, rwkv_k_k,
              rwkv_k_a, rwkv_r_k, rwkv_ln_w, rwkv_ln_b, w_rwkv_out, w_out, norm2_gain,
              w_group_router, b_group_router, w_expert_router, b_expert_router,
              w_expert_gate, w_expert_up, w_expert_down):
    for l in range(DEPTH_2):
        x = hybrid_layer(x, norm1_gain[l], w_in[l], q_norm_gain[l], k_norm_gain[l], rel_bias_table,
                         w_att_out[l], rwkv_shift_mu[l], rwkv_w0[l], rwkv_w_up[l], rwkv_a0[l],
                         rwkv_a_up[l], rwkv_g_up[l], rwkv_k_k[l], rwkv_k_a[l], rwkv_r_k[l],
                         rwkv_ln_w[l], rwkv_ln_b[l], w_rwkv_out[l], w_out[l], norm2_gain[l],
                         w_group_router[l], b_group_router[l], w_expert_router[l],
                         b_expert_router[l], w_expert_gate[l], w_expert_up[l], w_expert_down[l])
    return x


def setup_inputs(seed=0):
    out = dict(first_inputs(seed))
    for name, value in second_inputs(seed + 1).items():
        if name != "x":
            out[name + "_2"] = value
    return out


def reference(
    x, g_mix, w_in, g_q, w_uq, g_kv, w_ukv, g_ret, w_out, g_mlp, w_ff1, w_ff2, g_final,
    norm1_gain_2, w_in_2, q_norm_gain_2, k_norm_gain_2, rel_bias_table_2, w_att_out_2,
    rwkv_shift_mu_2, rwkv_w0_2, rwkv_w_up_2, rwkv_a0_2, rwkv_a_up_2, rwkv_g_up_2, rwkv_k_k_2,
    rwkv_k_a_2, rwkv_r_k_2, rwkv_ln_w_2, rwkv_ln_b_2, w_rwkv_out_2, w_out_2, norm2_gain_2,
    w_group_router_2, b_group_router_2, w_expert_router_2, b_expert_router_2, w_expert_gate_2,
    w_expert_up_2, w_expert_down_2,
):
    x = first_block(
        x, g_mix, w_in, g_q, w_uq, g_kv, w_ukv, g_ret, w_out, g_mlp, w_ff1, w_ff2, g_final,
    )
    return second_block(
        x, norm1_gain_2, w_in_2, q_norm_gain_2, k_norm_gain_2, rel_bias_table_2, w_att_out_2,
        rwkv_shift_mu_2, rwkv_w0_2, rwkv_w_up_2, rwkv_a0_2, rwkv_a_up_2, rwkv_g_up_2,
        rwkv_k_k_2, rwkv_k_a_2, rwkv_r_k_2, rwkv_ln_w_2, rwkv_ln_b_2, w_rwkv_out_2, w_out_2,
        norm2_gain_2, w_group_router_2, b_group_router_2, w_expert_router_2, b_expert_router_2,
        w_expert_gate_2, w_expert_up_2, w_expert_down_2,
    )


_drawn_inputs = setup_inputs


def setup_inputs(seed=0):
    import zlib

    import numpy as np

    out = dict(_drawn_inputs(seed))
    spreads = {}
    factors = {'q_norm_gain_2': 3.31,
     'k_norm_gain_2': 5.541,
     'rwkv_ln_b_2': 4.073,
     'b_group_router_2': 56.13,
     'b_expert_router_2': 3.072}
    for name, (base, spread) in spreads.items():
        noise = np.random.default_rng([zlib.crc32(name.encode()), seed]).standard_normal(out[name].shape)
        drawn = base * np.exp(spread * noise) if base else spread * noise
        out[name] = jnp.asarray(drawn.astype(out[name].dtype))
    for name, factor in factors.items():
        out[name] = (out[name] * factor).astype(out[name].dtype)
    return out
```

```python
from contextlib import ExitStack

import numpy as np
import concourse.bass as bass
import concourse.mybir as mybir
from concourse.alu_op_type import AluOpType as ALU

F32 = mybir.dt.float32
ACT = mybir.ActivationFunctionType
AX = mybir.AxisListType



def col_blocks(width):
    return [(c, min(512, width - c)) for c in range(0, width, 512)]


P = 128
SEQ, D = 256, 1024
T = SEQ // P
KD = D // P
DEPTH = 2
EPS = 1e-6
ROPE_THETA = 10000.0
MLA_H, NOPE, ROPE, MLA_V = 8, 64, 32, 64
QK = NOPE + ROPE
Q_RANK, KV_RANK = 768, 256
DSA_H, DSA_E = 4, 64
IDX_H, IDX_E = 8, 32
TOPK = min(256, SEQ // 4)
RET_H, RET_E = 4, 64
D_FF = 4 * D
(C_CQ, C_CKV, C_KR, C_AQ, C_AK, C_AV, C_QI, C_KI, C_WI, C_RQ, C_RK, C_RV, C_RG, IN_W) = np.cumsum(
    [0, Q_RANK, KV_RANK, ROPE, DSA_H * DSA_E, DSA_E, DSA_E, IDX_H * IDX_E, IDX_E, IDX_H,
     RET_H * RET_E, RET_H * RET_E, RET_H * RET_E, RET_H * RET_E]).tolist()
MASKED = -1e38
TAKEN = -3e38
FFB = D_FF // 512
GRP, HPG, ATT_E = 3, 4, 64
ATT_H = GRP * HPG
ATT_W = ATT_H * ATT_E
PATTERNS = ((128, 1), (512, 4), (2048, 16))
BUCKETS, REL_MAX = 32, 2048
RW_H, RW_E = 8, 64
RW_W = RW_H * RW_E
LORA_W, LORA_A, LORA_G = 64, 64, 160
C_R, C_K, C_V, C_XW, C_XA, C_XG, RW_IN = np.cumsum([0, RW_W, RW_W, RW_W, LORA_W, LORA_A, LORA_G]).tolist()
GN_EPS = 64e-5
GATE_W = 2 * D
EG, EPG, D_EXP = 4, 8, 512
NE = EG * EPG
PAIRS = RW_H // 2
DECAY_RATE = -float(np.exp(-0.5))
RW_BLOCKS, QKV_BLOCKS, GATE_BLOCKS = col_blocks(RW_IN), col_blocks(3 * ATT_W), col_blocks(GATE_W)
LEVELS = [2 ** i for i in range(1, 7)]
G_MIX, G_QKV, G_MLP, G_RET, N_GAIN = 0, 8, 16, 24, 26

SLOT = 4096
SLOTS = 4


IN_BLOCKS = col_blocks(IN_W)


class Units:

    def __init__(self, full, read_act, read_dve, plan):
        self.full, self.read = full, {"A": read_act, "V": read_dve}
        self.u, last, cnt = {}, {}, {"A": 0, "V": 0}
        for stage, i, bank, eng in plan:
            banks = bank if isinstance(bank, tuple) else (bank,)
            cnt[eng] += 1
            self.u[stage, i] = (len(self.u) + 1, banks, eng, cnt[eng], [last[b] for b in banks if b in last])
            for b in banks:
                last[b] = (eng, cnt[eng])
        self.n, self.cnt = len(self.u), cnt


class UnitView:

    def __init__(self, units, eng, psum, turn=None):
        self.U, self.e, self.ps, self.turn = units, eng, psum, turn
        self.issued, self.emptied = 0, {"A": 0, "V": 0}
        self.seen = {"A": 0, "V": 0, "full": 0}

    def _at(self, per_turn, k):
        return k if self.turn is None else self.turn * per_turn + k

    def full_count(self, key):
        return self.U.u[key][0] if self.turn is None else (self.turn + 1) * self.U.n + self.U.u[key][0]

    def bank(self, key):
        banks = self.U.u[key][1]
        return self.ps[:, banks[0]:banks[-1] + 1, :].rearrange("p b w -> p (b w)")

    def begin(self, key):
        prev = self.U.u[key][4]
        for eng in "AV":
            self._wait_count(eng, max((c for e, c in prev if e == eng), default=0))
        return self.bank(key)

    def _wait_count(self, eng, idx):
        if idx > self.seen[eng]:
            self.seen[eng] = idx
            self.e.wait_ge(self.U.read[eng], self._at(self.U.cnt[eng], idx))

    def finish(self, key, ins):
        self.issued += 1
        assert self.U.u[key][0] == self.issued, (key, self.issued)
        ins.then_inc(self.U.full, 1)

    def wait_full(self, key):
        if self.U.u[key][0] > self.seen["full"]:
            self.seen["full"] = self.U.u[key][0]
            self.e.wait_ge(self.U.full, self.full_count(key))
        return self.bank(key)

    def emptied_by(self, key, ins, eng):
        n, bank, want, idx, _ = self.U.u[key]
        self.emptied[eng] += 1
        assert want == eng and idx == self.emptied[eng], (key, want, eng, idx, self.emptied)
        ins.then_inc(self.U.read[eng], 1)

    def wait_emptied(self, *keys):
        for eng in "AV":
            idx = [self.U.u[key][3] for key in keys if self.U.u[key][2] == eng]
            if idx:
                self._wait_count(eng, max(idx))


class Signal:

    def __init__(self, sem, per_turn):
        self.sem, self.per_turn = sem, per_turn

    def wait(self, eng, k, turn=None):
        eng.wait_ge(self.sem, k if turn is None else turn * self.per_turn + k)


class WeightRing:

    def __init__(self, loaded, blocks, first_slot=0):
        self.loaded, self.blocks = loaded, blocks
        self.where, per = {}, [0] * SLOTS
        held = {}
        self.prev = {}
        for j, (name, release) in enumerate(blocks):
            s = (first_slot + j) % SLOTS
            per[s] += 1
            self.where[name] = (s, per[s])
            self.prev[name] = held.get(s)
            held[s] = release
        self.per, self.last = per, held
        self.next_slot = (first_slot + len(blocks)) % SLOTS


def interleave(stage, n, banks, engs):
    return [(stage, i, banks[i % len(banks)], engs[i % len(engs)]) for i in range(n)]


GROUPS = [(False, t, tuple(range(h, h + 4 // (t + 1)))) for t in range(T) for h in range(0, MLA_H, 4 // (t + 1))] + \
         [(True, t, (h, h + 2)) for t in range(T) for h in range(2)]
NG = len(GROUPS)
IDX_UNITS = [(t, (h, h + 4)) for t in range(T) for h in range(IDX_H // 2)]
RET_UNITS = [(t, s, h) for t, s in ((0, 0), (1, 0), (1, 1)) for h in range(2)]


def layer_plan():
    plan = interleave("tr1", 4, (0, 1, 2, 3), "AV")
    plan += interleave("proj", len(IN_BLOCKS) * T, (4, 5, 6, 7), "VA")
    plan += interleave("idxT", T, (0, 1), "V")
    plan += interleave("tr2", 4, (2, 3, 4, 5), "AV")
    plan += interleave("idxS", len(IDX_UNITS), (6, 7), "A")
    plan += interleave("uq", 2 * T, (0, 1, 2, 3), "AA")
    plan += interleave("ukv", 2 * T, (4, 5, 0, 1), "AA")
    plan += interleave("dsaT", T, (2, 3), "A")
    plan += interleave("retT", T, (6, 7), "A")
    plan += interleave("mlaT", 4 * T, (0, 1, 2, 3), "A")
    plan += interleave("retS", len(RET_UNITS), (4, 5, 6, 7), "V")
    for i in range(NG + 2):
        if i < NG:
            plan.append(("S", i, (0, 1)[i % 2], "V"))
        if 1 <= i <= NG:
            plan.append(("PT", i - 1, (2, 3)[i % 2], "A"))
        if i >= 2:
            plan.append(("O", i - 2, (4, 5)[i % 2], "V"))
    plan += interleave("retO", T, (6, 7), "V")
    plan += interleave("mixT", 4, (0, 1, 2, 3), "AV")
    plan += interleave("wout", 2 * T, (4, 5, 6, 7), "V")
    plan += interleave("tr3", 4, (0, 1, 2, 3), "AV")
    for b in range(FFB):
        plan += [("ff1", 2 * b + j, (2 * b + j) % 4, "V") for j in range(2)]
    plan += interleave("ff2", 2 * T, (4, 5, 6, 7), "V")
    return plan


def layer_weights():
    blocks = [(("in", b), ("proj", T * b + T - 1)) for b in range(len(IN_BLOCKS))]
    blocks += [(("uq", c), ("uq", T * c + T - 1)) for c in range(2)]
    blocks += [(("ukv", 0), ("ukv", 2 * T - 1))]
    blocks += [(("out", c), ("wout", T * c + T - 1)) for c in range(2)]
    for b in range(FFB):
        blocks += [(("ff1", b), ("ff1", 2 * b + 1))]
        if b >= 1:
            blocks += [(("ff2", b - 1), ("ff1", 2 * b + 2) if b + 1 < FFB else ("ff2", 2 * T - 1))]
    return blocks + [(("ff2", FFB - 1), ("ff2", 2 * T - 1))]


ATT_UNITS = [(t, h) for t in range(T) for h in range(HPG)]
NA = len(ATT_UNITS)
CORE = [(t, par) for t in range(T) for par in range(2)]
PROJ_RW, PROJ_QKV, PROJ_GATE = (T * len(b) for b in (RW_BLOCKS, QKV_BLOCKS, GATE_BLOCKS))


def second_plan():
    plan = interleave("tr1", 4, (0, 1, 2, 3), "AV")
    plan += interleave("rw", PROJ_RW, (4, 5, 6, 7), "VA")
    plan += interleave("bias", 1, (0,), "V")
    plan += interleave("qkv", PROJ_QKV, (1, 2, 3, 0), "VA")
    plan += interleave("loraT", T, (4, 5), "A")
    plan += interleave("lora", 3 * T, (6, 7, 4, 5, 6, 7), "VVA")
    plan += interleave("gate", PROJ_GATE, (0, 1, 2, 3), "A")
    plan += interleave("qkT", 6, (4, 5, 6, 7), "A")
    for i in range(NA + 2):
        if i < NA:
            plan.append(("S", i, ((0, 1), (2, 3))[i % 2], "A"))
        if 1 <= i <= NA:
            plan.append(("PT", i - 1, (4, 5), "A"))
        if i >= 2:
            plan.append(("O", i - 2, (6, 7)[i % 2], "V"))
    plan += interleave("cum", 2 * T, (0, 1, 2, 3), "AV")
    plan += interleave("sdec", 1, (4,), "A")
    plan += interleave("rwT", 8, (5, 6, 7, 0), "A")
    plan += interleave("attT", 1, (1,), "A")
    plan += interleave("yatt", 2 * T, (2, 3, 4, 1), "V")
    for t in range(T):
        for par in range(2):
            plan += [(m, 2 * t + par, 4 * par + b, "V") for b, m in enumerate(("NT", "N", "Mak", "Mrb"))]
            plan += [("Mrk", 2 * t + par, 4 * par, "V")]
        for i in range(len(LEVELS)):
            for par in range(2):
                plan.append(("X", (2 * t + par) * 8 + i, 4 * par + 1, "V"))
            for par in range(2):
                if i < len(LEVELS) - 1:
                    plan.append(("TX", (2 * t + par) * 8 + i, 4 * par + 2, "V"))
                plan.append(("XT", (2 * t + par) * 8 + i, 4 * par + 3, "A"))
        plan += [("RHS", 2 * t + par, 4 * par, "A") for par in range(2)]
        plan += [("U", 2 * t + par, 4 * par + 1, "A") for par in range(2)]
        plan += [("OUT", 2 * t + par, 4 * par + 2, "V") for par in range(2)]
        if t == 0:
            plan += [("state", 0, 3, "V")]
    plan += interleave("oT", 2, (0, 1), "A")
    plan += interleave("yrw", 2 * T, (2, 3, 4, 5), "V")
    plan += interleave("mixT", 4, (6, 7, 0, 1), "A")
    plan += interleave("wout", 2 * T, (2, 3, 4, 5), "V")
    plan += interleave("tr2", 4, (6, 7, 0, 1), "AV")
    plan += interleave("route", T, (2, 3), "V")
    plan += interleave("rank", T + 1, (4, 5, 6), "V")
    return plan


def second_weights():
    blocks = []
    for stage, cols in (("rw", RW_BLOCKS), ("qkv", QKV_BLOCKS), ("gate", GATE_BLOCKS)):
        blocks += [((stage, b), (stage, T * b + T - 1)) for b in range(len(cols))]
    blocks += [(("att_out", 0), ("yatt", 2 * T - 1)), (("rwkv_out", 0), ("yrw", 2 * T - 1))]
    return blocks + [(("out", c), ("wout", T * c + T - 1)) for c in range(2)]


EPT = 2
MOE_SLOTS = 3 * EPT


SLOTS_E = 64
PASSES = SEQ // SLOTS_E
TURNS = NE // EPT


def moe_plan():
    return [("gx", 0, 4, "V"), ("gx", 1, 5, "V"), ("gt", 0, 6, "A"), ("gate", 0, 7, "A"), ("up", 0, 4, "V"),
            ("hT", 0, 5, "A"), ("y", 0, 6, "A"), ("y", 1, 7, "V")]


def shape_tables():
    pos = np.arange(SEQ, dtype=np.float32)
    i = np.arange(P)
    c = {}
    c["ident"] = np.eye(P)
    c["causal"] = np.where(np.arange(T * P)[None, :] <= i[:, None] + P, 0.0, MASKED)
    for dim in (ROPE, DSA_E):
        inv = np.float32(ROPE_THETA) ** (-np.arange(0, dim, 2, dtype=np.float32) / np.float32(dim))
        ang = (pos[:, None] * inv[None, :]).astype(np.float32)
        for name, f in (("cos", np.cos), ("sin", np.sin)):
            c[f"{name}{dim}"] = f(ang).reshape(T, P, dim // 2).transpose(1, 0, 2).reshape(P, -1)
    gamma = np.log1p(-np.exp2(-5.0 - np.arange(RET_H)))
    dist = np.arange(T)[:, None, None] * P + i[None, None, :] - i[None, :, None]
    dec = np.where(dist >= 0, np.exp(np.maximum(dist, 0)[None] * gamma[:, None, None, None]), 0.0) * RET_E ** -0.5
    c["decay"] = dec.transpose(2, 1, 0, 3).reshape(P, -1)
    before, mid = (i[:, None] <= i[None, :]), (i < P // 2)[:, None]
    c["cum_incl"] = DECAY_RATE * (before.astype(float) - mid)
    c["cum_excl"] = DECAY_RATE * ((i[:, None] < i[None, :]).astype(float) - mid)
    c["halves"] = DECAY_RATE * np.concatenate([mid, ~mid], axis=1)
    c["minus_strict"] = -1.0 * (i[:, None] < i[None, :])
    c["incl"] = 1.0 * before
    def level(m):
        r, k = i[:, None], i[None, :]
        return (r // (2 * m) == k // (2 * m)) & (r // m % 2 == 1) & (k // m % 2 == 0)
    c["minus_level1"] = -1.0 * level(1)
    c["level1T"] = 1.0 * level(1).T
    c["levels"] = np.concatenate([level(m) for m in LEVELS], axis=1)
    d = np.float32(255) - np.arange(384, dtype=np.float32)
    exact = BUCKETS // 2
    far = exact + (np.log(np.maximum(d, 1) / np.float32(exact)) / np.float32(np.log(REL_MAX / exact))
                   * np.float32(BUCKETS - exact)).astype(np.int32)
    bucket = np.where(d < exact, np.maximum(d, 0), np.minimum(far, BUCKETS - 1)).astype(int)
    hot = np.zeros((P, 384))
    hot[bucket, np.arange(384)] = 1.0
    c["bucket_hot"] = hot
    for g, (win, dil) in enumerate(PATTERNS):
        hot[BUCKETS + g * HPG:BUCKETS + (g + 1) * HPG] = np.where((d >= 0) & (d <= win) & (d % dil == 0), 0.0, MASKED)
    c["flip"] = np.eye(P)[::-1]
    c["places"] = np.tile(np.arange(SLOTS_E), (P, 1))
    c["rank"] = np.tile(np.arange(EPG, 0, -1), (P, 1))
    return {k: np.ascontiguousarray(v, dtype=np.float32) for k, v in c.items()}


SHARED = ("ident", "causal")
FIRST = ("cos32", "sin32", "cos64", "sin64", "decay")
SECOND = ("cum_incl", "cum_excl", "halves", "minus_strict", "incl", "minus_level1", "level1T", "levels",
          "bucket_hot", "flip", "places", "rank")
ROWS, _at = {}, 0
for _n, _w in (("mu", RW_IN), ("w0", RW_W), ("a0", RW_W), ("k_k", RW_W), ("k_a", RW_W), ("r_k", RW_W), ("ln_w", RW_W),
               ("ln_b", RW_W), ("q_gain", GRP * ATT_E), ("k_gain", GRP * ATT_E), ("g_final", D), ("b_route", EG + NE)):
    ROWS[_n] = (_at, _w)
    _at += _w


def pack(tables, names):
    return np.ascontiguousarray(np.concatenate([tables[n] for n in names], axis=1))


def offsets(tables, names):
    at, out = 0, {}
    for n in names:
        out[n] = (at, tables[n].shape[1])
        at += tables[n].shape[1]
    return out, at


def program(nc, io, out):
    tables = shape_tables()
    with ExitStack() as ctx:
        def sb(name, words, rows=P):
            return ctx.enter_context(nc.sbuf_tensor(name, [rows, words], F32))

        def sem(name):
            return ctx.enter_context(nc.semaphore(name))

        def sig(name, per_turn):
            return Signal(sem(name), per_turn)

        ring = sb("ring", SLOTS * SLOT)
        xs = sb("xs", T * D)
        x = xs[:].rearrange("p (t d) -> p t d", t=T)
        hTs = sb("hTs", KD * SEQ)
        hT = hTs[:].rearrange("p (k s) -> p k s", k=KD)
        shared_at, shared_w = offsets(tables, SHARED)
        first_at, first_w = offsets(tables, FIRST)
        second_at, second_w = offsets(tables, SECOND)
        shared_c = sb("shared_c", shared_w)
        phase_c = sb("phase_c", second_w)
        arena = sb("arena", 29572)
        gains = sb("gains", N_GAIN)
        stat = sb("stat", 96)
        stat2 = sb("stat2", 224)
        psum = ctx.enter_context(nc.psum_tensor("psum", [P, 8, 512], F32))

        def shared(name):
            o, w = shared_at[name]
            return shared_c[:, o:o + w]

        def first(name):
            o, w = first_at[name]
            return phase_c[:, o:o + w]

        def second(name):
            o, w = second_at[name]
            return phase_c[:, o:o + w]

        ident, causal = shared("ident"), shared("causal")

        def slot(s, n=SLOT):
            return ring[:, s * SLOT:s * SLOT + n]

        def area(o, n):
            return arena[:, o:o + n]

        proj = area(0, T * IN_W).rearrange("p (t w) -> p t w", t=T)
        xn = area(5520, T * D).rearrange("p (t d) -> p t d", t=T)
        q = area(7568, T * MLA_H * QK).rearrange("p (t h e) -> p t h e", t=T, h=MLA_H)
        kfull = area(9104, T * MLA_H * QK).rearrange("p (t h e) -> p t h e", t=T, h=MLA_H)
        mix = area(7568, T * D).rearrange("p (t d) -> p t d", t=T)
        kv = area(10640, T * MLA_H * 128).rearrange("p (t h e) -> p t h e", t=T, h=MLA_H)
        qTm = area(12688, MLA_H * SEQ).rearrange("p (h s) -> p h s", h=MLA_H)
        kTm = area(14736, MLA_H * SEQ).rearrange("p (h s) -> p h s", h=MLA_H)
        dsaT = area(16784, 3 * SEQ).rearrange("p (c s) -> p c s", c=3)
        retT = area(17552, 4 * SEQ).rearrange("p (c s) -> p c s", c=4)
        idxT = area(18576, 3 * SEQ).rearrange("p (c s) -> p c s", c=3)
        rel = area(19344, 2 * 512).rearrange("p (b w) -> p b w", b=2)
        score = area(20368, 256)
        left = area(20624, 256)
        dsa_mask = area(20880, T * SEQ).rearrange("p (t s) -> p t s", t=T)
        ki4 = area(20368, T * P).rearrange("p (t c e) -> p t c e", t=T, c=4)
        kd = area(12688, T * P).rearrange("p (t c e) -> p t c e", t=T, c=2)
        scores = [proj[:, 0, b * 512:b * 512 + 512] for b in range(2)]
        probsT = [proj[:, 1, b * 512:b * 512 + 512] for b in range(2)]
        ret_s = [xn.rearrange("p t d -> p (t d)")[:, b * 256:b * 256 + 256] for b in range(len(RET_UNITS))]
        ret_o = rel[:, 0, :].rearrange("p (g e) -> p g e", e=RET_E)
        ret_sq = rel[:, 1, :].rearrange("p (g e) -> p g e", e=RET_E)
        relu_h = [area(14736 + b * 512, 512) for b in range(4)]
        uT = area(12688, 2048).rearrange("p (b f s) -> p b f s", b=2, f=4)
        dve_tmp = [rel[:, b, :] for b in range(2)]
        pool_tmp = [area(14736 + b * 512, 512) for b in range(2)]

        sumsq, std, rstd = stat[:, 0:4], stat[:, 4:8], stat[:, 8:12]
        wi = stat[:, 12:28].rearrange("p (t h) -> p t h", t=T)
        top8 = stat[:, 28:36]
        rowmax, rowsum = stat[:, 36:40], stat[:, 40:44]
        rinv = [stat[:, 44 + 4 * b:48 + 4 * b] for b in range(3)]
        ret_mean, ret_var, ret_rstd = stat[:, 56:64], stat[:, 64:72], stat[:, 72:80]
        eps_c = stat[:, 80:81]

        qkv = area(0, T * 3 * ATT_W).rearrange("p (t w) -> p t w", t=T)
        pf = area(4608, T * RW_IN).rearrange("p (t w) -> p t w", t=T)
        gates = area(8256, T * GATE_W).rearrange("p (t w) -> p t w", t=T)
        xn2 = area(8256, T * D).rearrange("p (t d) -> p t d", t=T)
        wide = lambda o: area(o, T * RW_W).rearrange("p (t w) -> p t w", t=T)
        bufA, bufB, bufK, bufR, rw_g = (wide(12352 + 1024 * j) for j in range(5))
        prev = area(12352, T * RW_IN).rearrange("p (t w) -> p t w", t=T)
        mu = area(16000, RW_IN)
        vec = {n: area(17472 + RW_W * j, RW_W) for j, n in enumerate(("w0", "a0", "k_k", "k_a", "r_k", "ln_w", "ln_b"))}
        qT = area(21056, ATT_H // 2 * SEQ).rearrange("p (c s) -> p c s", s=SEQ)
        kT = area(22592, ATT_H // 2 * SEQ).rearrange("p (c s) -> p c s", s=SEQ)
        g_final = area(21056, D)
        lora_w = area(22592, 3 * RW_W).rearrange("p (j w) -> p j w", j=3)
        bias_m = area(24128, ATT_H * SEQ).rearrange("p (h k) -> p h k", h=ATT_H)
        bias_row = area(24128, 384)
        bias_tab = area(24512, ATT_H)
        qk_gain = area(24600, 2 * GRP * ATT_E).rearrange("p (j g e) -> p j g e", j=2, g=GRP)
        att_s = [area(27200 + 768 * b, 768) for b in range(2)]
        qk_sq = area(27200, T * ATT_W).rearrange("p (t w) -> p t w", t=T)
        att_p = area(28736, 768)
        loraT = area(28736, 3 * SEQ).rearrange("p (j s) -> p j s", j=3)
        att = hTs[:, 0:512].rearrange("p (t w) -> p t w", t=T)
        attT = hTs[:, 512:1024].rearrange("p (k s) -> p k s", k=2)
        oT = hTs[:, 1024:2048].rearrange("p (k s) -> p k s", k=4)
        rwT = [area(1024 * j, 1024).rearrange("p (c s) -> p c s", c=PAIRS) for j in range(4)]
        core = [{n: area(21056 + 3584 * par + 512 * j, 512).rearrange("p (c s) -> p c s", c=PAIRS)
                 for j, n in enumerate(("NT", "T", "TT", "X", "Mak", "Mrb", "Mrk"))} for par in range(2)]
        rhs = [core[par]["X"].rearrange("p c s -> p (c s)")[:, 0:PAIRS * RW_E].rearrange("p (c e) -> p c e", c=PAIRS)
               for par in range(2)]
        rw_u = area(28224, RW_W).rearrange("p (h e) -> p h e", h=RW_H)
        state = area(28736, PAIRS * RW_E).rearrange("p (c e) -> p c e", c=PAIRS)
        minus_state = area(28992, PAIRS * RW_E).rearrange("p (c e) -> p c e", c=PAIRS)
        rw_o = bufA.rearrange("p t (h e) -> p (t h) e", e=RW_E)
        rw_sq = bufK.rearrange("p t (h e) -> p (t h) e", e=RW_E)
        w_route = area(29248, KD * (EG + NE)).rearrange("p (k n) -> p k n", k=KD)
        b_route = area(29536, EG + NE)
        logits = area(21056, T * (EG + NE)).rearrange("p (t n) -> p t n", t=T)
        ra = [area(21200 + 64 * j, T * NE) for j in range(8)]
        moe_slot = [ring[:, s * SLOT:(s + 1) * SLOT] for s in range(SLOTS)] + [area(j * SLOT, SLOT) for j in range(2)]
        xe = area(12352, KD * P).rearrange("p (k n) -> p k n", k=KD)
        silu_g = area(13376, D_EXP)
        hid = area(13888, D_EXP)
        hidT = area(14400, D_EXP).rearrange("p (f n) -> p f n", f=D_EXP // P)
        y_rows = area(15424, D)
        take = area(16448, T * P).rearrange("p (t j n) -> p t j n", t=T, j=EPT)
        give = area(16704, T * P).rearrange("p (t j n) -> p t j n", t=T, j=EPT)
        giveT = area(16960, SEQ)
        place = area(17216, PASSES * NE * T).rearrange("p (q e t) -> p q e t", q=PASSES, t=T)
        gate_tab = area(17472, PASSES * NE * T).rearrange("p (q e t) -> p q e t", q=PASSES, t=T)
        zeros, ones = area(17728, P), area(17856, P)
        taken = area(17984, T * NE).rearrange("p (t e) -> p t e", t=T)
        place_now, gate_now = (stat2[:, 180 + 4 * j:184 + 4 * j].rearrange("p (e t) -> p e t", t=T) for j in range(2))
        fullest = stat2[:, 192:196]
        turns_f = stat2[:, 196:197]
        turns_i = ctx.enter_context(nc.sbuf_tensor("turns_i", [P, 1], mybir.dt.int32))
        qk_ss = stat2[:, 0:48].rearrange("p (j t h) -> p j t h", j=2, t=T)
        kk_n, bonus, rw_mean, rw_var = (stat2[:, 48 + 16 * j:64 + 16 * j] for j in range(4))
        sdec = stat2[:, 112:116]
        gn_eps_c = stat2[:, 190:191]
        bias_dram = nc.dram_tensor("bias_by_distance", (ATT_H, 384), F32).ap()

        consts_loaded = sem("consts_loaded")
        x_loaded = sem("x_loaded")
        consts_set = sem("consts_set")
        out_stored = sem("out_stored")
        slot_loaded = [sem(f"slot_loaded{s}") for s in range(SLOTS)]
        gains_loaded = sem("gains_loaded")
        LU = Units(sem("layer_unit_full"), sem("layer_emptied_act"), sem("layer_emptied_dve"), layer_plan())
        LW = WeightRing(slot_loaded, layer_weights())
        std_ready = sig("std_ready", 3)
        xn_ready = sig("xn_ready", 3 * T)
        idx_roped = sig("idx_roped", 1)
        kr_roped = sig("kr_roped", 1)
        q_roped = sig("q_roped", 1)
        kfull_ready = sig("kfull_ready", 1)
        dsa_roped = sig("dsa_roped", 1)
        ret_roped = sig("ret_roped", 1)
        rel_read = sig("rel_read", len(IDX_UNITS))
        shifted = sig("shifted", NG)
        probs_ready = sig("probs_ready", NG)
        silu_ready = sig("silu_ready", 1)
        ret_var_ready = sig("ret_var_ready", 1)
        ret_std_ready = sig("ret_std_ready", 1)
        ret_ready = sig("ret_ready", 1)
        hid_ready = sig("hid_ready", 2 * FFB)
        x_done = sig("x_done", 1)

        SU = Units(sem("second_unit_full"), sem("second_emptied_act"), sem("second_emptied_dve"), second_plan())
        SW = WeightRing(slot_loaded, second_weights(), LW.next_slot)
        second_c_loaded = sem("second_c_loaded")
        gains2_loaded = sem("gains2_loaded")
        g_final_loaded = sem("g_final_loaded")
        std2_ready = sem("std2_ready")
        x_normed = sem("x_normed")
        xn2_ready = sem("xn2_ready")
        mu_loaded, vec_loaded, lora_loaded = sem("mu_loaded"), sem("vec_loaded"), sem("lora_loaded")
        qk_gain_loaded, bias_tab_loaded, route_loaded = sem("qk_gain_loaded"), sem("bias_tab_loaded"), sem("route_loaded")
        prev_zero = sem("prev_zero")
        prev_loaded = sem("prev_loaded")
        pm_ready = sem("pm_ready")
        lora_in = sem("lora_in")
        wa_in = sem("wa_in")
        wa_ready = sem("wa_ready")
        kk_ss, kk_std = sem("kk_ss"), sem("kk_std")
        preproc_done = sem("preproc_done")
        bonus_ready, bonus_v = sem("bonus_ready"), sem("bonus_v")
        bias_done, bias_stored, bias_loaded = sem("bias_done"), sem("bias_stored"), sem("bias_loaded")
        qk_ss_ready, qk_std = sem("qk_ss_ready"), sem("qk_std")
        qk_ready = sem("qk_ready")
        att_max = sem("att_max")
        att_exp = sem("att_exp")
        exp_incl, exp_excl = sem("exp_incl"), sem("exp_excl")
        scaled = sem("scaled")
        core_masked = sem("core_masked")
        core_start = sem("core_start")
        state_ready = sem("state_ready")
        gn_ss, gn_std = sem("gn_ss"), sem("gn_std")
        o_ready = sem("o_ready")
        mixed = sem("mixed")
        route_max, route_exp = sem("route_max"), sem("route_exp")
        pair_diff, pair_exp = sem("pair_diff"), sem("pair_exp")
        gate_ready = sem("gate_ready")
        EU = Units(sem("moe_unit_full"), sem("moe_emptied_act"), sem("moe_emptied_dve"), moe_plan())
        moe_loaded = [sem(f"moe_loaded{s}") for s in range(MOE_SLOTS)]
        moe_done = sem("moe_done")
        fills_ready = sem("fills_ready")
        taken_ready = sem("taken_ready")
        places_ready = sem("places_ready")
        take_ready = sig("take_ready", 1)
        FU = Units(sem("final_unit_full"), sem("final_emptied_act"), sem("final_emptied_dve"), interleave("acc", 2 * T, (0, 1, 2, 3), "V"))

        def second_weight(name):
            kind, b = name
            if kind in ("rw", "qkv", "gate"):
                first_col = {"qkv": 0, "rw": 3 * ATT_W, "gate": 3 * ATT_W + RW_IN}[kind]
                c, w = {"rw": RW_BLOCKS, "qkv": QKV_BLOCKS, "gate": GATE_BLOCKS}[kind][b]
                return io["w_in_2"][0, :, first_col + c:first_col + c + w].rearrange("(k p) n -> p k n", p=P), KD, w
            if kind == "att_out":
                return io["w_att_out_2"][0].rearrange("(k p) n -> p k n", p=P), HPG * ATT_E // P, D
            if kind == "rwkv_out":
                return io["w_rwkv_out_2"][0].rearrange("(k p) n -> p k n", p=P), RW_W // P, D
            return io["w_out_2"][0, :, b * 512:b * 512 + 512].rearrange("(k p) n -> p k n", p=P), KD, 512

        def second_slot(name):
            _, k, w = second_weight(name)
            return slot(SW.where[name][0], k * w).rearrange("p (k n) -> p k n", k=k)

        def loads_before(s):
            return DEPTH * LW.per[s]

        block = ctx.enter_context(nc.Block())

        def layer_weight(name, l):
            kind, b = name
            if kind == "in":
                c, w = IN_BLOCKS[b]
                return io["w_in"][l, :, c:c + w].rearrange("(k p) n -> p k n", p=P), KD, w
            if kind == "uq":
                w = MLA_H * QK // 2
                return io["w_uq"][l, :, b * w:b * w + w].rearrange("(k p) n -> p k n", p=P), Q_RANK // P, w
            if kind == "ukv":
                return io["w_ukv"][l].rearrange("(k p) n -> p k n", p=P), KV_RANK // P, MLA_H * 128
            if kind == "out":
                return io["w_out"][l, :, b * 512:b * 512 + 512].rearrange("(k p) n -> p k n", p=P), KD, 512
            if kind == "ff1":
                return io["w_ff1"][l, :, b * 512:b * 512 + 512].rearrange("(k p) n -> p k n", p=P), KD, 512
            return io["w_ff2"][l, b * 512:b * 512 + 512, :].rearrange("(k p) n -> p k n", p=P), 4, D

        def layer_slot(name):
            kind, b = name
            k, w = {"in": (KD, IN_BLOCKS[b][1] if kind == "in" else 0), "uq": (Q_RANK // P, MLA_H * QK // 2),
                    "ukv": (KV_RANK // P, MLA_H * 128), "out": (KD, 512), "ff1": (KD, 512), "ff2": (4, D)}[kind]
            return slot(LW.where[name][0], k * w).rearrange("p (k n) -> p k n", k=k)

        @block.sync
        def _(sp):
            sp.dma_start(shared_c[:], io["shared_c"]).then_inc(consts_loaded, 16)
            sp.dma_start(x, io["x"][0].rearrange("(t p) d -> p t d", p=P)).then_inc(x_loaded, 16)
            sp.dma_start(phase_c[:, 0:first_w], io["first_c"]).then_inc(consts_loaded, 16)
            with sp.Fori(0, DEPTH) as l:
                units = UnitView(LU, sp, psum, l)
                for j, (name, _) in enumerate(LW.blocks):
                    s = LW.where[name][0]
                    prev = LW.prev[name]
                    if prev:
                        sp.wait_ge(LU.full, units.full_count(prev))
                    else:
                        sp.wait_ge(LU.full, l * LU.n + LU.u[LW.last[s]][0])
                    src, k, w = layer_weight(name, l)
                    sp.dma_start(slot(s, k * w).rearrange("p (k n) -> p k n", k=k), src).then_inc(slot_loaded[s], 16)
            units = UnitView(SU, sp, psum)
            for name, _ in SW.blocks:
                s = SW.where[name][0]
                if SW.prev[name]:
                    units.wait_full(SW.prev[name])
                else:
                    sp.wait_ge(LU.full, DEPTH * LU.n + LU.u[LW.last[s]][0])
                src, k, w = second_weight(name)
                sp.dma_start(slot(s, k * w).rearrange("p (k n) -> p k n", k=k), src).then_inc(slot_loaded[s], 16)

            def matrices(first_expert):
                for i, (w, k) in enumerate((("w_expert_gate_2", KD), ("w_expert_up_2", KD), ("w_expert_down_2", D_EXP // P))):
                    for j in range(EPT):
                        s = EPT * i + j
                        yield (moe_slot[s].rearrange("p (k n) -> p k n", k=k),
                               io[w][0, first_expert + j].rearrange("(k p) n -> p k n", p=P), s)

            for dst, src, s in matrices(0):
                units.wait_full(SW.last[s] if s < SLOTS else ("oT", 1))
                sp.dma_start(dst, src).then_inc(moe_loaded[s], 16)
            sp.wait_ge(places_ready, 1)
            with sp.Fori(1, sp.value_load(turns_i[0:1, 0:1], min_val=TURNS, max_val=TURNS * PASSES)) as turn:
                for dst, src, s in matrices(turn % TURNS * EPT):
                    if s % EPT == 0:
                        sp.wait_ge(EU.full, turn * EU.n + EU.u[(("gate", 0), ("up", 0), ("y", 1))[s // EPT]][0])
                    sp.dma_start(dst, src).then_inc(moe_loaded[s], 16)
            sp.wait_ge(moe_done, 1)
            sp.dma_start(out[0].rearrange("(t p) d -> p t d", p=P), x).then_inc(out_stored, 16)
            sp.wait_ge(out_stored, 16)

        def weights_in(pe, ring_plan, name, turn):
            s, i = ring_plan.where[name]
            pe.wait_ge(ring_plan.loaded[s], turn * (16 * ring_plan.per[s]) + 16 * i)

        def transposes(pe, units, stage, src):
            for j in range(4):
                bank = units.begin((stage, j))
                for kk in range(2):
                    for t in range(T):
                        k = 2 * j + kk
                        ins = pe.transpose(bank[:, kk * SEQ + t * P:kk * SEQ + (t + 1) * P],
                                           src[:, t, k * P:(k + 1) * P], ident)
                units.finish((stage, j), ins)

        def token_major(pe, units, key, lhs, w):
            bank = units.begin(key)
            n, k = w.shape[2], w.shape[1]
            for i in range(k):
                ins = pe.matmul(bank[:, 0:n], lhs(i), w[:, i, :], start=(i == 0), stop=(i == k - 1))
            units.finish(key, ins)

        @block.tensor
        def _(pe):
            pe.wait_ge(consts_loaded, 32)
            pe.sem_inc(LU.full, LU.n)
            with pe.Fori(0, DEPTH) as l:
                units = UnitView(LU, pe, psum, l)

                def tok(t, first_k=0):
                    return lambda k: hT[:, first_k + k, t * P:(t + 1) * P]

                xn_ready.wait(pe, T, l)
                transposes(pe, units, "tr1", xn)
                units.wait_emptied(*(("tr1", j) for j in range(4)))
                for b in range(len(IN_BLOCKS)):
                    weights_in(pe, LW, ("in", b), l)
                    for t in range(T):
                        token_major(pe, units, ("proj", T * b + t), tok(t), layer_slot(("in", b)))
                idx_roped.wait(pe, 1, l)
                for t in range(T):
                    bank = units.begin(("idxT", t))
                    for c in range(2):
                        pe.transpose(bank[:, c * P:(c + 1) * P], proj[:, t, C_QI + c * P:C_QI + (c + 1) * P], ident)
                    ins = pe.transpose(bank[:, 2 * P:3 * P], ki4[:, t, :, :].rearrange("p c e -> p (c e)"), ident)
                    units.finish(("idxT", t), ins)
                xn_ready.wait(pe, 2 * T, l)
                transposes(pe, units, "tr2", xn)
                units.wait_emptied(*(("idxT", t) for t in range(T)))
                for i, (t, heads) in enumerate(IDX_UNITS):
                    bank, nk = units.begin(("idxS", i)), (t + 1) * P
                    for j, h in enumerate(heads):
                        r = slice(IDX_E * (h % 4), IDX_E * (h % 4 + 1))
                        ins = pe.matmul(bank[:, j * nk:(j + 1) * nk], idxT[r, h // 4, t * P:(t + 1) * P],
                                        idxT[r, 2, 0:nk], start=True, stop=True)
                    units.finish(("idxS", i), ins)
                units.wait_emptied(*(("tr2", j) for j in range(4)))
                for c in range(2):
                    weights_in(pe, LW, ("uq", c), l)
                    for t in range(T):
                        token_major(pe, units, ("uq", T * c + t), tok(t), layer_slot(("uq", c)))
                weights_in(pe, LW, ("ukv", 0), l)
                for c in range(2):
                    for t in range(T):
                        token_major(pe, units, ("ukv", T * c + t), tok(t, Q_RANK // P),
                                    layer_slot(("ukv", 0))[:, :, c * 512:(c + 1) * 512])
                dsa_roped.wait(pe, 1, l)
                for t in range(T):
                    bank = units.begin(("dsaT", t))
                    for c in range(2):
                        pe.transpose(bank[:, c * P:(c + 1) * P], proj[:, t, C_AQ + c * P:C_AQ + (c + 1) * P], ident)
                    ins = pe.transpose(bank[:, 2 * P:3 * P], kd[:, t, :, :].rearrange("p c e -> p (c e)"), ident)
                    units.finish(("dsaT", t), ins)
                ret_roped.wait(pe, 1, l)
                for t in range(T):
                    bank = units.begin(("retT", t))
                    for c in range(4):
                        ins = pe.transpose(bank[:, c * P:(c + 1) * P], proj[:, t, C_RQ + c * P:C_RQ + (c + 1) * P], ident)
                    units.finish(("retT", t), ins)
                q_roped.wait(pe, 1, l)
                kfull_ready.wait(pe, 1, l)
                for t in range(T):
                    for j in range(4):
                        bank = units.begin(("mlaT", 4 * t + j))
                        src = (q, kfull)[j // 2]
                        for c in range(4):
                            ins = pe.transpose(bank[0:QK, c * P:(c + 1) * P], src[:, t, 4 * (j % 2) + c, :], ident)
                        units.finish(("mlaT", 4 * t + j), ins)
                units.wait_emptied(*(("retT", t) for t in range(T)))
                for i, (t, s, h0) in enumerate(RET_UNITS):
                    bank = units.begin(("retS", i))
                    r = slice(RET_E * h0, RET_E * (h0 + 1))
                    for j, h in enumerate((h0, h0 + 2)):
                        ins = pe.matmul(bank[:, j * P:(j + 1) * P], retT[r, 2 + h // 2, s * P:(s + 1) * P],
                                        retT[r, h // 2, t * P:(t + 1) * P], start=True, stop=True)
                    units.finish(("retS", i), ins)
                units.wait_emptied(*(("dsaT", t) for t in range(T)), *(("mlaT", j) for j in range(4 * T)))

                def attend_scores(g):
                    dsa, t, heads = GROUPS[g]
                    bank, nk = units.begin(("S", g)), (t + 1) * P
                    for j, h in enumerate(heads):
                        if dsa:
                            r = slice(DSA_E * (h % 2), DSA_E * (h % 2 + 1))
                            qT, kT = dsaT[r, h // 2, t * P:(t + 1) * P], dsaT[r, 2, 0:nk]
                        else:
                            qT, kT = qTm[0:QK, h, t * P:(t + 1) * P], kTm[0:QK, h, 0:nk]
                        ins = pe.matmul(bank[:, j * nk:(j + 1) * nk], qT, kT, start=True, stop=True)
                    units.finish(("S", g), ins)

                def turn_probs(g):
                    probs_ready.wait(pe, g + 1, l)
                    bank = units.begin(("PT", g))
                    for c in range(len(GROUPS[g][2]) * (GROUPS[g][1] + 1)):
                        ins = pe.transpose(bank[:, c * P:(c + 1) * P], scores[g % 2][:, c * P:(c + 1) * P], ident)
                    units.finish(("PT", g), ins)

                def attend_values(g):
                    dsa, t, heads = GROUPS[g]
                    units.wait_emptied(("PT", g))
                    bank = units.begin(("O", g))
                    for j, h in enumerate(heads):
                        for s in range(t + 1):
                            c = j * (t + 1) + s
                            v = proj[:, s, C_AV:C_AV + DSA_E] if dsa else kv[:, s, h, NOPE:NOPE + MLA_V]
                            ins = pe.matmul(bank[:, j * MLA_V:(j + 1) * MLA_V], probsT[g % 2][:, c * P:(c + 1) * P], v,
                                            start=(s == 0), stop=(s == t))
                    units.finish(("O", g), ins)

                for i in range(NG + 2):
                    if i < NG:
                        attend_scores(i)
                    if 1 <= i <= NG:
                        turn_probs(i - 1)
                    if i >= 2:
                        attend_values(i - 2)
                units.wait_emptied(*(("retS", i) for i in range(len(RET_UNITS))))
                for t in range(T):
                    bank = units.begin(("retO", t))
                    for h in range(RET_H):
                        mine = [i for i, u in enumerate(RET_UNITS) if (u[0], u[2]) == (t, h % 2)]
                        for i in mine:
                            s = RET_UNITS[i][1]
                            ins = pe.matmul(bank[:, h * RET_E:(h + 1) * RET_E], ret_s[i][:, h // 2 * P:(h // 2 + 1) * P],
                                            proj[:, s, C_RV + h * RET_E:C_RV + (h + 1) * RET_E],
                                            start=(i == mine[0]), stop=(i == mine[-1]))
                    units.finish(("retO", t), ins)
                units.wait_emptied(*(("O", g) for g in range(NG)))
                ret_ready.wait(pe, 1, l)
                transposes(pe, units, "mixT", mix)
                units.wait_emptied(*(("mixT", j) for j in range(4)))
                for c in range(2):
                    weights_in(pe, LW, ("out", c), l)
                    for t in range(T):
                        token_major(pe, units, ("wout", T * c + t), tok(t), layer_slot(("out", c)))
                xn_ready.wait(pe, 3 * T, l)
                transposes(pe, units, "tr3", xn)
                units.wait_emptied(*(("tr3", j) for j in range(4)))

                def ff1(b):
                    weights_in(pe, LW, ("ff1", b), l)
                    w = layer_slot(("ff1", b))
                    for j in range(2):
                        bank = units.begin(("ff1", 2 * b + j))
                        for f in range(2):
                            c = 2 * j + f
                            for k in range(KD):
                                ins = pe.matmul(bank[:, f * SEQ:(f + 1) * SEQ], w[:, k, c * P:(c + 1) * P], hT[:, k, :],
                                                start=(k == 0), stop=(k == KD - 1))
                        units.finish(("ff1", 2 * b + j), ins)

                def ff2(b):
                    weights_in(pe, LW, ("ff2", b), l)
                    hid_ready.wait(pe, 2 * b + 2, l)
                    w = layer_slot(("ff2", b))
                    for u in range(2 * T):
                        t, c = u % T, u // T
                        bank = units.begin(("ff2", u)) if b == 0 else units.bank(("ff2", u))
                        for f in range(4):
                            ins = pe.matmul(bank, uT[:, b % 2, f, t * P:(t + 1) * P], w[:, f, c * 512:(c + 1) * 512],
                                            start=(b == 0 and f == 0), stop=(b == FFB - 1 and f == 3))
                        if b == FFB - 1:
                            units.finish(("ff2", u), ins)

                for b in range(FFB):
                    ff1(b)
                    if b:
                        ff2(b - 1)
                ff2(FFB - 1)
            units = UnitView(SU, pe, psum)

            def weights(name):
                s, i = SW.where[name]
                pe.wait_ge(slot_loaded[s], 16 * (loads_before(s) + i))
                return second_slot(name)

            def project(stage, blocks):
                for b in range(len(blocks)):
                    w = weights((stage, b))
                    for t in range(T):
                        token_major(pe, units, (stage, T * b + t), lambda k: hT[:, k, t * P:(t + 1) * P], w)

            pe.wait_ge(xn2_ready, T)
            transposes(pe, units, "tr1", xn2)
            units.wait_emptied(*(("tr1", j) for j in range(4)))
            project("rw", RW_BLOCKS)
            pe.wait_ge(second_c_loaded, 16)
            pe.wait_ge(bias_tab_loaded, 32)
            bank, r = units.begin(("bias", 0)), slice(0, BUCKETS + ATT_H)
            units.finish(("bias", 0), pe.matmul(bank[0:ATT_H, 0:384], bias_tab[r, :], second("bucket_hot")[r, :],
                                                start=True, stop=True))
            project("qkv", QKV_BLOCKS)
            pe.wait_ge(lora_in, 1)
            for t in range(T):
                bank = units.begin(("loraT", t))
                pe.transpose(bank[:, 0:P], pf[:, t, C_XW:C_XG], ident)
                pe.transpose(bank[:, P:2 * P], pf[:, t, C_XG:C_XG + P], ident)
                units.finish(("loraT", t), pe.transpose(bank[0:LORA_G - P, 2 * P:3 * P], pf[:, t, C_XG + P:RW_IN], ident))
            pe.wait_ge(lora_loaded, 64)
            units.wait_emptied(*(("loraT", t) for t in range(T)))
            for t in range(T):
                c = slice(t * P, (t + 1) * P)
                for j, r in enumerate((slice(0, LORA_W), slice(LORA_W, P))):
                    bank = units.begin(("lora", 3 * t + j))
                    units.finish(("lora", 3 * t + j), pe.matmul(bank, loraT[r, 0, c], lora_w[r, 0, :], start=True, stop=True))
                bank, rest = units.begin(("lora", 3 * t + 2)), slice(0, LORA_G - P)
                pe.matmul(bank, loraT[:, 1, c], lora_w[:, 1, :], start=True, stop=False)
                units.finish(("lora", 3 * t + 2), pe.matmul(bank, loraT[rest, 2, c], lora_w[rest, 2, :], start=False, stop=True))
            project("gate", GATE_BLOCKS)
            pe.wait_ge(bias_loaded, 16)
            pe.wait_ge(qk_ready, 1)
            for j in range(6):
                bank = units.begin(("qkT", j))
                for c in range(2):
                    for t in range(T):
                        col = j // 3 * ATT_W + (2 * (j % 3) + c) * P
                        ins = pe.transpose(bank[:, c * SEQ + t * P:c * SEQ + (t + 1) * P], qkv[:, t, col:col + P], ident)
                units.finish(("qkT", j), ins)
            units.wait_emptied(*(("qkT", j) for j in range(6)))
            for i in range(NA + 2):
                if i < NA:
                    t, hg = ATT_UNITS[i]
                    bank, nk = units.begin(("S", i)), (t + 1) * P
                    r = slice(ATT_E * (hg % 2), ATT_E * (hg % 2 + 1))
                    per_bank = 512 // SEQ if t else GRP
                    for g0 in range(0, GRP, per_bank):
                        g1 = min(g0 + per_bank, GRP)
                        pe.matmul(bank[:, g0 * nk:g1 * nk].rearrange("p (g k) -> p g k", k=nk), second("flip"),
                                  bias_m[:, g0 * HPG + hg:(g1 - 1) * HPG + hg + 1:HPG, SEQ - nk:SEQ], start=True, stop=False)
                        for g in range(g0, g1):
                            c = (g * HPG + hg) // 2
                            ins = pe.matmul(bank[:, g * nk:(g + 1) * nk], qT[r, c, t * P:(t + 1) * P], kT[r, c, 0:nk],
                                            start=False, stop=(g == g1 - 1))
                    units.finish(("S", i), ins)
                if 1 <= i <= NA:
                    t = ATT_UNITS[i - 1][0]
                    pe.wait_ge(att_exp, i)
                    bank = units.begin(("PT", i - 1))
                    for c in range(GRP * (t + 1)):
                        ins = pe.transpose(bank[:, c * P:(c + 1) * P], att_s[(i - 1) % 2][:, c * P:(c + 1) * P], ident)
                    units.finish(("PT", i - 1), ins)
                if i >= 2:
                    t, hg = ATT_UNITS[i - 2]
                    units.wait_emptied(("PT", i - 2))
                    bank = units.begin(("O", i - 2))
                    for g in range(GRP):
                        for s in range(t + 1):
                            v = 2 * ATT_W + (g * HPG + hg) * ATT_E
                            c = g * (t + 1) + s
                            ins = pe.matmul(bank[:, 0:ATT_E], att_p[:, c * P:(c + 1) * P], qkv[:, s, v:v + ATT_E],
                                            start=(c == 0), stop=(c == GRP * (t + 1) - 1))
                    units.finish(("O", i - 2), ins)
            pe.wait_ge(wa_ready, 1)
            for t in range(T):
                for j, n in enumerate(("cum_incl", "cum_excl")):
                    bank = units.begin(("cum", 2 * t + j))
                    units.finish(("cum", 2 * t + j), pe.matmul(bank, second(n), bufR[:, t, :], start=True, stop=True))
            bank = units.begin(("sdec", 0))
            for c in range(PAIRS):
                pe.matmul(bank[:, c:c + 1], bufR[:, 0, c * P:(c + 1) * P], second("halves")[:, 1:2], start=True, stop=False)
                ins = pe.matmul(bank[:, c:c + 1], bufR[:, 1, c * P:(c + 1) * P], second("halves")[:, 0:1], start=False, stop=True)
            units.finish(("sdec", 0), ins)
            for t in range(T):
                pe.wait_ge(scaled, t + 1)
                for j, src in enumerate((bufA, bufB, bufK, bufR)):
                    bank = units.begin(("rwT", 4 * t + j))
                    for c in range(PAIRS):
                        ins = pe.transpose(bank[:, c * P:(c + 1) * P], src[:, t, c * P:(c + 1) * P], ident)
                    units.finish(("rwT", 4 * t + j), ins)
            units.wait_emptied(*(("O", i) for i in range(NA)))
            bank = units.begin(("attT", 0))
            for k in range(2):
                for t in range(T):
                    ins = pe.transpose(bank[:, k * SEQ + t * P:k * SEQ + (t + 1) * P], att[:, t, k * P:(k + 1) * P], ident)
            units.finish(("attT", 0), ins)
            w = weights(("att_out", 0))
            units.wait_emptied(("attT", 0))
            for u in range(2 * T):
                t, c = u // 2, u % 2
                token_major(pe, units, ("yatt", u), lambda k: attT[:, k, t * P:(t + 1) * P], w[:, :, c * 512:(c + 1) * 512])
            units.wait_emptied(*(("rwT", j) for j in range(8)))
            for t in range(T):
                tok = slice(t * P, (t + 1) * P)
                for par in range(2):
                    r, n = slice(RW_E * par, RW_E * (par + 1)), 2 * t + par
                    A, B, K, Rr = (rwT[j][r] for j in range(4))
                    for name, left_m, right_m in (("NT", B, A), ("N", A, B), ("Mak", K, A), ("Mrb", B, Rr), ("Mrk", K, Rr)):
                        bank = units.begin((name, n))
                        for c in range(PAIRS):
                            ins = pe.matmul(bank[:, c * P:(c + 1) * P], left_m[:, c, tok], right_m[:, c, tok],
                                            start=True, stop=True)
                        units.finish((name, n), ins)
                for i in range(len(LEVELS)):
                    for par in range(2):
                        n, m = 2 * t + par, core[par]
                        if i == 0:
                            pe.wait_ge(core_start, n + 1)
                        else:
                            units.wait_emptied(("TX", 8 * n + i - 1), ("XT", 8 * n + i - 1))
                        bank = units.begin(("X", 8 * n + i))
                        for c in range(PAIRS):
                            ins = pe.matmul(bank[:, c * P:(c + 1) * P], m["NT"][:, c, :], m["T"][:, c, :], start=True, stop=True)
                        units.finish(("X", 8 * n + i), ins)
                    for par in range(2):
                        n, m = 2 * t + par, core[par]
                        units.wait_emptied(("X", 8 * n + i))
                        if i < len(LEVELS) - 1:
                            bank = units.begin(("TX", 8 * n + i))
                            for c in range(PAIRS):
                                ins = pe.matmul(bank[:, c * P:(c + 1) * P], m["TT"][:, c, :], m["X"][:, c, :], start=True, stop=True)
                            units.finish(("TX", 8 * n + i), ins)
                        bank = units.begin(("XT", 8 * n + i))
                        for c in range(PAIRS):
                            o = bank[:, c * P:(c + 1) * P]
                            pe.matmul(o, ident, m["TT"][:, c, :], start=True, stop=False)
                            ins = pe.matmul(o, m["X"][:, c, :], m["TT"][:, c, :], start=False, stop=True)
                        units.finish(("XT", 8 * n + i), ins)

                def value(c, par):
                    h = 2 * c + par
                    return pf[:, t, C_V + h * RW_E:C_V + (h + 1) * RW_E]

                if t:
                    pe.wait_ge(state_ready, 1)
                for par in range(2):
                    n, m, r = 2 * t + par, core[par], slice(RW_E * par, RW_E * (par + 1))
                    units.wait_emptied(("Mak", n), ("Mrb", n), ("Mrk", n), ("XT", 8 * n + len(LEVELS) - 1))
                    bank = units.begin(("RHS", n))
                    for c in range(PAIRS):
                        o = bank[:, c * RW_E:(c + 1) * RW_E]
                        ins = pe.matmul(o, m["Mak"][:, c, :], value(c, par), start=True, stop=(t == 0))
                        if t:
                            ins = pe.matmul(o, rwT[0][r, c, tok], minus_state[r, c, :], start=False, stop=True)
                    units.finish(("RHS", n), ins)
                for par in range(2):
                    n, m = 2 * t + par, core[par]
                    units.wait_emptied(("RHS", n))
                    bank = units.begin(("U", n))
                    for c in range(PAIRS):
                        ins = pe.matmul(bank[:, c * RW_E:(c + 1) * RW_E], m["TT"][:, c, :], rhs[par][:, c, :], start=True, stop=True)
                    units.finish(("U", n), ins)
                for par in range(2):
                    n, m, r = 2 * t + par, core[par], slice(RW_E * par, RW_E * (par + 1))
                    units.wait_emptied(("U", n))
                    bank = units.begin(("OUT", n))
                    for c in range(PAIRS):
                        o = bank[:, c * RW_E:(c + 1) * RW_E]
                        pe.matmul(o, m["Mrb"][:, c, :], rw_u[:, 2 * c + par, :], start=True, stop=False)
                        ins = pe.matmul(o, m["Mrk"][:, c, :], value(c, par), start=False, stop=(t == 0))
                        if t:
                            ins = pe.matmul(o, rwT[3][r, c, tok], state[r, c, :], start=False, stop=True)
                    units.finish(("OUT", n), ins)
                if t == 0:
                    bank = units.begin(("state", 0))
                    for c in range(PAIRS):
                        o, cols = bank[:, c * P:(c + 1) * P], slice(c * P, (c + 1) * P)
                        pe.matmul(o, bufB[:, 0, cols], rw_u[:, 2 * c:2 * c + 2, :].rearrange("p h e -> p (h e)"), start=True, stop=False)
                        ins = pe.matmul(o, bufK[:, 0, cols], pf[:, 0, C_V + c * P:C_V + (c + 1) * P], start=False, stop=True)
                    units.finish(("state", 0), ins)
            pe.wait_ge(o_ready, 1)
            for j in range(2):
                bank = units.begin(("oT", j))
                for kk in range(2):
                    for t in range(T):
                        k = 2 * j + kk
                        ins = pe.transpose(bank[:, kk * SEQ + t * P:kk * SEQ + (t + 1) * P], bufA[:, t, k * P:(k + 1) * P], ident)
                units.finish(("oT", j), ins)
            w = weights(("rwkv_out", 0))
            units.wait_emptied(("oT", 0), ("oT", 1))
            for u in range(2 * T):
                t, c = u // 2, u % 2
                token_major(pe, units, ("yrw", u), lambda k: oT[:, k, t * P:(t + 1) * P], w[:, :, c * 512:(c + 1) * 512])
            pe.wait_ge(mixed, 1)
            transposes(pe, units, "mixT", gates[:, :, 0:D])
            units.wait_emptied(*(("mixT", j) for j in range(4)))
            for c in range(2):
                w = weights(("out", c))
                for t in range(T):
                    token_major(pe, units, ("wout", T * c + t), lambda k: hT[:, k, t * P:(t + 1) * P], w)
            pe.wait_ge(xn2_ready, 2 * T)
            transposes(pe, units, "tr2", xn2)
            units.wait_emptied(*(("tr2", j) for j in range(4)))
            pe.wait_ge(route_loaded, 48)
            for t in range(T):
                token_major(pe, units, ("route", t), lambda k: hT[:, k, t * P:(t + 1) * P], w_route)
            pe.wait_ge(fills_ready, 1)
            pe.wait_ge(taken_ready, 1)
            for i in range(T + 1):
                bank = units.begin(("rank", i))[:, 0:NE]
                left = [ones] * i + [second("incl")] if i < T else [ones] * T
                for s, m in enumerate(left):
                    ins = pe.matmul(bank, m, taken[:, s, :], start=(s == 0), stop=(s == len(left) - 1))
                units.finish(("rank", i), ins)
            units.wait_emptied(*(("route", t) for t in range(T)), *(("rank", i) for i in range(T + 1)))
            final = UnitView(FU, pe, psum)
            for u in range(2 * T):
                pe.matmul(final.bank(("acc", u)), zeros, second("levels")[:, 0:512], start=True, stop=False)
            pe.sem_inc(EU.full, EU.n)
            pe.wait_ge(places_ready, 1)
            with pe.Fori(0, pe.value_load(turns_i[0:1, 0:1], min_val=TURNS, max_val=TURNS * PASSES)) as turn:
                units = UnitView(EU, pe, psum, turn)

                def arrived(s, k):
                    pe.wait_ge(moe_loaded[s], turn * 16 + 16)
                    return moe_slot[s].rearrange("p (k n) -> p k n", k=k)

                take_ready.wait(pe, 1, turn)
                for i in range(2):
                    bank = units.begin(("gx", i))
                    for kk in range(4):
                        k = 4 * i + kk
                        for t in range(T):
                            ins = pe.matmul(bank[:, kk * P:(kk + 1) * P], xn2[:, t, k * P:(k + 1) * P],
                                            take[:, t, :, :].rearrange("p j n -> p (j n)"), start=(t == 0), stop=(t == T - 1))
                    units.finish(("gx", i), ins)
                bank = units.begin(("gt", 0))
                for t in range(T):
                    ins = pe.transpose(bank[:, t * P:(t + 1) * P], give[:, t, :, :].rearrange("p j n -> p (j n)"), ident)
                units.finish(("gt", 0), ins)
                units.wait_emptied(("gx", 0), ("gx", 1))
                half = lambda j: slice(j * SLOTS_E, (j + 1) * SLOTS_E)
                for i, stage in enumerate(("gate", "up")):
                    w = [arrived(EPT * i + j, KD) for j in range(EPT)]
                    bank = units.begin((stage, 0))
                    for k in range(KD):
                        for j in range(EPT):
                            ins = pe.matmul(bank[half(j), :], xe[:, k, half(j)], w[j][:, k, :], start=(k == 0), stop=(k == KD - 1))
                    units.finish((stage, 0), ins)
                units.wait_emptied(("up", 0))
                bank = units.begin(("hT", 0))
                for f in range(D_EXP // P):
                    ins = pe.transpose(bank[:, f * P:(f + 1) * P], hid[:, f * P:(f + 1) * P], ident)
                units.finish(("hT", 0), ins)
                w = [arrived(2 * EPT + j, D_EXP // P) for j in range(EPT)]
                units.wait_emptied(("hT", 0))
                for c in range(2):
                    bank = units.begin(("y", c))
                    for f in range(D_EXP // P):
                        for j in range(EPT):
                            ins = pe.matmul(bank[half(j), :], hidT[:, f, half(j)], w[j][:, f, c * 512:(c + 1) * 512],
                                            start=(f == 0), stop=(f == D_EXP // P - 1))
                    units.finish(("y", c), ins)
                units.wait_emptied(("gt", 0), ("y", 0), ("y", 1))
                for u in range(2 * T):
                    t, c = u // 2, u % 2
                    pe.matmul(final.bank(("acc", u)), giveT[:, t * P:(t + 1) * P], y_rows[:, c * 512:(c + 1) * 512],
                              start=False, stop=False)
            for u in range(2 * T):
                final.finish(("acc", u), pe.matmul(final.bank(("acc", u)), zeros, second("levels")[:, 0:512], start=False, stop=True))

        def sums_of_squares(act, parts, ready):
            for rows, scratch, c, _ in parts:
                act.activation(scratch, rows, ACT.Square, accum_out=sumsq[:, c:c + 1])
            act.drain()
            for _, _, c, width in parts:
                ins = act.activation(std[:, c:c + 1], sumsq[:, c:c + 1], ACT.Sqrt, bias=eps_c, scale=1.0 / width)
            ins.then_inc(ready, 1)

        def act_transposed(act, units, stage, gain):
            for j in range(0, 4, 2):
                bank = units.wait_full((stage, j))
                for kk in range(2):
                    k = 2 * j + kk
                    ins = act.activation(hT[:, k, :], bank[:, kk * SEQ:(kk + 1) * SEQ], ACT.Copy, scale=gain(k))
                units.emptied_by((stage, j), ins, "A")

        def dve_transposed(dve, units, stage, gain):
            for j in range(1, 4, 2):
                bank = units.wait_full((stage, j))
                for kk in range(2):
                    k = 2 * j + kk
                    ins = dve.tensor_scalar(hT[:, k, :], bank[:, kk * SEQ:(kk + 1) * SEQ], gain(k), None, ALU.mult)
                units.emptied_by((stage, j), ins, "V")

        @block.scalar
        def _(act):
            act.wait_ge(x_loaded, 16)
            act.wait_ge(consts_set, 1)
            with act.Fori(0, DEPTH) as l:
                units = UnitView(LU, act, psum, l)

                def gain(first_col):
                    return lambda k: gains[:, first_col + k:first_col + k + 1]

                def copy_out(key, dst, n):
                    bank = units.wait_full(key)
                    units.emptied_by(key, act.activation(dst, bank[:, 0:n], ACT.Copy), "A")

                x_done.wait(act, 1, l)
                act.dma_start(gains[:], io["gains"][l]).then_inc(gains_loaded, 16)
                sums_of_squares(act, [(x[:, t, :], xn[:, t, :], t, D) for t in range(T)], std_ready.sem)
                act.wait_ge(gains_loaded, l * 16 + 16)
                act_transposed(act, units, "tr1", gain(G_MIX))
                for b, (c, w) in enumerate(IN_BLOCKS):
                    copy_out(("proj", T * b + 1), proj[:, 1, c:c + w], w)
                units.wait_emptied(*(("proj", T * b + t) for t in range(T) for b in range(2)))
                sums_of_squares(act, [(proj[:, t, C_CQ:C_CKV], xn[:, t, C_CQ:C_CKV], t, Q_RANK) for t in range(T)] +
                                [(proj[:, t, C_CKV:C_KR], xn[:, t, C_CKV:C_KR], T + t, KV_RANK) for t in range(T)], std_ready.sem)
                act_transposed(act, units, "tr2", gain(G_QKV))
                for i, (t, heads) in enumerate(IDX_UNITS):
                    bank, n = units.wait_full(("idxS", i)), len(heads) * (t + 1) * P
                    if i >= 2:
                        rel_read.wait(act, i - 1, l)
                    else:
                        idx_roped.wait(act, 1, l)
                        kr_roped.wait(act, 1, l)
                    units.emptied_by(("idxS", i), act.activation(rel[:, i % 2, 0:n], bank[:, 0:n], ACT.Relu), "A")
                w = MLA_H * QK // 2
                for c in range(2):
                    for t in range(T):
                        copy_out(("uq", T * c + t),
                                 q[:, t, :, :].rearrange("p h e -> p (h e)")[:, c * w:(c + 1) * w], w)
                for c in range(2):
                    for t in range(T):
                        copy_out(("ukv", T * c + t),
                                 kv[:, t, 4 * c:4 * c + 4, :].rearrange("p h e -> p (h e)"), 512)
                units.wait_emptied(*(("ukv", j) for j in range(2 * T)))
                kr_roped.wait(act, 1, l)
                for t in range(T):
                    act.activation(kfull[:, t, :, 0:NOPE], kv[:, t, :, 0:NOPE], ACT.Copy)
                    ins = act.activation(kfull[:, t, :, NOPE:QK],
                                         proj[:, t, None, C_KR:C_AQ].to_broadcast([P, MLA_H, ROPE]), ACT.Copy)
                ins.then_inc(kfull_ready.sem, 1)
                for t in range(T):
                    bank = units.wait_full(("dsaT", t))
                    units.emptied_by(("dsaT", t), act.activation(
                        dsaT[:, :, t * P:(t + 1) * P], bank[:, 0:3 * P].rearrange("p (c s) -> p c s", c=3), ACT.Copy), "A")
                for t in range(T):
                    bank = units.wait_full(("retT", t))
                    units.emptied_by(("retT", t), act.activation(
                        retT[:, :, t * P:(t + 1) * P], bank.rearrange("p (c s) -> p c s", c=4), ACT.Copy), "A")
                for t in range(T):
                    for j in range(4):
                        bank = units.wait_full(("mlaT", 4 * t + j))
                        dst = (qTm, kTm)[j // 2][0:QK, 4 * (j % 2):4 * (j % 2) + 4, t * P:(t + 1) * P]
                        units.emptied_by(("mlaT", 4 * t + j), act.activation(
                            dst, bank[0:QK, :].rearrange("p (c s) -> p c s", c=4), ACT.Copy), "A")
                width = lambda g: len(GROUPS[g][2]) * (GROUPS[g][1] + 1) * P
                for i in range(NG + 1):
                    if i < NG:
                        shifted.wait(act, i + 1, l)
                        act.activation(scores[i % 2][:, 0:width(i)], scores[i % 2][:, 0:width(i)], ACT.Exp).then_inc(probs_ready.sem, 1)
                    if i >= 1:
                        g = i - 1
                        bank = units.wait_full(("PT", g))
                        units.emptied_by(("PT", g), act.activation(probsT[g % 2][:, 0:width(g)], bank[:, 0:width(g)], ACT.Copy), "A")
                act.activation(proj[:, :, C_RG:IN_W], proj[:, :, C_RG:IN_W], ACT.Silu).then_inc(silu_ready.sem, 1)
                ret_var_ready.wait(act, 1, l)
                act.activation(ret_rstd, ret_var, ACT.Sqrt, bias=eps_c, scale=1.0 / RET_E).then_inc(ret_std_ready.sem, 1)
                for j in range(0, 4, 2):
                    bank = units.wait_full(("mixT", j))
                    units.emptied_by(("mixT", j), act.activation(
                        hT[:, 2 * j:2 * j + 2, :].rearrange("p k s -> p (k s)"), bank, ACT.Copy), "A")
                units.wait_emptied(("wout", 2 * T - 1))
                sums_of_squares(act, [(x[:, t, :], xn[:, t, :], t, D) for t in range(T)], std_ready.sem)
                act_transposed(act, units, "tr3", gain(G_MLP))
                for i in range(2 * FFB):
                    b, j = i // 2, i % 2
                    units.wait_emptied(("ff1", i))
                    if b >= 2:
                        units.wait_full(("ff1", 2 * b))
                    act.activation(uT[:, b % 2, 2 * j:2 * j + 2, :].rearrange("p f s -> p (f s)"),
                                   relu_h[i % 4], ACT.Square).then_inc(hid_ready.sem, 1)
            units = UnitView(SU, act, psum)

            def gain2(first_col):
                return lambda k: gains[:, first_col + k:first_col + k + 1]

            def empty(key, dst, n, func=ACT.Copy):
                bank = units.wait_full(key)
                units.emptied_by(key, act.activation(dst, bank[:, 0:n], func), "A")

            x_rows = lambda: [(x[:, t, :], xn2[:, t, :], t, D) for t in range(T)]
            x_done.wait(act, DEPTH + 1)
            act.dma_start(gains[:, 0:2 * KD], io["gains2"]).then_inc(gains2_loaded, 16)
            act.dma_start(phase_c[:], io["second_c"]).then_inc(second_c_loaded, 16)
            sums_of_squares(act, x_rows(), std2_ready)
            act.wait_ge(x_normed, 1)
            sums_of_squares(act, x_rows(), std2_ready)
            act.wait_ge(gains2_loaded, 16)
            act_transposed(act, units, "tr1", gain2(0))
            for b, (c, w) in enumerate(RW_BLOCKS):
                empty(("rw", T * b + 1), pf[:, 1, c:c + w], w)
            for b, (c, w) in enumerate(QKV_BLOCKS):
                empty(("qkv", T * b + 1), qkv[:, 1, c:c + w], w)
            act.wait_ge(pm_ready, 1)
            act.activation(pf[:, :, C_XG:RW_IN], pf[:, :, C_XG:RW_IN], ACT.Sigmoid)
            act.activation(pf[:, :, C_XW:C_XA], pf[:, :, C_XW:C_XA], ACT.Tanh).then_inc(lora_in, 1)
            for t in range(T):
                bank = units.wait_full(("loraT", t))
                act.activation(loraT[:, 0:2, t * P:(t + 1) * P], bank[:, 0:2 * P].rearrange("p (j s) -> p j s", j=2), ACT.Copy)
                units.emptied_by(("loraT", t), act.activation(
                    loraT[0:LORA_G - P, 2, t * P:(t + 1) * P], bank[0:LORA_G - P, 2 * P:3 * P], ACT.Copy), "A")
            for t in range(T):
                empty(("lora", 3 * t + 2), rw_g[:, t, :], RW_W)
            act.wait_ge(wa_in, 1)
            act.activation(bufB, bufB, ACT.Sigmoid)
            act.activation(bufR, bufR, ACT.Sigmoid).then_inc(wa_ready, 1)
            for b, (c, w) in enumerate(GATE_BLOCKS):
                for t in range(T):
                    empty(("gate", T * b + t), gates[:, t, c:c + w], w, ACT.Sigmoid)
            act.wait_ge(kk_ss, 1)
            act.activation(kk_n, kk_n, ACT.Sqrt).then_inc(kk_std, 1)
            act.wait_ge(qk_ss_ready, 1)
            act.activation(stat2[:, 0:48], stat2[:, 0:48], ACT.Sqrt, bias=eps_c, scale=1.0 / ATT_E).then_inc(qk_std, 1)
            for j in range(6):
                dst = (qT, kT)[j // 3][:, 2 * (j % 3):2 * (j % 3) + 2, :].rearrange("p c s -> p (c s)")
                empty(("qkT", j), dst, 512)
            for i in range(NA + 1):
                if i < NA:
                    n = GRP * (ATT_UNITS[i][0] + 1) * P
                    act.wait_ge(att_max, i + 1)
                    act.activation(att_s[i % 2][:, 0:n], units.wait_full(("S", i))[:, 0:n], ACT.Exp,
                                   bias=rowmax[:, i % 2:i % 2 + 1], accum_out=rowsum[:, i % 2:i % 2 + 1])
                    act.drain()
                    units.emptied_by(("S", i), act.activation(stat[:, 91:92], stat[:, 91:92], ACT.Copy), "A")
                    act.sem_inc(att_exp, 1)
                if i >= 1:
                    n = GRP * (ATT_UNITS[i - 1][0] + 1) * P
                    if i >= 2:
                        units.wait_full(("O", i - 2))
                    empty(("PT", i - 1), att_p[:, 0:n], n)
            for t in range(T):
                incl, excl = units.wait_full(("cum", 2 * t)), units.wait_full(("cum", 2 * t + 1))
                act.wait_ge(preproc_done, 1)
                if t:
                    units.wait_full(("sdec", 0))
                act.activation(bufK[:, t, :], incl, ACT.Exp, scale=-1.0)
                act.activation(excl, excl, ACT.Exp).then_inc(exp_excl, 1)
                if t == 0:
                    units.wait_full(("sdec", 0))
                act.activation(bufR[:, t, :], incl, ACT.Exp)
                act.drain()
                units.emptied_by(("cum", 2 * t), act.activation(stat[:, 90:91], stat[:, 90:91], ACT.Copy), "A")
                act.sem_inc(exp_incl, 1)
            empty(("sdec", 0), sdec, PAIRS, ACT.Exp)
            for t in range(T):
                for j in range(4):
                    bank = units.wait_full(("rwT", 4 * t + j))
                    units.emptied_by(("rwT", 4 * t + j), act.activation(
                        rwT[j][:, :, t * P:(t + 1) * P], bank.rearrange("p (c s) -> p c s", c=PAIRS), ACT.Copy), "A")
            empty(("attT", 0), hTs[:, 512:1024], 512)
            for t in range(T):
                for i in range(len(LEVELS)):
                    for par in range(2):
                        empty(("XT", 8 * (2 * t + par) + i), core[par]["TT"].rearrange("p c s -> p (c s)"), 512)
                for par in range(2):
                    empty(("RHS", 2 * t + par), rhs[par].rearrange("p c e -> p (c e)"), PAIRS * RW_E)
                for par in range(2):
                    bank = units.wait_full(("U", 2 * t + par))
                    units.emptied_by(("U", 2 * t + par), act.activation(
                        rw_u[:, par:RW_H:2, :], bank[:, 0:PAIRS * RW_E].rearrange("p (c e) -> p c e", c=PAIRS), ACT.Copy), "A")
            act.wait_ge(gn_ss, 1)
            act.activation(rw_var, rw_var, ACT.Sqrt, bias=gn_eps_c, scale=1.0 / RW_E).then_inc(gn_std, 1)
            for j in range(2):
                empty(("oT", j), oT[:, 2 * j:2 * j + 2, :].rearrange("p k s -> p (k s)"), 512)
            for j in range(4):
                empty(("mixT", j), hT[:, 2 * j:2 * j + 2, :].rearrange("p k s -> p (k s)"), 512)
            units.wait_emptied(("wout", 2 * T - 1))
            sums_of_squares(act, x_rows(), std2_ready)
            act_transposed(act, units, "tr2", gain2(KD))
            act.wait_ge(route_max, 1)
            act.activation(ra[0][:, 0:T * EG], ra[0][:, 0:T * EG], ACT.Exp).then_inc(route_exp, 1)
            act.wait_ge(pair_diff, 1)
            act.activation(ra[5][:, 0:T], ra[5][:, 0:T], ACT.Exp).then_inc(pair_exp, 1)
            act.wait_ge(places_ready, 1)
            with act.Fori(0, act.value_load(turns_i[0:1, 0:1], min_val=TURNS, max_val=TURNS * PASSES)) as turn:
                units = UnitView(EU, act, psum, turn)
                bank = units.wait_full(("gt", 0))
                units.emptied_by(("gt", 0), act.activation(giveT, bank[:, 0:SEQ], ACT.Copy), "A")
                bank = units.wait_full(("gate", 0))
                units.emptied_by(("gate", 0), act.activation(silu_g, bank, ACT.Silu), "A")
                bank = units.wait_full(("hT", 0))
                units.emptied_by(("hT", 0), act.activation(hidT.rearrange("p f n -> p (f n)"), bank, ACT.Copy), "A")
                bank = units.wait_full(("y", 0))
                units.emptied_by(("y", 0), act.activation(y_rows[:, 0:512], bank, ACT.Copy), "A")

        def rotate(e, x1, x2, cos, sin, tmp):
            shape = x1.shape
            cos, sin = (a.unsqueeze(2).to_broadcast(shape) for a in (cos, sin))
            m1, m2 = (b[:, 0:int(np.prod(shape[1:]))].rearrange("p (t h e) -> p t h e", t=shape[1], h=shape[2]) for b in tmp)
            e.tensor_tensor(m1, x1, sin, ALU.mult)
            e.tensor_tensor(m2, x2, sin, ALU.mult)
            e.drain()
            e.tensor_tensor(x1, x1, cos, ALU.mult)
            e.tensor_tensor(x2, x2, cos, ALU.mult)
            e.drain()
            e.tensor_tensor(x1, x1, m2, ALU.subtract)
            return e.tensor_tensor(x2, x2, m1, ALU.add)

        def angles(dim):
            return (first(f"{n}{dim}").rearrange("p (t e) -> p t e", t=T) for n in ("cos", "sin"))

        def halves(a):
            e = a.shape[3] // 2
            return a[:, :, :, 0:e], a[:, :, :, e:2 * e]

        def heads_of(c0, c1, e):
            return proj[:, :, c0:c1].rearrange("p t (h e) -> p t h e", e=e)

        @block.gpsimd
        def _(pool):
            pool.wait_ge(consts_loaded, 32)
            with pool.Fori(0, DEPTH) as l:
                units = UnitView(LU, pool, psum, l)

                def wait_columns(c0, c1):
                    units.wait_emptied(*(("proj", T * b + t) for t in range(T)
                                         for b, (c, w) in enumerate(IN_BLOCKS) if c < c1 and c0 < c + w))

                wait_columns(C_AQ, C_AV)
                rotate(pool, *halves(heads_of(C_AQ, C_AV, DSA_E)), *angles(DSA_E), pool_tmp)
                pool.drain()
                for t in range(T):
                    ins = pool.tensor_copy(kd[:, t, :, :], proj[:, t, None, C_AK:C_AV].to_broadcast([P, 2, DSA_E]))
                ins.then_inc(dsa_roped.sem, 1)
                wait_columns(C_RQ, C_RV)
                rotate(pool, *halves(heads_of(C_RQ, C_RV, RET_E)), *angles(RET_E), pool_tmp).then_inc(ret_roped.sem, 1)
            units = UnitView(SU, pool, psum)

            def row(name):
                o, w = ROWS[name]
                return io["rows2"][0:1, o:o + w].to_broadcast([P, w])

            pool.wait_ge(x_done.sem, DEPTH + 1)
            pool.dma_start(g_final, row("g_final")).then_inc(g_final_loaded, 16)
            pool.dma_start(mu, row("mu")).then_inc(mu_loaded, 16)
            pool.dma_start(bias_tab[0:BUCKETS, :], io["rel_bias_table_2"]).then_inc(bias_tab_loaded, 16)
            pool.dma_start(bias_tab[BUCKETS:BUCKETS + ATT_H, :], io["shared_c"][0:ATT_H, 0:ATT_H]).then_inc(bias_tab_loaded, 16)
            for j, n in enumerate(("q_gain", "k_gain")):
                pool.dma_start(qk_gain[:, j, :, :].rearrange("p g e -> p (g e)"), row(n)).then_inc(qk_gain_loaded, 16)
            pool.dma_start(lora_w[0:LORA_W, 0, :], io["rwkv_w_up_2"][0]).then_inc(lora_loaded, 16)
            pool.dma_start(lora_w[LORA_W:P, 0, :], io["rwkv_a_up_2"][0]).then_inc(lora_loaded, 16)
            pool.dma_start(lora_w[:, 1, :], io["rwkv_g_up_2"][0, 0:P, :]).then_inc(lora_loaded, 16)
            pool.dma_start(lora_w[0:LORA_G - P, 2, :], io["rwkv_g_up_2"][0, P:LORA_G, :]).then_inc(lora_loaded, 16)
            pool.memset(prev[0:1, 0, :], 0.0).then_inc(prev_zero, 1)
            units.wait_emptied(*(("rw", j) for j in range(PROJ_RW)))
            for t in range(T):
                pool.dma_start(prev[1:P, t, :], pf[0:P - 1, t, :]).then_inc(prev_loaded, 16)
            pool.dma_start(prev[0:1, 1, :], pf[P - 1:P, 0, :]).then_inc(prev_loaded, 16)
            pool.wait_ge(pm_ready, 1)
            for n in vec:
                pool.dma_start(vec[n], row(n)).then_inc(vec_loaded, 16)
            pool.wait_ge(bias_done, 1)
            pool.dma_start(bias_dram, bias_row[0:ATT_H, :]).then_inc(bias_stored, 16)
            pool.wait_ge(bias_stored, 16)
            pool.wait_ge(qk_ready, 1)
            pool.dma_start(bias_m, bass.AP(bias_dram.tensor, 0, [[1, P], [384, ATT_H], [1, SEQ]])).then_inc(bias_loaded, 16)
            pool.wait_ge(bonus_ready, 1)
            pool.wait_ge(scaled, T)
            pool.dma_start(w_route[:, :, 0:EG], io["w_group_router_2"][0].rearrange("(k p) n -> p k n", p=P)).then_inc(route_loaded, 16)
            pool.dma_start(w_route[:, :, EG:], io["w_expert_router_2"][0].rearrange("(k p) n -> p k n", p=P)).then_inc(route_loaded, 16)
            pool.dma_start(b_route, row("b_route")).then_inc(route_loaded, 16)
            pool.tensor_tensor(pf[:, :, C_R:C_K].rearrange("p t (h e) -> p t h e", e=RW_E),
                               pf[:, :, C_V:C_XW].rearrange("p t (h e) -> p t h e", e=RW_E),
                               bonus.rearrange("p (t h) -> p t h", t=T).unsqueeze(3).to_broadcast([P, T, RW_H, RW_E]),
                               ALU.mult).then_inc(bonus_v, 1)
            pool.memset(zeros, 0.0)
            pool.memset(ones, 1.0).then_inc(fills_ready, 1)
            eye = ident.unsqueeze(1).to_broadcast([P, PAIRS, P])
            for n, (t, par) in enumerate(CORE):
                m = core[par]
                pool.wait_ge(core_masked, n + 1)
                pool.tensor_tensor(m["TT"], m["NT"], second("level1T").unsqueeze(1).to_broadcast([P, PAIRS, P]), ALU.mult)
                pool.tensor_tensor(m["T"], m["T"], eye, ALU.add)
                pool.drain()
                pool.tensor_tensor(m["TT"], m["TT"], eye, ALU.add).then_inc(core_start, 1)

        def scale_rows(dve, parts):
            dve.reciprocal(rstd, std)
            dve.drain()
            for rows, scaled, c in parts:
                ins = dve.tensor_scalar(scaled, rows, rstd[:, c:c + 1], None, ALU.mult)
            return ins

        @block.vector
        def _(dve):
            dve.memset(stat[:], 1.0)
            dve.drain()
            dve.memset(eps_c, EPS).then_inc(consts_set, 1)
            dve.wait_ge(consts_loaded, 32)
            dve.wait_ge(x_loaded, 16)
            dve.sem_inc(x_done.sem, 1)
            with dve.Fori(0, DEPTH) as l:
                units = UnitView(LU, dve, psum, l)

                def gain(first_col):
                    return lambda k: gains[:, first_col + k:first_col + k + 1]

                def norm(k):
                    std_ready.wait(dve, k, l)
                    scale_rows(dve, [(x[:, t, :], xn[:, t, :], t) for t in range(T)]).then_inc(xn_ready.sem, T)

                def wait_columns(c0, c1):
                    units.wait_emptied(*(("proj", T * b + t) for t in range(T)
                                         for b, (c, w) in enumerate(IN_BLOCKS) if c < c1 and c0 < c + w))

                norm(1)
                dve.wait_ge(gains_loaded, l * 16 + 16)
                dve_transposed(dve, units, "tr1", gain(G_MIX))
                for b, (c, w) in enumerate(IN_BLOCKS):
                    bank = units.wait_full(("proj", T * b))
                    units.emptied_by(("proj", T * b), dve.tensor_copy(proj[:, 0, c:c + w], bank[:, 0:w]), "V")
                wait_columns(C_QI, C_RQ)
                rotate(dve, *halves(heads_of(C_QI, C_WI, IDX_E)), *angles(IDX_E), dve_tmp)
                dve.drain()
                dve.tensor_scalar(wi, proj[:, :, C_WI:C_RQ], IDX_H ** -0.5 * IDX_E ** -0.5, None, ALU.mult)
                for t in range(T):
                    ins = dve.tensor_copy(ki4[:, t, :, :], proj[:, t, None, C_KI:C_WI].to_broadcast([P, 4, IDX_E]))
                ins.then_inc(idx_roped.sem, 1)
                std_ready.wait(dve, 2, l)
                scale_rows(dve, [(proj[:, t, C_CQ:C_CKV], xn[:, t, C_CQ:C_CKV], t) for t in range(T)] +
                           [(proj[:, t, C_CKV:C_KR], xn[:, t, C_CKV:C_KR], T + t) for t in range(T)]
                           ).then_inc(xn_ready.sem, T)
                wait_columns(C_KR, C_AQ)
                rotate(dve, *halves(heads_of(C_KR, C_AQ, ROPE)), *angles(ROPE), dve_tmp).then_inc(kr_roped.sem, 1)
                for t in range(T):
                    bank = units.wait_full(("idxT", t))
                    units.emptied_by(("idxT", t), dve.tensor_copy(
                        idxT[:, :, t * P:(t + 1) * P], bank[:, 0:3 * P].rearrange("p (c s) -> p c s", c=3)), "V")
                dve_transposed(dve, units, "tr2", gain(G_QKV))
                for t in range(T):
                    nk = (t + 1) * P
                    s, r = score[:, 0:nk], left[:, 0:nk]
                    for i, (ti, heads) in enumerate(IDX_UNITS):
                        if ti != t:
                            continue
                        if heads[0]:
                            dve.drain()
                        units.wait_emptied(("idxS", i))
                        for j, h in enumerate(heads):
                            rel_h = rel[:, i % 2, j * nk:(j + 1) * nk]
                            if h == 0:
                                ins = dve.tensor_scalar(s, rel_h, wi[:, t, h:h + 1], None, ALU.mult)
                            else:
                                if j:
                                    dve.drain()
                                ins = dve.scalar_tensor_tensor(s, rel_h, wi[:, t, h:h + 1], s, ALU.mult, ALU.add)
                        ins.then_inc(rel_read.sem, 1)
                    dve.drain()
                    hidden = causal[:, T * P - nk:T * P]
                    dve.tensor_tensor(s, s, hidden, ALU.add)
                    dve.drain()
                    for i in range(TOPK // 8):
                        dve.max(top8, r if i else s)
                        dve.drain()
                        dve.match_replace(r, top8, r if i else s, TAKEN)
                        dve.drain()
                    dve.tensor_scalar(r, r, TAKEN, -MASKED, ALU.is_equal, ALU.mult)
                    dve.drain()
                    dve.scalar_tensor_tensor(dsa_mask[:, t, 0:nk], r, MASKED, hidden, ALU.add, ALU.add)
                units.wait_emptied(*(("uq", j) for j in range(2 * T)))
                rotate(dve, *halves(q[:, :, :, NOPE:QK]), *angles(ROPE), dve_tmp).then_inc(q_roped.sem, 1)
                decay = first("decay").rearrange("p (d h s) -> p d h s", d=T, h=RET_H)
                for i, (t, s, h0) in enumerate(RET_UNITS):
                    bank = units.wait_full(("retS", i))
                    units.emptied_by(("retS", i), dve.tensor_tensor(
                        ret_s[i].rearrange("p (h s) -> p h s", h=2), bank[:, 0:2 * P].rearrange("p (h s) -> p h s", h=2),
                        decay[:, t - s, h0:RET_H:2, :], ALU.mult), "V")

                def mask_and_shift(g):
                    dsa, t, heads = GROUPS[g]
                    nk, nh = (t + 1) * P, len(heads)
                    bank = units.wait_full(("S", g))[:, 0:nh * nk].rearrange("p (h k) -> p h k", h=nh)
                    s = scores[g % 2][:, 0:nh * nk].rearrange("p (h k) -> p h k", h=nh)
                    mask = dsa_mask[:, t, 0:nk] if dsa else causal[:, T * P - nk:T * P]
                    scale = DSA_E ** -0.5 if dsa else QK ** -0.5
                    units.emptied_by(("S", g), dve.scalar_tensor_tensor(
                        s, bank, scale, mask.unsqueeze(1).to_broadcast([P, nh, nk]), ALU.mult, ALU.add), "V")
                    dve.drain()
                    dve.tensor_reduce(rowmax[:, 0:nh], s, AX.X, ALU.max)
                    dve.drain()
                    dve.tensor_tensor(s, s, rowmax[:, 0:nh].unsqueeze(2).to_broadcast([P, nh, nk]),
                                      ALU.subtract).then_inc(shifted.sem, 1)

                def row_sums(g):
                    nh, n = len(GROUPS[g][2]), len(GROUPS[g][2]) * (GROUPS[g][1] + 1) * P
                    probs_ready.wait(dve, g + 1, l)
                    dve.tensor_reduce(rowsum[:, 0:nh], scores[g % 2][:, 0:n].rearrange("p (h k) -> p h k", h=nh), AX.X, ALU.add)
                    dve.drain()
                    dve.reciprocal(rinv[g % 3][:, 0:nh], rowsum[:, 0:nh])
                    dve.drain()

                def attend_out(g):
                    dsa, t, heads = GROUPS[g]
                    bank, nh = units.wait_full(("O", g)), len(heads)
                    first_head = heads[0] + (MLA_H if dsa else 0)
                    step = heads[1] - heads[0]
                    units.emptied_by(("O", g), dve.tensor_tensor(
                        mix[:, t, :].rearrange("p (h e) -> p h e", e=MLA_V)[:, first_head:first_head + step * (nh - 1) + 1:step, :],
                        bank[:, 0:nh * MLA_V].rearrange("p (h e) -> p h e", h=nh),
                        rinv[g % 3][:, 0:nh].unsqueeze(2).to_broadcast([P, nh, MLA_V]), ALU.mult), "V")

                dve.drain()
                for i in range(NG + 2):
                    if i < NG:
                        mask_and_shift(i)
                    if 1 <= i <= NG:
                        row_sums(i - 1)
                    if i >= 2:
                        attend_out(i - 2)
                for t in range(T):
                    g = slice(t * RET_H, (t + 1) * RET_H)
                    bank = units.wait_full(("retO", t))[:, 0:RET_H * RET_E].rearrange("p (h e) -> p h e", h=RET_H)
                    dve.tensor_reduce(ret_mean[:, g], bank, AX.X, ALU.add)
                    dve.drain()
                    dve.tensor_scalar(ret_mean[:, g], ret_mean[:, g], 1.0 / RET_E, None, ALU.mult)
                    dve.drain()
                    units.emptied_by(("retO", t), dve.tensor_tensor(
                        ret_o[:, g, :], bank, ret_mean[:, g].unsqueeze(2).to_broadcast([P, RET_H, RET_E]), ALU.subtract), "V")
                dve.drain()
                dve.tensor_tensor(ret_sq, ret_o, ret_o, ALU.mult)
                dve.drain()
                dve.tensor_reduce(ret_var, ret_sq, AX.X, ALU.add).then_inc(ret_var_ready.sem, 1)
                ret_std_ready.wait(dve, 1, l)
                dve.reciprocal(ret_rstd, ret_rstd)
                dve.drain()
                dve.tensor_tensor(ret_o, ret_o, ret_rstd.unsqueeze(2).to_broadcast([P, T * RET_H, RET_E]), ALU.mult)
                dve.drain()
                silu_ready.wait(dve, 1, l)
                dve.tensor_tensor(mix[:, :, D - RET_H * RET_E:D],
                                  ret_o.rearrange("p (t h) e -> p t (h e)", t=T), proj[:, :, C_RG:IN_W],
                                  ALU.mult).then_inc(ret_ready.sem, 1)
                for j in range(1, 4, 2):
                    bank = units.wait_full(("mixT", j))
                    for kk in range(2):
                        k = 2 * j + kk
                        src = bank[:, kk * SEQ:(kk + 1) * SEQ]
                        ret_k = k - (KD - 2)
                        if ret_k < 0:
                            ins = dve.tensor_copy(hT[:, k, :], src)
                        else:
                            ins = dve.tensor_scalar(hT[:, k, :], src, gain(G_RET)(ret_k), None, ALU.mult)
                    units.emptied_by(("mixT", j), ins, "V")
                for c in range(2):
                    for t in range(T):
                        bank = units.wait_full(("wout", T * c + t))
                        xc = x[:, t, c * 512:(c + 1) * 512]
                        units.emptied_by(("wout", T * c + t), dve.tensor_tensor(xc, bank, xc, ALU.add), "V")
                norm(3)
                dve_transposed(dve, units, "tr3", gain(G_MLP))
                for i in range(2 * FFB):
                    bank = units.wait_full(("ff1", i))
                    if i >= 4:
                        hid_ready.wait(dve, i - 3, l)
                    units.emptied_by(("ff1", i), dve.tensor_scalar(relu_h[i % 4], bank, 0.0, None, ALU.max), "V")
                for u in range(2 * T):
                    t, c = u % T, u // T
                    bank = units.wait_full(("ff2", u))
                    xc = x[:, t, c * 512:(c + 1) * 512]
                    units.emptied_by(("ff2", u), dve.tensor_tensor(xc, bank, xc, ALU.add), "V")
                dve.drain()
                dve.sem_inc(x_done.sem, 1)
            units = UnitView(SU, dve, psum)

            def gain2(first_col):
                return lambda k: gains[:, first_col + k:first_col + k + 1]

            def per_head(a, shape):
                return a.unsqueeze(len(shape) - 1).to_broadcast(shape)

            def channels(name):
                return vec[name].unsqueeze(1).to_broadcast([P, T, RW_W])

            def done(ins):
                dve.drain()

            mul, add, sub = ALU.mult, ALU.add, ALU.subtract
            dve.memset(gn_eps_c, GN_EPS)
            dve.wait_ge(g_final_loaded, 16)
            dve.wait_ge(std2_ready, 1)
            dve.reciprocal(rstd, std)
            dve.drain()
            for t in range(T):
                ins = dve.scalar_tensor_tensor(x[:, t, :], x[:, t, :], rstd[:, t:t + 1], g_final, mul, mul)
            ins.then_inc(x_normed, 1)
            dve.wait_ge(std2_ready, 2)
            scale_rows(dve, [(x[:, t, :], xn2[:, t, :], t) for t in range(T)]).then_inc(xn2_ready, T)
            dve.wait_ge(gains2_loaded, 16)
            dve_transposed(dve, units, "tr1", gain2(0))
            for b, (c, w) in enumerate(RW_BLOCKS):
                bank = units.wait_full(("rw", T * b))
                units.emptied_by(("rw", T * b), dve.tensor_copy(pf[:, 0, c:c + w], bank[:, 0:w]), "V")
            bank = units.wait_full(("bias", 0))
            units.emptied_by(("bias", 0), dve.tensor_copy(bias_row[0:ATT_H, :], bank[0:ATT_H, 0:384]), "V")
            dve.drain()
            dve.sem_inc(bias_done, 1)
            dve.wait_ge(mu_loaded, 16)
            dve.wait_ge(prev_zero, 1)
            dve.wait_ge(prev_loaded, 48)
            dve.tensor_tensor(prev, prev, pf, sub)
            dve.drain()
            dve.tensor_tensor(prev, prev, mu.unsqueeze(1).to_broadcast([P, T, RW_IN]), mul)
            dve.drain()
            dve.tensor_tensor(pf, pf, prev, add).then_inc(pm_ready, 1)
            for b, (c, w) in enumerate(QKV_BLOCKS):
                bank = units.wait_full(("qkv", T * b))
                units.emptied_by(("qkv", T * b), dve.tensor_copy(qkv[:, 0, c:c + w], bank[:, 0:w]), "V")
            dve.wait_ge(vec_loaded, 16 * len(vec))
            for t in range(T):
                for j, (dst, n) in enumerate(((bufR, "w0"), (bufB, "a0"))):
                    bank = units.wait_full(("lora", 3 * t + j))
                    ins = dve.tensor_tensor(dst[:, t, :], bank, vec[n], add)
                    units.emptied_by(("lora", 3 * t + j), ins, "V")
            dve.drain()
            dve.sem_inc(wa_in, 1)
            r_, k_, v_ = (pf[:, :, c:c + RW_W] for c in (C_R, C_K, C_V))
            heads = lambda a: a.rearrange("p t (h e) -> p t h e", e=RW_E)
            hshape = [P, T, RW_H, RW_E]
            th = lambda a: a.rearrange("p (t h) -> p t h", t=T)
            dve.tensor_tensor(bufA, k_, channels("k_k"), mul)
            dve.drain()
            dve.tensor_tensor(bufK, bufA, bufA, mul)
            dve.drain()
            dve.tensor_reduce(th(kk_n), heads(bufK), AX.X, add).then_inc(kk_ss, 1)
            units.wait_emptied(*(("qkv", j) for j in range(PROJ_QKV)))
            qk = [qkv[:, :, j * ATT_W:(j + 1) * ATT_W].rearrange("p t (h e) -> p t h e", e=ATT_E) for j in range(2)]
            sq = qk_sq.rearrange("p t (h e) -> p t h e", e=ATT_E)
            for j in range(2):
                dve.tensor_tensor(sq, qk[j], qk[j], mul)
                dve.drain()
                ins = dve.tensor_reduce(qk_ss[:, j, :, :], sq, AX.X, add)
                if j == 0:
                    dve.drain()
            ins.then_inc(qk_ss_ready, 1)
            dve.wait_ge(qk_gain_loaded, 32)
            dve.wait_ge(qk_std, 1)
            dve.reciprocal(stat2[:, 0:48], stat2[:, 0:48])
            dve.drain()
            dve.tensor_scalar(qk_ss[:, 0, :, :], qk_ss[:, 0, :, :], ATT_E ** -0.5, None, mul)
            dve.drain()
            for j in range(2):
                dve.tensor_tensor(qk[j], qk[j], per_head(qk_ss[:, j, :, :], [P, T, ATT_H, ATT_E]), mul)
            dve.drain()
            for j in range(2):
                for t in range(T):
                    a = qk[j][:, t, :, :].rearrange("p (g h) e -> p g h e", g=GRP)
                    ins = dve.tensor_tensor(a, a, qk_gain[:, j, :, :].unsqueeze(2).to_broadcast([P, GRP, HPG, ATT_E]), mul)
            ins.then_inc(qk_ready, 1)
            dve.wait_ge(kk_std, 1)
            dve.wait_ge(wa_ready, 1)
            dve.tensor_scalar(kk_n, kk_n, 1e-12, None, ALU.max)
            dve.drain()
            dve.reciprocal(kk_n, kk_n)
            dve.drain()
            dve.tensor_tensor(heads(bufA), heads(bufA), per_head(th(kk_n), hshape), mul)
            for t in range(T):
                dve.scalar_tensor_tensor(bufK[:, t, :], bufB[:, t, :], -1.0, vec["k_a"], add, mul)
            dve.drain()
            for t in range(T):
                dve.scalar_tensor_tensor(k_[:, t, :], bufK[:, t, :], 1.0, k_[:, t, :], add, mul)
            dve.tensor_tensor(bufB, bufB, bufA, mul)
            dve.drain()
            dve.tensor_tensor(bufK, r_, k_, mul)
            dve.drain()
            dve.tensor_tensor(bufK, bufK, channels("r_k"), mul)
            dve.drain()
            dve.tensor_reduce(th(bonus), heads(bufK), AX.X, add).then_inc(bonus_ready, 1)
            dve.drain()
            dve.sem_inc(preproc_done, 1)
            for i in range(NA + 2):
                if i < NA:
                    t, hg = ATT_UNITS[i]
                    nk = (t + 1) * P
                    m = rowmax[:, i % 2:i % 2 + 1]
                    dve.tensor_reduce(m, units.wait_full(("S", i))[:, 0:GRP * nk], AX.X, ALU.max)
                    dve.drain()
                    dve.tensor_scalar(m, m, -1.0, None, mul).then_inc(att_max, 1)
                if 1 <= i <= NA:
                    dve.wait_ge(att_exp, i)
                    dve.reciprocal(rinv[(i - 1) % 3][:, 0:1], rowsum[:, (i - 1) % 2:(i - 1) % 2 + 1])
                    dve.drain()
                if i >= 2:
                    t, hg = ATT_UNITS[i - 2]
                    bank = units.wait_full(("O", i - 2))
                    units.emptied_by(("O", i - 2), dve.tensor_scalar(
                        att[:, t, hg * ATT_E:(hg + 1) * ATT_E], bank[:, 0:ATT_E], rinv[(i - 2) % 3][:, 0:1], None, mul), "V")
            for t in range(T):
                dve.wait_ge(exp_excl, t + 1)
                excl = units.bank(("cum", 2 * t + 1))
                units.emptied_by(("cum", 2 * t + 1), dve.tensor_tensor(bufA[:, t, :], excl, bufA[:, t, :], mul), "V")
                dve.wait_ge(exp_incl, t + 1)
                dve.tensor_tensor(bufB[:, t, :], bufB[:, t, :], bufK[:, t, :], mul)
                dve.tensor_tensor(bufR[:, t, :], bufR[:, t, :], r_[:, t, :], mul)
                dve.drain()
                dve.tensor_tensor(bufK[:, t, :], bufK[:, t, :], k_[:, t, :], mul)
                dve.drain()
                dve.sem_inc(scaled, 1)
            for u in range(2 * T):
                t, c = u // 2, u % 2
                bank = units.wait_full(("yatt", u))
                g = gates[:, t, c * 512:(c + 1) * 512]
                units.emptied_by(("yatt", u), dve.tensor_tensor(g, bank, g, mul), "V")
            every = lambda name: second(name).unsqueeze(1).to_broadcast([P, PAIRS, P])
            for t in range(T):
                for par in range(2):
                    n, m = 2 * t + par, core[par]
                    four = lambda key: units.wait_full(key).rearrange("p (c s) -> p c s", c=PAIRS)
                    for name, dst, mask in (("NT", "NT", "minus_strict"), ("N", "T", "minus_level1"), ("Mak", "Mak", "minus_strict"),
                                            ("Mrb", "Mrb", "incl"), ("Mrk", "Mrk", "incl")):
                        bank = four((name, n))
                        units.emptied_by((name, n), dve.tensor_tensor(m[dst], bank, every(mask), mul), "V")
                        if name == "N":
                            dve.drain()
                            dve.sem_inc(core_masked, 1)
                for i in range(len(LEVELS)):
                    level = second("levels")[:, i * P:(i + 1) * P].unsqueeze(1).to_broadcast([P, PAIRS, P])
                    for par in range(2):
                        key = ("X", 8 * (2 * t + par) + i)
                        bank = units.wait_full(key).rearrange("p (c s) -> p c s", c=PAIRS)
                        units.emptied_by(key, dve.tensor_tensor(core[par]["X"], bank, level, mul), "V")
                    if i < len(LEVELS) - 1:
                        for par in range(2):
                            key, a = ("TX", 8 * (2 * t + par) + i), core[par]["T"]
                            bank = units.wait_full(key).rearrange("p (c s) -> p c s", c=PAIRS)
                            units.emptied_by(key, dve.tensor_tensor(a, bank, a, add), "V")
                for par in range(2):
                    key = ("OUT", 2 * t + par)
                    bank = units.wait_full(key)[:, 0:PAIRS * RW_E].rearrange("p (c e) -> p c e", c=PAIRS)
                    units.emptied_by(key, dve.tensor_copy(rw_o[:, t * RW_H + par:(t + 1) * RW_H:2, :], bank), "V")
                if t == 0:
                    bank = units.wait_full(("state", 0)).rearrange("p (c e) -> p c e", c=PAIRS)
                    units.wait_emptied(("sdec", 0))
                    for par in range(2):
                        r = slice(RW_E * par, RW_E * (par + 1))
                        ins = dve.tensor_tensor(state[r], bank[r, :, RW_E * par:RW_E * (par + 1)],
                                                sdec[r].unsqueeze(2).to_broadcast([RW_E, PAIRS, RW_E]), mul)
                    units.emptied_by(("state", 0), ins, "V")
                    dve.drain()
                    dve.tensor_scalar(minus_state, state, -1.0, None, mul).then_inc(state_ready, 1)
            gshape = [P, T * RW_H, RW_E]
            dve.drain()
            dve.tensor_reduce(rw_mean, rw_o, AX.X, add)
            dve.drain()
            dve.tensor_scalar(rw_mean, rw_mean, 1.0 / RW_E, None, mul)
            dve.drain()
            dve.tensor_tensor(rw_o, rw_o, per_head(rw_mean, gshape), sub)
            dve.drain()
            dve.tensor_tensor(rw_sq, rw_o, rw_o, mul)
            dve.drain()
            dve.tensor_reduce(rw_var, rw_sq, AX.X, add).then_inc(gn_ss, 1)
            dve.wait_ge(gn_std, 1)
            dve.reciprocal(rw_var, rw_var)
            dve.drain()
            dve.tensor_tensor(rw_o, rw_o, per_head(rw_var, gshape), mul)
            dve.drain()
            dve.tensor_tensor(bufA, bufA, channels("ln_w"), mul)
            dve.drain()
            dve.tensor_tensor(bufA, bufA, channels("ln_b"), add)
            dve.drain()
            dve.wait_ge(bonus_v, 1)
            dve.tensor_tensor(bufA, bufA, r_, add)
            dve.drain()
            dve.tensor_tensor(bufA, bufA, rw_g, mul).then_inc(o_ready, 1)
            for u in range(2 * T):
                t, c = u // 2, u % 2
                bank = units.wait_full(("yrw", u))
                g = gates[:, t, D + c * 512:D + (c + 1) * 512]
                units.emptied_by(("yrw", u), dve.tensor_tensor(g, bank, g, mul), "V")
            dve.drain()
            dve.tensor_tensor(gates[:, :, 0:D], gates[:, :, 0:D], gates[:, :, D:2 * D], add).then_inc(mixed, 1)
            for c in range(2):
                for t in range(T):
                    bank = units.wait_full(("wout", T * c + t))
                    xc = x[:, t, c * 512:(c + 1) * 512]
                    units.emptied_by(("wout", T * c + t), dve.tensor_tensor(xc, bank, xc, add), "V")
            dve.wait_ge(std2_ready, 3)
            scale_rows(dve, [(x[:, t, :], xn2[:, t, :], t) for t in range(T)]).then_inc(xn2_ready, T)
            dve_transposed(dve, units, "tr2", gain2(KD))
            dve.wait_ge(route_loaded, 48)
            for t in range(T):
                bank = units.wait_full(("route", t))
                units.emptied_by(("route", t), dve.tensor_tensor(logits[:, t, :], bank[:, 0:EG + NE], b_route, add), "V")
            dve.drain()
            small = stat[:, 12:36]
            best, total, first1, second1 = (small[:, T * j:T * j + T] for j in range(4))
            pick = small[:, 8:8 + T]

            def first_of(values, n, m, hot, tmp):
                rank = second("rank")[:, EPG - n:EPG].unsqueeze(1).to_broadcast([P, T, n])
                dve.tensor_reduce(m, values, AX.X, ALU.max)
                dve.drain()
                dve.tensor_tensor(tmp, values, m.unsqueeze(2).to_broadcast([P, T, n]), ALU.is_equal)
                dve.drain()
                dve.tensor_tensor(tmp, tmp, rank, mul)
                dve.drain()
                dve.tensor_reduce(pick, tmp, AX.X, ALU.max)
                dve.drain()
                dve.tensor_tensor(hot, tmp, pick.unsqueeze(2).to_broadcast([P, T, n]), ALU.is_equal)
                dve.drain()

            tn = lambda a, n: a[:, 0:T * n].rearrange("p (t n) -> p t n", t=T)
            shifted_g, hot_g, tmp_g = tn(ra[0], EG), tn(ra[1], EG), tn(ra[7], EG)
            glog, elog = logits[:, :, 0:EG], logits[:, :, EG:].rearrange("p t (g e) -> p t g e", g=EG)
            first_of(glog, EG, best, hot_g, tmp_g)
            dve.tensor_tensor(shifted_g, glog, best.unsqueeze(2).to_broadcast([P, T, EG]), sub).then_inc(route_max, 1)
            full = ra[2].rearrange("p (t g e) -> p t g e", t=T, g=EG)
            dve.tensor_tensor(full, elog, hot_g.unsqueeze(3).to_broadcast([P, T, EG, EPG]), mul)
            dve.drain()
            chosen, hot1, hot2, tmp_e = tn(ra[3], EPG), tn(ra[4], EPG), tn(ra[6], EPG), tn(ra[7], EPG)
            dve.tensor_reduce(chosen, full.rearrange("p t g e -> p t e g"), AX.X, add)
            dve.drain()
            first_of(chosen, EPG, first1, hot1, tmp_e)
            dve.tensor_scalar(tmp_e, hot1, MASKED, None, mul)
            dve.drain()
            dve.tensor_tensor(chosen, chosen, tmp_e, add)
            dve.drain()
            first_of(chosen, EPG, second1, hot2, tmp_e)
            diff = ra[5][:, 0:T]
            dve.tensor_tensor(diff, second1, first1, sub).then_inc(pair_diff, 1)
            dve.wait_ge(route_exp, 1)
            dve.tensor_reduce(total, shifted_g, AX.X, add)
            dve.wait_ge(pair_exp, 1)
            dve.tensor_scalar(best, diff, 1.0, None, add)
            dve.drain()
            dve.tensor_tensor(total, total, best, mul)
            dve.drain()
            dve.reciprocal(first1, total)
            dve.drain()
            dve.tensor_tensor(second1, first1, diff, mul)
            dve.drain()
            dve.tensor_tensor(tmp_e, hot1, hot2, add)
            dve.drain()
            spread_e = lambda a, t: a[:, t, :].unsqueeze(1).to_broadcast([P, EG, EPG])
            spread_g = lambda t: hot_g[:, t, :].unsqueeze(2).to_broadcast([P, EG, EPG])
            for t in range(T):
                ins = dve.tensor_tensor(taken[:, t, :].rearrange("p (g e) -> p g e", g=EG), spread_g(t), spread_e(tmp_e, t), mul)
            ins.then_inc(taken_ready, 1)
            dve.tensor_tensor(hot1, hot1, first1.unsqueeze(2).to_broadcast([P, T, EPG]), mul)
            dve.tensor_tensor(hot2, hot2, second1.unsqueeze(2).to_broadcast([P, T, EPG]), mul)
            dve.drain()
            dve.tensor_tensor(hot1, hot1, hot2, add)
            dve.drain()
            for t in range(T):
                for q_ in range(PASSES):
                    dve.tensor_tensor(gate_tab[:, q_, :, t].rearrange("p (g e) -> p g e", g=EG), spread_g(t), spread_e(hot1, t), mul)
            units.wait_full(("rank", T))
            for t in range(T):
                bank = units.wait_full(("rank", t))
                units.emptied_by(("rank", t), dve.tensor_tensor(taken[:, t, :], bank[:, 0:NE], taken[:, t, :], mul), "V")
            bank = units.wait_full(("rank", T))
            units.emptied_by(("rank", T), dve.tensor_reduce(fullest[:, 0:1], bank[:, 0:NE], AX.X, ALU.max), "V")
            dve.drain()
            for t in range(T):
                for q_ in range(PASSES):
                    dve.tensor_scalar(place[:, q_, :, t], taken[:, t, :], -1.0 - q_ * SLOTS_E, None, add)
            for q_ in range(1, PASSES):
                dve.tensor_scalar(fullest[:, q_:q_ + 1], fullest[:, 0:1], q_ * SLOTS_E + 0.5, float(TURNS), ALU.is_gt, mul)
            dve.drain()
            dve.tensor_reduce(turns_f, fullest[:, 1:PASSES], AX.X, add)
            dve.drain()
            dve.tensor_scalar(turns_i[:], turns_f, float(TURNS), None, add)
            dve.drain()
            dve.sem_inc(places_ready, 1)
            dve.wait_ge(places_ready, 1)
            places = second("places")
            table = lambda a, turn: a.rearrange("p q e t -> p (q e) t")[:, bass.ds(turn * EPT, EPT), :]
            with dve.Fori(0, dve.value_load(turns_i[0:1, 0:1], min_val=TURNS, max_val=TURNS * PASSES)) as turn:
                units = UnitView(EU, dve, psum, turn)
                dve.tensor_copy(place_now, table(place, turn))
                dve.tensor_copy(gate_now, table(gate_tab, turn))
                dve.drain()
                for t in range(T):
                    for j in range(EPT):
                        at, g = place_now[:, j, t:t + 1], gate_now[:, j, t:t + 1]
                        dve.tensor_scalar(take[:, t, j, :], places, at, None, ALU.is_equal)
                        ins = dve.tensor_scalar(give[:, t, j, :], places, at, g, ALU.is_equal, mul)
                ins.then_inc(take_ready.sem, 1)
                for i in range(2):
                    bank = units.wait_full(("gx", i)).rearrange("p (k n) -> p k n", k=4)
                    norm2 = gains[:, KD + 4 * i:KD + 4 * i + 4].unsqueeze(2).to_broadcast([P, 4, P])
                    units.emptied_by(("gx", i), dve.tensor_tensor(xe[:, 4 * i:4 * i + 4, :], bank, norm2, mul), "V")
                bank = units.wait_full(("up", 0))
                units.wait_emptied(("gate", 0))
                units.emptied_by(("up", 0), dve.tensor_tensor(hid, bank, silu_g, mul), "V")
                bank = units.wait_full(("y", 1))
                units.emptied_by(("y", 1), dve.tensor_copy(y_rows[:, 512:D], bank), "V")
                dve.drain()
            final = UnitView(FU, dve, psum)
            for u in range(2 * T):
                t, c = u // 2, u % 2
                bank = final.wait_full(("acc", u))
                xc = x[:, t, c * 512:(c + 1) * 512]
                final.emptied_by(("acc", u), dve.tensor_tensor(xc, bank, xc, add), "V")
            dve.drain()
            dve.sem_inc(moe_done, 1)


def kernel(**inputs):
    import concourse.bacc as bacc
    from concourse.bass_utils import run_bass_kernel_spmd as run

    nc = bacc.Bacc("TRN2", target_bir_lowering=False, num_devices=1)
    tables = shape_tables()
    arrays = {name: np.ascontiguousarray(a) for name, a in inputs.items() if name not in SMALL}
    cols = lambda a: np.asarray(a).reshape(DEPTH, -1, P).transpose(0, 2, 1)
    arrays["gains"] = np.ascontiguousarray(np.concatenate(
        [cols(inputs[n]) for n in ("g_mix", "g_q", "g_kv", "g_mlp", "g_ret")], axis=2))
    arrays["gains2"] = np.ascontiguousarray(np.concatenate(
        [np.asarray(inputs[n]).reshape(-1, P).T for n in ("norm1_gain_2", "norm2_gain_2")], axis=1))
    arrays["rows2"] = np.concatenate([np.asarray(inputs[n]).reshape(-1) for n in ROW_INPUTS])[None]
    for name, names in (("shared_c", SHARED), ("first_c", FIRST), ("second_c", SECOND)):
        arrays[name] = pack(tables, names)
    io = {n: nc.dram_tensor(f"in_{n}", a.shape, F32, kind="ExternalInput").ap() for n, a in arrays.items()}
    out = nc.dram_tensor("out", (1, SEQ, D), F32, kind="ExternalOutput").ap()
    program(nc, io, out)
    return run(nc, [{f"in_{n}": a for n, a in arrays.items()}], core_ids=[0]).results[0]["out"]


ROW_INPUTS = ("rwkv_shift_mu_2", "rwkv_w0_2", "rwkv_a0_2", "rwkv_k_k_2", "rwkv_k_a_2", "rwkv_r_k_2", "rwkv_ln_w_2",
              "rwkv_ln_b_2", "q_norm_gain_2", "k_norm_gain_2", "g_final", "b_group_router_2", "b_expert_router_2")
SMALL = ("g_mix", "g_q", "g_kv", "g_mlp", "g_ret", "norm1_gain_2", "norm2_gain_2") + ROW_INPUTS
```

```python
from contextlib import ExitStack

import numpy as np
import concourse.bass as bass
import concourse.mybir as mybir
from concourse.alu_op_type import AluOpType as ALU

F32 = mybir.dt.float32
F32R = mybir.dt.float32r
ACT = mybir.ActivationFunctionType
AX = mybir.AxisListType



def col_blocks(width):
    return [(c, min(512, width - c)) for c in range(0, width, 512)]


P = 128
SEQ, D = 256, 1024
T = SEQ // P
KD = D // P
DEPTH = 2
EPS = 1e-6
ROPE_THETA = 10000.0
MLA_H, NOPE, ROPE, MLA_V = 8, 64, 32, 64
QK = NOPE + ROPE
Q_RANK, KV_RANK = 768, 256
DSA_H, DSA_E = 4, 64
IDX_H, IDX_E = 8, 32
TOPK = min(256, SEQ // 4)
RET_H, RET_E = 4, 64
D_FF = 4 * D
(C_CQ, C_CKV, C_KR, C_AQ, C_AK, C_AV, C_QI, C_KI, C_WI, C_RQ, C_RK, C_RV, C_RG, IN_W) = np.cumsum(
    [0, Q_RANK, KV_RANK, ROPE, DSA_H * DSA_E, DSA_E, DSA_E, IDX_H * IDX_E, IDX_E, IDX_H,
     RET_H * RET_E, RET_H * RET_E, RET_H * RET_E, RET_H * RET_E]).tolist()
MASKED = -1e38
TAKEN = -3e38
FFB = D_FF // 512
GRP, HPG, ATT_E = 3, 4, 64
ATT_H = GRP * HPG
ATT_W = ATT_H * ATT_E
PATTERNS = ((128, 1), (512, 4), (2048, 16))
BUCKETS, REL_MAX = 32, 2048
RW_H, RW_E = 8, 64
RW_W = RW_H * RW_E
LORA_W, LORA_A, LORA_G = 64, 64, 160
C_R, C_K, C_V, C_XW, C_XA, C_XG, RW_IN = np.cumsum([0, RW_W, RW_W, RW_W, LORA_W, LORA_A, LORA_G]).tolist()
GN_EPS = 64e-5
GATE_W = 2 * D
EG, EPG, D_EXP = 4, 8, 512
NE = EG * EPG
PAIRS = RW_H // 2
DECAY_RATE = -float(np.exp(-0.5))
RW_BLOCKS, QKV_BLOCKS, GATE_BLOCKS = col_blocks(RW_IN), col_blocks(3 * ATT_W), col_blocks(GATE_W)
LEVELS = [2 ** i for i in range(1, 7)]
G_MIX, G_QKV, G_MLP, G_RET, N_GAIN = 0, 8, 16, 24, 26

SLOT = 4096
SLOTS = 4
PIECE = 2048
RAWS, SPLITS = 3, 3
PIECE2 = 1024
RAWS2, SPLITS2 = 6, 4


IN_BLOCKS = col_blocks(IN_W)


class Units:

    def __init__(self, full, read_act, read_dve, plan):
        self.full, self.read = full, {"A": read_act, "V": read_dve}
        self.u, last, cnt = {}, {}, {"A": 0, "V": 0}
        for stage, i, bank, eng in plan:
            banks = bank if isinstance(bank, tuple) else (bank,)
            cnt[eng] += 1
            self.u[stage, i] = (len(self.u) + 1, banks, eng, cnt[eng], [last[b] for b in banks if b in last])
            for b in banks:
                last[b] = (eng, cnt[eng])
        self.n, self.cnt = len(self.u), cnt


class UnitView:

    def __init__(self, units, eng, psum, turn=None):
        self.U, self.e, self.ps, self.turn = units, eng, psum, turn
        self.issued, self.emptied = 0, {"A": 0, "V": 0}
        self.seen = {"A": 0, "V": 0, "full": 0}

    def _at(self, per_turn, k):
        return k if self.turn is None else self.turn * per_turn + k

    def full_count(self, key):
        return self.U.u[key][0] if self.turn is None else (self.turn + 1) * self.U.n + self.U.u[key][0]

    def bank(self, key):
        banks = self.U.u[key][1]
        return self.ps[:, banks[0]:banks[-1] + 1, :].rearrange("p b w -> p (b w)")

    def begin(self, key):
        prev = self.U.u[key][4]
        for eng in "AV":
            self._wait_count(eng, max((c for e, c in prev if e == eng), default=0))
        return self.bank(key)

    def _wait_count(self, eng, idx):
        if idx > self.seen[eng]:
            self.seen[eng] = idx
            self.e.wait_ge(self.U.read[eng], self._at(self.U.cnt[eng], idx))

    def finish(self, key, ins):
        self.issued += 1
        assert self.U.u[key][0] == self.issued, (key, self.issued)
        ins.then_inc(self.U.full, 1)

    def wait_full(self, key):
        if self.U.u[key][0] > self.seen["full"]:
            self.seen["full"] = self.U.u[key][0]
            self.e.wait_ge(self.U.full, self.full_count(key))
        return self.bank(key)

    def emptied_by(self, key, ins, eng):
        n, bank, want, idx, _ = self.U.u[key]
        self.emptied[eng] += 1
        assert want == eng and idx == self.emptied[eng], (key, want, eng, idx, self.emptied)
        ins.then_inc(self.U.read[eng], 1)

    def wait_emptied(self, *keys):
        for eng in "AV":
            idx = [self.U.u[key][3] for key in keys if self.U.u[key][2] == eng]
            if idx:
                self._wait_count(eng, max(idx))


class Signal:

    def __init__(self, sem, per_turn):
        self.sem, self.per_turn = sem, per_turn

    def wait(self, eng, k, turn=None):
        eng.wait_ge(self.sem, k if turn is None else turn * self.per_turn + k)


class WeightRing:

    def __init__(self, loaded, blocks, first_slot=0):
        self.loaded, self.blocks = loaded, blocks
        self.where, per = {}, [0] * SLOTS
        held = {}
        self.prev = {}
        for j, (name, release) in enumerate(blocks):
            s = (first_slot + j) % SLOTS
            per[s] += 1
            self.where[name] = (s, per[s])
            self.prev[name] = held.get(s)
            held[s] = release
        self.per, self.last = per, held


class SplitWeights:

    def __init__(self, pieces, units, loaded, hi, lo, used, raw, split, looped):
        self.raws, self.splits, self.looped = len(loaded), split.shape[1], looped
        self.pieces, self.U, self.loaded, self.hi, self.lo, self.used = pieces, units, loaded, hi, lo, used
        self.raw_mem, self.split_mem = raw, split
        self.n = len(pieces)
        self.index = {name: j for j, (name, _, _) in enumerate(pieces)}
        self.lo_order = {e: [j for j in range(self.n) if pieces[j][1] == e] for e in "PV"}
        self.used_order = [j for j in range(self.n) if pieces[j][2] is None]

    def held_before(self, j, slots):
        if j >= slots:
            return 0, j - slots
        return 1, max(i for i in range(self.n) if i % slots == j)

    def raw(self, j, n):
        return self.raw_mem[:, j % self.raws, 0:n]

    def part(self, j, which, n):
        return self.split_mem[:, j % self.splits, which, 0:n]

    def wait_loaded(self, eng, j, turn):
        mine = [i for i in range(self.n) if i % self.raws == j % self.raws]
        eng.wait_ge(self.loaded[j % self.raws], turn * (16 * len(mine)) + 16 * (mine.index(j) + 1))

    def wait_hi(self, eng, j, turn):
        eng.wait_ge(self.hi, turn * self.n + j + 1)

    def wait_lo(self, eng, j, turn, ago=0):
        order = self.lo_order[self.pieces[j][1]]
        eng.wait_ge(self.lo[self.pieces[j][1]], (turn + (self.looped - ago)) * len(order) + order.index(j) + 1)

    def wait_raw_free(self, eng, j, turn):
        ago, i = self.held_before(j, self.raws)
        if self.looped or not ago:
            self.wait_lo(eng, i, turn, ago)

    def wait_split_free(self, view, j, turn):
        ago, i = self.held_before(j, self.splits)
        unit = self.pieces[i][2]
        if ago and not self.looped:
            return
        if unit is None:
            view.e.wait_ge(self.used, (turn + (self.looped - ago)) * len(self.used_order) + self.used_order.index(i) + 1)
        elif ago:
            view.e.wait_ge(self.U.full, turn * self.U.n + self.U.u[unit][0])
        else:
            view.wait_full(unit)


def interleave(stage, n, banks, engs):
    return [(stage, i, banks[i % len(banks)], engs[i % len(engs)]) for i in range(n)]


GROUPS = [(False, t, tuple(range(h, h + 4 // (t + 1)))) for t in range(T) for h in range(0, MLA_H, 4 // (t + 1))] + \
         [(True, t, (h, h + 2)) for t in range(T) for h in range(2)]
NG = len(GROUPS)
IDX_UNITS = [(t, (h, h + 4)) for t in range(T) for h in range(IDX_H // 2)]
RET_UNITS = [(t, s, h) for t, s in ((0, 0), (1, 0), (1, 1)) for h in range(2)]


def layer_plan():
    plan = interleave("tr1", 4, (0, 1, 2, 3), "V")
    plan += interleave("proj", len(IN_BLOCKS) * T, (4, 5, 6, 7), "VA")
    plan += interleave("idxT", T, (0, 1), "V")
    plan += interleave("tr2", 4, (2, 3, 4, 5), "V")
    plan += interleave("idxS", len(IDX_UNITS), (6, 7), "A")
    plan += interleave("uq", 2 * T, (0, 1, 2, 3), "AA")
    plan += interleave("ukv", 2 * T, (4, 5, 0, 1), "AA")
    plan += interleave("dsaT", T, (2, 3), "V")
    plan += interleave("retT", T, (6, 7), "V")
    plan += interleave("retS", len(RET_UNITS), (4, 5, 6, 7), "V")
    plan += interleave("mlaT", 4 * T, (0, 1, 2, 3), "A")
    plan += interleave("retO", T, (6, 7), "V")
    for i in range(NG + 2):
        if i < NG:
            plan.append(("S", i, (0, 1)[i % 2], "V"))
        if 1 <= i <= NG:
            plan.append(("PT", i - 1, (2, 3)[i % 2], "A"))
        if i >= 2:
            plan.append(("O", i - 2, (4, 5)[i % 2], "V"))
    plan += interleave("mixT", 4, (0, 1, 2, 3), "V")
    plan += interleave("wout", 2 * T, (4, 5, 6, 7), "V")
    plan += interleave("tr3", 4, (0, 1, 2, 3), "V")
    for b in range(FFB):
        plan += [("ff1", 2 * b + j, (2 * b + j) % 4, "V") for j in range(2)]
    plan += interleave("ff2", 2 * T, (4, 5, 6, 7), "V")
    return plan


def layer_pieces():
    p = [(("in", b, i), "P", ("proj", T * b + T - 1) if i else None) for b in range(len(IN_BLOCKS)) for i in range(2)]
    p += [(("uq", 0, i), "P", ("uq", 2 * T - 1) if i == 2 else None) for i in range(3)]
    p += [(("ukv", 0, 0), "P", ("ukv", 2 * T - 1))]
    p += [(("out", c, i), "P", ("wout", T * c + T - 1) if i else None) for c in range(2) for i in range(2)]
    ff1 = lambda b: [(("ff1", b, j), "PV"[j], ("ff1", 2 * b + j)) for j in range(2)]
    ff2 = lambda b: [(("ff2", b, i), "PV"[i], ("ff2", 2 * T - 1) if b == FFB - 1 and i else None) for i in range(2)]
    for b in range(FFB):
        p += ff1(b) + (ff2(b - 1) if b else [])
    return p + ff2(FFB - 1)


ATT_UNITS = [(t, h) for t in range(T) for h in range(HPG)]
NA = len(ATT_UNITS)
CORE = [(t, par) for t in range(T) for par in range(2)]
PROJ_RW, PROJ_QKV, PROJ_GATE = (T * len(b) for b in (RW_BLOCKS, QKV_BLOCKS, GATE_BLOCKS))


def second_plan():
    plan = interleave("tr1", 4, (0, 1, 2, 3), "V")
    plan += interleave("rw", PROJ_RW, (4, 5, 6, 7), "VA")
    plan += interleave("bias", 1, (0,), "V")
    plan += interleave("qkv", PROJ_QKV, (1, 2, 3, 0), "VA")
    plan += interleave("loraT", T, (4, 5), "A")
    plan += interleave("lora", 3 * T, (6, 7, 4, 5, 6, 7), "VVA")
    plan += interleave("gate", PROJ_GATE, (0, 1, 2, 3), "A")
    plan += interleave("qkT", 6, (4, 5, 6, 7), "A")
    for i in range(NA + 2):
        if i < NA:
            plan.append(("S", i, ((0, 1), (2, 3))[i % 2], "A"))
        if 1 <= i <= NA:
            plan.append(("PT", i - 1, (4, 5), "A"))
        if i >= 2:
            plan.append(("O", i - 2, (6, 7)[i % 2], "V"))
    plan += interleave("cum", 2 * T, (0, 1, 2, 3), "AV")
    plan += interleave("sdec", 1, (4,), "A")
    plan += interleave("rwT", 8, (5, 6, 7, 0), "A")
    plan += interleave("attT", 1, (1,), "A")
    plan += interleave("yatt", 2 * T, (2, 3, 4, 1), "V")
    for t in range(T):
        for par in range(2):
            plan += [(m, 2 * t + par, 4 * par + b, "V") for b, m in enumerate(("NT", "N", "Mak", "Mrb"))]
            plan += [("Mrk", 2 * t + par, 4 * par, "V")]
        for i in range(len(LEVELS)):
            for par in range(2):
                plan += [("TT", (2 * t + par) * 8 + i, 4 * par + 3, "A")] if i else []
                plan.append(("X", (2 * t + par) * 8 + i, 4 * par + 1, "V"))
            for par in range(2):
                plan.append(("TX" if i < len(LEVELS) - 1 else "XT", (2 * t + par) * 8 + i, 4 * par + 2, "V"))
        plan += [("RHS", 2 * t + par, 4 * par, "A") for par in range(2)]
        plan += [("U", 2 * t + par, 4 * par + 1, "A") for par in range(2)]
        plan += [("OUT", 2 * t + par, 4 * par + 2, "V") for par in range(2)]
        if t == 0:
            plan += [("state", 0, 3, "V")]
    plan += interleave("oT", 2, (0, 1), "A")
    plan += interleave("yrw", 2 * T, (2, 3, 4, 5), "V")
    plan += interleave("mixT", 4, (6, 7, 0, 1), "A")
    plan += interleave("wout", 2 * T, (2, 3, 4, 5), "V")
    plan += interleave("tr2", 4, (6, 7, 0, 1), "AV")
    plan += interleave("route", T, (2, 3), "V")
    plan += interleave("rank", T + 1, (4, 5, 6), "V")
    return plan


def second_pieces():
    return [((stage, b, i), "P", (stage, T * b + T - 1) if i == 3 else None)
            for stage, cols in (("rw", RW_BLOCKS), ("qkv", QKV_BLOCKS), ("gate", GATE_BLOCKS))
            for b in range(len(cols)) for i in range(4)]


def second_weights():
    blocks = [(("att_out", 0), ("yatt", 2 * T - 1)), (("rwkv_out", 0), ("yrw", 2 * T - 1))]
    return blocks + [(("out", c), ("wout", T * c + T - 1)) for c in range(2)]


EPT = 2
MOE_SLOTS = 3 * EPT


SLOTS_E = 64
PASSES = SEQ // SLOTS_E
TURNS = NE // EPT


def moe_plan():
    return [("gx", 0, 4, "V"), ("gx", 1, 5, "V"), ("gt", 0, 6, "A"), ("gate", 0, 7, "A"), ("up", 0, 4, "V"),
            ("hT", 0, 5, "A"), ("y", 0, 6, "A"), ("y", 1, 7, "V")]


def shape_tables():
    pos = np.arange(SEQ, dtype=np.float32)
    i = np.arange(P)
    c = {}
    c["ident"] = np.eye(P)
    c["causal"] = np.where(np.arange(T * P)[None, :] <= i[:, None] + P, 0.0, MASKED)
    for dim in (ROPE, DSA_E):
        inv = np.float32(ROPE_THETA) ** (-np.arange(0, dim, 2, dtype=np.float32) / np.float32(dim))
        ang = (pos[:, None] * inv[None, :]).astype(np.float32)
        for name, f in (("cos", np.cos), ("sin", np.sin)):
            c[f"{name}{dim}"] = f(ang).reshape(T, P, dim // 2).transpose(1, 0, 2).reshape(P, -1)
    gamma = np.log1p(-np.exp2(-5.0 - np.arange(RET_H)))
    dist = np.arange(T)[:, None, None] * P + i[None, None, :] - i[None, :, None]
    dec = np.where(dist >= 0, np.exp(np.maximum(dist, 0)[None] * gamma[:, None, None, None]), 0.0) * RET_E ** -0.5
    c["decay"] = dec.transpose(2, 1, 0, 3).reshape(P, -1)
    before, mid = (i[:, None] <= i[None, :]), (i < P // 2)[:, None]
    c["cum_incl"] = DECAY_RATE * (before.astype(float) - mid)
    c["cum_excl"] = DECAY_RATE * ((i[:, None] < i[None, :]).astype(float) - mid)
    c["halves"] = DECAY_RATE * np.concatenate([mid, ~mid], axis=1)
    c["minus_strict"] = -1.0 * (i[:, None] < i[None, :])
    c["incl"] = 1.0 * before
    def level(m):
        r, k = i[:, None], i[None, :]
        return (r // (2 * m) == k // (2 * m)) & (r // m % 2 == 1) & (k // m % 2 == 0)
    c["minus_level1"] = -1.0 * level(1)
    c["level1T"] = 1.0 * level(1).T
    c["levels"] = np.concatenate([level(m) for m in LEVELS], axis=1)
    d = np.float32(255) - np.arange(384, dtype=np.float32)
    exact = BUCKETS // 2
    far = exact + (np.log(np.maximum(d, 1) / np.float32(exact)) / np.float32(np.log(REL_MAX / exact))
                   * np.float32(BUCKETS - exact)).astype(np.int32)
    bucket = np.where(d < exact, np.maximum(d, 0), np.minimum(far, BUCKETS - 1)).astype(int)
    hot = np.zeros((P, 384))
    hot[bucket, np.arange(384)] = 1.0
    c["bucket_hot"] = hot
    for g, (win, dil) in enumerate(PATTERNS):
        hot[BUCKETS + g * HPG:BUCKETS + (g + 1) * HPG] = np.where((d >= 0) & (d <= win) & (d % dil == 0), 0.0, MASKED)
    c["flip"] = np.eye(P)[::-1]
    c["places"] = np.tile(np.arange(SLOTS_E), (P, 1))
    c["rank"] = np.tile(np.arange(EPG, 0, -1), (P, 1))
    return {k: np.ascontiguousarray(v, dtype=np.float32) for k, v in c.items()}


SHARED = ("ident", "causal")
FIRST = ("cos32", "sin32", "cos64", "sin64", "decay")
SECOND = ("cum_incl", "cum_excl", "halves", "minus_strict", "incl", "minus_level1", "level1T", "levels",
          "bucket_hot", "flip", "places", "rank")
ROWS, _at = {}, 0
for _n, _w in (("mu", RW_IN), ("w0", RW_W), ("a0", RW_W), ("k_k", RW_W), ("k_a", RW_W), ("r_k", RW_W), ("ln_w", RW_W),
               ("ln_b", RW_W), ("q_gain", GRP * ATT_E), ("k_gain", GRP * ATT_E), ("g_final", D), ("b_route", EG + NE)):
    ROWS[_n] = (_at, _w)
    _at += _w


def pack(tables, names):
    return np.ascontiguousarray(np.concatenate([tables[n] for n in names], axis=1))


def offsets(tables, names):
    at, out = 0, {}
    for n in names:
        out[n] = (at, tables[n].shape[1])
        at += tables[n].shape[1]
    return out, at


def program(nc, io, out):
    tables = shape_tables()
    with ExitStack() as ctx:
        def sb(name, words, rows=P):
            return ctx.enter_context(nc.sbuf_tensor(name, [rows, words], F32))

        def sem(name):
            return ctx.enter_context(nc.semaphore(name))

        def sig(name, per_turn):
            return Signal(sem(name), per_turn)

        xs = sb("xs", T * D)
        x = xs[:].rearrange("p (t d) -> p t d", t=T)
        shared_at, shared_w = offsets(tables, SHARED)
        first_at, first_w = offsets(tables, FIRST)
        second_at, second_w = offsets(tables, SECOND)
        shared_c = sb("shared_c", shared_w)
        phase_c = sb("phase_c", second_w)
        gains = sb("gains", N_GAIN)
        stat = sb("stat", 96)
        stat2 = sb("stat2", 224)
        turns_i = ctx.enter_context(nc.sbuf_tensor("turns_i", [P, 1], mybir.dt.int32))
        with ExitStack() as first_block:
            def first_sb(name, shape, dtype=F32R):
                return first_block.enter_context(nc.sbuf_tensor(name, [P] + shape, dtype))

            arena1 = first_sb("arena1", [21392], F32)
            uT = first_sb("hidden_split", [2, 2, 4, SEQ])
            hTp = first_sb("h_split", [2, KD, SEQ])
            split = first_sb("weights_split", [SPLITS, 2, PIECE])
            raw = first_sb("weights_raw", [RAWS, PIECE], F32)
        arena2 = sb("arena2", 29572)
        with ExitStack() as projections:
            def second_sb(name, shape, dtype=F32R):
                return projections.enter_context(nc.sbuf_tensor(name, [P] + shape, dtype))

            hTp2 = second_sb("h_split2", [2, KD, SEQ])
            second_sb("gap2", [12], F32)
            split2 = second_sb("weights_split2", [SPLITS2, 2, PIECE2])
            raw2 = second_sb("weights_raw2", [RAWS2, PIECE2], F32)
        hTs = sb("hTs", KD * SEQ)
        hT = hTs[:].rearrange("p (k s) -> p k s", k=KD)
        ring = sb("ring", SLOTS * SLOT)
        psum = ctx.enter_context(nc.psum_tensor("psum", [P, 8, 512], F32))

        def shared(name):
            o, w = shared_at[name]
            return shared_c[:, o:o + w]

        def first(name):
            o, w = first_at[name]
            return phase_c[:, o:o + w]

        def second(name):
            o, w = second_at[name]
            return phase_c[:, o:o + w]

        ident, causal = shared("ident"), shared("causal")

        def slot(s, n=SLOT):
            return ring[:, s * SLOT:s * SLOT + n]

        def area(o, n):
            return arena1[:, o:o + n]

        proj = area(0, T * IN_W).rearrange("p (t w) -> p t w", t=T)
        xn = area(5520, T * D).rearrange("p (t d) -> p t d", t=T)
        q = area(7568, T * MLA_H * QK).rearrange("p (t h e) -> p t h e", t=T, h=MLA_H)
        kfull = area(9104, T * MLA_H * QK).rearrange("p (t h e) -> p t h e", t=T, h=MLA_H)
        mix = area(7568, T * D).rearrange("p (t d) -> p t d", t=T)
        kv = area(10640, T * MLA_H * 128).rearrange("p (t h e) -> p t h e", t=T, h=MLA_H)
        qTm = area(12688, MLA_H * SEQ).rearrange("p (h s) -> p h s", h=MLA_H)
        kTm = area(14736, MLA_H * SEQ).rearrange("p (h s) -> p h s", h=MLA_H)
        dsaT = area(16784, 3 * SEQ).rearrange("p (c s) -> p c s", c=3)
        retT = area(17552, 4 * SEQ).rearrange("p (c s) -> p c s", c=4)
        idxT = area(18576, 3 * SEQ).rearrange("p (c s) -> p c s", c=3)
        rel = area(19344, 2 * 512).rearrange("p (b w) -> p b w", b=2)
        score = area(20368, 256)
        left = area(20624, 256)
        dsa_mask = area(20880, T * SEQ).rearrange("p (t s) -> p t s", t=T)
        ki4 = area(20368, T * P).rearrange("p (t c e) -> p t c e", t=T, c=4)
        kd = area(12688, T * P).rearrange("p (t c e) -> p t c e", t=T, c=2)
        scores = [proj[:, 0, b * 512:b * 512 + 512] for b in range(2)]
        probsT = [proj[:, 1, b * 512:b * 512 + 512] for b in range(2)]
        ret_s = [xn.rearrange("p t d -> p (t d)")[:, b * 256:b * 256 + 256] for b in range(len(RET_UNITS))]
        ret_o = rel[:, 0, :].rearrange("p (g e) -> p g e", e=RET_E)
        ret_sq = rel[:, 1, :].rearrange("p (g e) -> p g e", e=RET_E)
        hid_sq = [area(14736 + b * 512, 512) for b in range(4)]
        dve_tmp = [rel[:, b, :] for b in range(2)]
        pool_tmp = [area(14736 + b * 512, 512) for b in range(2)]

        sumsq, std, rstd = stat[:, 0:4], stat[:, 4:8], stat[:, 8:12]
        wi = stat[:, 12:28].rearrange("p (t h) -> p t h", t=T)
        top8 = stat[:, 28:36]
        rowmax, rowsum = stat[:, 36:40], stat[:, 40:44]
        rowmax2 = [rowmax, stat[:, 82:86]]
        rinv = [stat[:, 44 + 4 * b:48 + 4 * b] for b in range(3)]
        ret_mean, ret_var, ret_rstd = stat[:, 56:64], stat[:, 64:72], stat[:, 72:80]
        eps_c = stat[:, 80:81]

        def area(o, n):
            return arena2[:, o:o + n]

        qkv = area(0, T * 3 * ATT_W).rearrange("p (t w) -> p t w", t=T)
        pf = area(4608, T * RW_IN).rearrange("p (t w) -> p t w", t=T)
        gates = area(8256, T * GATE_W).rearrange("p (t w) -> p t w", t=T)
        xn2 = area(8256, T * D).rearrange("p (t d) -> p t d", t=T)
        wide = lambda o: area(o, T * RW_W).rearrange("p (t w) -> p t w", t=T)
        bufA, bufB, bufK, bufR, rw_g = (wide(12352 + 1024 * j) for j in range(5))
        prev = area(12352, T * RW_IN).rearrange("p (t w) -> p t w", t=T)
        mu = area(16000, RW_IN)
        vec = {n: area(17472 + RW_W * j, RW_W) for j, n in enumerate(("w0", "a0", "k_k", "k_a", "r_k", "ln_w", "ln_b"))}
        qT = area(21056, ATT_H // 2 * SEQ).rearrange("p (c s) -> p c s", s=SEQ)
        kT = area(22592, ATT_H // 2 * SEQ).rearrange("p (c s) -> p c s", s=SEQ)
        g_final = area(21056, D)
        lora_w = area(22592, 3 * RW_W).rearrange("p (j w) -> p j w", j=3)
        bias_m = area(24128, ATT_H * SEQ).rearrange("p (h k) -> p h k", h=ATT_H)
        bias_row = area(24128, 384)
        bias_tab = area(24512, ATT_H)
        qk_gain = area(24600, 2 * GRP * ATT_E).rearrange("p (j g e) -> p j g e", j=2, g=GRP)
        att_s = [area(27200 + 768 * b, 768) for b in range(2)]
        qk_sq = area(27200, T * ATT_W).rearrange("p (t w) -> p t w", t=T)
        att_p = area(28736, 768)
        loraT = area(28736, 3 * SEQ).rearrange("p (j s) -> p j s", j=3)
        att = hTs[:, 0:512].rearrange("p (t w) -> p t w", t=T)
        attT = hTs[:, 512:1024].rearrange("p (k s) -> p k s", k=2)
        oT = hTs[:, 1024:2048].rearrange("p (k s) -> p k s", k=4)
        rwT = [area(1024 * j, 1024).rearrange("p (c s) -> p c s", c=PAIRS) for j in range(4)]
        core = [{n: area(21056 + 3584 * par + 512 * j, 512).rearrange("p (c s) -> p c s", c=PAIRS)
                 for j, n in enumerate(("NT", "T", "TT", "X", "Mak", "Mrb", "Mrk"))} for par in range(2)]
        rhs = [core[par]["X"].rearrange("p c s -> p (c s)")[:, 0:PAIRS * RW_E].rearrange("p (c e) -> p c e", c=PAIRS)
               for par in range(2)]
        rw_u = area(28224, RW_W).rearrange("p (h e) -> p h e", h=RW_H)
        state = area(28736, PAIRS * RW_E).rearrange("p (c e) -> p c e", c=PAIRS)
        minus_state = area(28992, PAIRS * RW_E).rearrange("p (c e) -> p c e", c=PAIRS)
        rw_o = bufA.rearrange("p t (h e) -> p (t h) e", e=RW_E)
        rw_sq = bufK.rearrange("p t (h e) -> p (t h) e", e=RW_E)
        w_route = area(29248, KD * (EG + NE)).rearrange("p (k n) -> p k n", k=KD)
        b_route = area(29536, EG + NE)
        logits = area(21056, T * (EG + NE)).rearrange("p (t n) -> p t n", t=T)
        ra = [area(21200 + 64 * j, T * NE) for j in range(8)]
        moe_slot = [ring[:, s * SLOT:(s + 1) * SLOT] for s in range(SLOTS)] + [area(j * SLOT, SLOT) for j in range(2)]
        xe = area(12352, KD * P).rearrange("p (k n) -> p k n", k=KD)
        silu_g = area(13376, D_EXP)
        hid = area(13888, D_EXP)
        hidT = area(14400, D_EXP).rearrange("p (f n) -> p f n", f=D_EXP // P)
        y_rows = area(15424, D)
        take = area(16448, T * P).rearrange("p (t j n) -> p t j n", t=T, j=EPT)
        give = area(16704, T * P).rearrange("p (t j n) -> p t j n", t=T, j=EPT)
        giveT = area(16960, SEQ)
        place = area(17216, PASSES * NE * T).rearrange("p (q e t) -> p q e t", q=PASSES, t=T)
        gate_tab = area(17472, PASSES * NE * T).rearrange("p (q e t) -> p q e t", q=PASSES, t=T)
        zeros, ones = area(17728, P), area(17856, P)
        taken = area(17984, T * NE).rearrange("p (t e) -> p t e", t=T)
        place_now, gate_now = (stat2[:, 180 + 4 * j:184 + 4 * j].rearrange("p (e t) -> p e t", t=T) for j in range(2))
        fullest = stat2[:, 192:196]
        turns_f = stat2[:, 196:197]
        qk_ss = stat2[:, 0:48].rearrange("p (j t h) -> p j t h", j=2, t=T)
        kk_n, bonus, rw_mean, rw_var = (stat2[:, 48 + 16 * j:64 + 16 * j] for j in range(4))
        head_rows = lambda a, t: a[:, t * RW_H:(t + 1) * RW_H]
        sdec = stat2[:, 112:116]
        gn_eps_c = stat2[:, 190:191]
        bias_dram = nc.dram_tensor("bias_by_distance", (ATT_H, 384), F32).ap()

        consts_loaded = sem("consts_loaded")
        x_loaded = sem("x_loaded")
        consts_set = sem("consts_set")
        out_stored = sem("out_stored")
        slot_loaded = [sem(f"slot_loaded{s}") for s in range(SLOTS)]
        gains_loaded = sem("gains_loaded")
        LU = Units(sem("layer_unit_full"), sem("layer_emptied_act"), sem("layer_emptied_dve"), layer_plan())
        raw_loaded = [sem(f"raw_loaded{s}") for s in range(RAWS)]
        LW = SplitWeights(layer_pieces(), LU, raw_loaded, sem("weights_hi"), {"P": sem("weights_lo_pool"), "V": sem("weights_lo_dve")},
                          sem("weights_used"), raw, split, 1)
        hT_hi = sig("hT_hi", 16)
        hid_hi = sig("hid_hi", 2 * FFB)
        std_ready = sig("std_ready", 3)
        xn_ready = sig("xn_ready", 3 * T)
        idx_roped = sig("idx_roped", 1)
        kr_roped = sig("kr_roped", 1)
        q_roped = sig("q_roped", 1)
        kfull_ready = sig("kfull_ready", 1)
        dsa_roped = sig("dsa_roped", 1)
        ret_roped = sig("ret_roped", 1)
        rel_read = sig("rel_read", len(IDX_UNITS))
        rowmax_ready = sig("rowmax_ready", NG)
        shifted = sig("shifted", NG)
        probs_ready = sig("probs_ready", NG)
        silu_ready = sig("silu_ready", 1)
        ret_var_ready = sig("ret_var_ready", 1)
        ret_std_ready = sig("ret_std_ready", 1)
        ret_ready = sig("ret_ready", 1)
        hid_sq_ready = sig("hid_sq_ready", 2 * FFB)
        hid_ready = sig("hid_ready", 2 * FFB)
        x_done = sig("x_done", 1)

        SU = Units(sem("second_unit_full"), sem("second_emptied_act"), sem("second_emptied_dve"), second_plan())
        raw2_loaded = [sem(f"raw2_loaded{s}") for s in range(RAWS2)]
        PW = SplitWeights(second_pieces(), SU, raw2_loaded, sem("weights2_hi"), {"P": sem("weights2_lo"), "V": None},
                          sem("weights2_used"), raw2, split2, 0)
        hT2_hi = sig("hT2_hi", 4)
        SW = WeightRing(slot_loaded, second_weights())
        second_c_loaded = sem("second_c_loaded")
        gains2_loaded = sem("gains2_loaded")
        g_final_loaded = sem("g_final_loaded")
        std2_ready = sem("std2_ready")
        x_normed = sem("x_normed")
        xn2_ready = sem("xn2_ready")
        mu_loaded, vec_loaded, lora_loaded = sem("mu_loaded"), sem("vec_loaded"), sem("lora_loaded")
        qk_gain_loaded, bias_tab_loaded, route_loaded = sem("qk_gain_loaded"), sem("bias_tab_loaded"), sem("route_loaded")
        prev_zero = sem("prev_zero")
        prev_loaded = sem("prev_loaded")
        pm_ready = sem("pm_ready")
        lora_in = sem("lora_in")
        wa_in = sem("wa_in")
        wa_ready = sem("wa_ready")
        kk_ss, kk_std = sem("kk_ss"), sem("kk_std")
        preproc_done = sem("preproc_done")
        bonus_ready, bonus_v = sem("bonus_ready"), sem("bonus_v")
        bias_done, bias_stored, bias_loaded = sem("bias_done"), sem("bias_stored"), sem("bias_loaded")
        qk_ss_ready, qk_std = sem("qk_ss_ready"), sem("qk_std")
        qk_ready = sem("qk_ready")
        att_max = sem("att_max")
        att_exp = sem("att_exp")
        exp_incl, exp_excl = sem("exp_incl"), sem("exp_excl")
        scaled = sem("scaled")
        core_masked = sem("core_masked")
        core_start = sem("core_start")
        state_ready = sem("state_ready")
        gn_ss, gn_std = sem("gn_ss"), sem("gn_std")
        o_ready = sem("o_ready")
        mixed = sem("mixed")
        route_max, route_exp = sem("route_max"), sem("route_exp")
        pair_diff, pair_exp = sem("pair_diff"), sem("pair_exp")
        gate_ready = sem("gate_ready")
        EU = Units(sem("moe_unit_full"), sem("moe_emptied_act"), sem("moe_emptied_dve"), moe_plan())
        moe_loaded = [sem(f"moe_loaded{s}") for s in range(MOE_SLOTS)]
        moe_done = sem("moe_done")
        fills_ready = sem("fills_ready")
        taken_ready = sem("taken_ready")
        places_ready = sem("places_ready")
        take_ready = sig("take_ready", 1)
        FU = Units(sem("final_unit_full"), sem("final_emptied_act"), sem("final_emptied_dve"), interleave("acc", 2 * T, (0, 1, 2, 3), "V"))

        def second_weight(name):
            kind, b = name
            if kind == "att_out":
                return io["w_att_out_2"][0].rearrange("(k p) n -> p k n", p=P), HPG * ATT_E // P, D
            if kind == "rwkv_out":
                return io["w_rwkv_out_2"][0].rearrange("(k p) n -> p k n", p=P), RW_W // P, D
            return io["w_out_2"][0, :, b * 512:b * 512 + 512].rearrange("(k p) n -> p k n", p=P), KD, 512

        def second_piece(name):
            kind, b, i = name
            first_col = {"qkv": 0, "rw": 3 * ATT_W, "gate": 3 * ATT_W + RW_IN}[kind]
            c, w = {"rw": RW_BLOCKS, "qkv": QKV_BLOCKS, "gate": GATE_BLOCKS}[kind][b]
            src = io["w_in_2"][0, i * 256:(i + 1) * 256, first_col + c:first_col + c + w]
            return src.rearrange("(k p) n -> p k n", p=P), 2, w

        def second_slot(name):
            _, k, w = second_weight(name)
            return slot(SW.where[name][0], k * w).rearrange("p (k n) -> p k n", k=k)

        block = ctx.enter_context(nc.Block())

        def layer_weight(name, l):
            kind, b, i = name
            if kind == "in":
                c, w = IN_BLOCKS[b]
                src = io["w_in"][l, i * 512:(i + 1) * 512, c:c + w]
            elif kind == "uq":
                src, w = io["w_uq"][l, i * 2 * P:(i + 1) * 2 * P, :], MLA_H * QK
            elif kind == "ukv":
                src, w = io["w_ukv"][l], MLA_H * (NOPE + MLA_V)
            elif kind == "out":
                src, w = io["w_out"][l, i * 512:(i + 1) * 512, b * 512:(b + 1) * 512], 512
            elif kind == "ff1":
                src, w = io["w_ff1"][l, :, b * 512 + i * 256:b * 512 + (i + 1) * 256], 256
            else:
                src, w = io["w_ff2"][l, b * 512 + i * 256:b * 512 + (i + 1) * 256, :], D
            k = {"in": 4, "uq": 2, "ukv": KV_RANK // P, "out": 4, "ff1": KD, "ff2": 2}[kind]
            return src.rearrange("(k p) n -> p k n", p=P), k, w

        def piece_words(W, j):
            _, k, w = layer_weight(W.pieces[j][0], 0) if W is LW else second_piece(W.pieces[j][0])
            return k * w

        def split_low(W, eng, j, turn):
            n = piece_words(W, j)
            W.wait_hi(eng, j, turn)
            eng.tensor_tensor(W.part(j, 1, n), W.raw(j, n), W.part(j, 0, n).bitcast(F32),
                              ALU.subtract).then_inc(W.lo[W.pieces[j][1]], 1)

        def row(name):
            o, w = ROWS[name]
            return io["rows2"][0:1, o:o + w].to_broadcast([P, w])

        @block.sync
        def _(sp):
            sp.dma_start(shared_c[:], io["shared_c"]).then_inc(consts_loaded, 16)
            sp.dma_start(x, io["x"][0].rearrange("(t p) d -> p t d", p=P)).then_inc(x_loaded, 16)
            sp.dma_start(phase_c[:, 0:first_w], io["first_c"]).then_inc(consts_loaded, 16)
            with sp.Fori(0, DEPTH) as l:
                for j, (name, _, _) in enumerate(LW.pieces):
                    LW.wait_raw_free(sp, j, l)
                    src, k, w = layer_weight(name, l)
                    sp.dma_start(LW.raw(j, k * w).rearrange("p (k n) -> p k n", k=k), src).then_inc(raw_loaded[j % RAWS], 16)
            units = UnitView(SU, sp, psum)
            for e in "PV":
                sp.wait_ge(LW.lo[e], (DEPTH + 1) * len(LW.lo_order[e]))
            for j, (name, _, _) in enumerate(PW.pieces):
                PW.wait_raw_free(sp, j, 0)
                src, k, w = second_piece(name)
                sp.dma_start(PW.raw(j, k * w).rearrange("p (k n) -> p k n", k=k), src).then_inc(raw2_loaded[j % RAWS2], 16)
                if j == RAWS2 - 1:
                    sp.wait_ge(x_done.sem, DEPTH + 1)
                    sp.dma_start(g_final, row("g_final")).then_inc(g_final_loaded, 16)
                    sp.dma_start(mu, row("mu")).then_inc(mu_loaded, 16)
                    sp.dma_start(bias_tab[0:BUCKETS, :], io["rel_bias_table_2"]).then_inc(bias_tab_loaded, 16)
                    sp.dma_start(bias_tab[BUCKETS:BUCKETS + ATT_H, :], io["shared_c"][0:ATT_H, 0:ATT_H]).then_inc(bias_tab_loaded, 16)
                    for i, n in enumerate(("q_gain", "k_gain")):
                        sp.dma_start(qk_gain[:, i, :, :].rearrange("p g e -> p (g e)"), row(n)).then_inc(qk_gain_loaded, 16)
                    sp.dma_start(lora_w[0:LORA_W, 0, :], io["rwkv_w_up_2"][0]).then_inc(lora_loaded, 16)
                    sp.dma_start(lora_w[LORA_W:P, 0, :], io["rwkv_a_up_2"][0]).then_inc(lora_loaded, 16)
                    sp.dma_start(lora_w[:, 1, :], io["rwkv_g_up_2"][0, 0:P, :]).then_inc(lora_loaded, 16)
                    sp.dma_start(lora_w[0:LORA_G - P, 2, :], io["rwkv_g_up_2"][0, P:LORA_G, :]).then_inc(lora_loaded, 16)
                if name == ("qkv", 1, 2):
                    units.wait_emptied(*(("rw", i) for i in range(PROJ_RW)))
                    for t in range(T):
                        sp.dma_start(prev[1:P, t, :], pf[0:P - 1, t, :]).then_inc(prev_loaded, 16)
                    sp.dma_start(prev[0:1, 1, :], pf[P - 1:P, 0, :]).then_inc(prev_loaded, 16)
                    sp.wait_ge(bias_done, 1)
                    sp.dma_start(bias_dram, bias_row[0:ATT_H, :]).then_inc(bias_stored, 16)
                if name == ("qkv", 3, 1):
                    sp.wait_ge(pm_ready, 1)
                    for n in vec:
                        sp.dma_start(vec[n], row(n)).then_inc(vec_loaded, 16)
            sp.wait_ge(bias_stored, 16)
            sp.wait_ge(qk_ready, 1)
            sp.dma_start(bias_m, bass.AP(bias_dram.tensor, 0, [[1, P], [384, ATT_H], [1, SEQ]])).then_inc(bias_loaded, 16)
            units.wait_full(("gate", PROJ_GATE - 1))
            for name, _ in SW.blocks:
                s = SW.where[name][0]
                src, k, w = second_weight(name)
                sp.dma_start(slot(s, k * w).rearrange("p (k n) -> p k n", k=k), src).then_inc(slot_loaded[s], 16)

            def matrices(first_expert):
                for i, (w, k) in enumerate((("w_expert_gate_2", KD), ("w_expert_up_2", KD), ("w_expert_down_2", D_EXP // P))):
                    for j in range(EPT):
                        s = EPT * i + j
                        yield (moe_slot[s].rearrange("p (k n) -> p k n", k=k),
                               io[w][0, first_expert + j].rearrange("(k p) n -> p k n", p=P), s)

            for dst, src, s in matrices(0):
                units.wait_full(SW.last[s] if s < SLOTS else ("oT", 1))
                sp.dma_start(dst, src).then_inc(moe_loaded[s], 16)
            sp.wait_ge(places_ready, 1)
            with sp.Fori(1, sp.value_load(turns_i[0:1, 0:1], min_val=TURNS, max_val=TURNS * PASSES)) as turn:
                for dst, src, s in matrices(turn % TURNS * EPT):
                    if s % EPT == 0:
                        sp.wait_ge(EU.full, turn * EU.n + EU.u[(("gate", 0), ("up", 0), ("y", 1))[s // EPT]][0])
                    sp.dma_start(dst, src).then_inc(moe_loaded[s], 16)
            sp.wait_ge(moe_done, 1)
            sp.dma_start(out[0].rearrange("(t p) d -> p t d", p=P), x).then_inc(out_stored, 16)
            sp.wait_ge(out_stored, 16)

        def bridge(pe, units, key, n):
            bank = units.begin(key)
            for _ in range(n):
                pe.matmul(bank[:, 0:SEQ], ident, shared("causal")[:, 0:SEQ], start=True, stop=True)

        def transposes(pe, units, stage, src):
            for j in range(4):
                bank = units.begin((stage, j))
                for kk in range(2):
                    for t in range(T):
                        k = 2 * j + kk
                        ins = pe.transpose(bank[:, kk * SEQ + t * P:kk * SEQ + (t + 1) * P],
                                           src[:, t, k * P:(k + 1) * P], ident)
                units.finish((stage, j), ins)

        def token_major(pe, units, key, lhs, w):
            bank = units.begin(key)
            n, k = w.shape[2], w.shape[1]
            for i in range(k):
                ins = pe.matmul(bank[:, 0:n], lhs(i), w[:, i, :], start=(i == 0), stop=(i == k - 1))
            units.finish(key, ins)

        @block.tensor
        def _(pe):
            pe.wait_ge(consts_loaded, 32)
            def split_products(W, units, h, weight, turn):
                def product(out, a, b, first, last):
                    pe.matmul(out, a[0], b[0], start=first, stop=False)
                    pe.matmul(out, a[0], b[1], start=False, stop=False)
                    return pe.matmul(out, a[1], b[0], start=False, stop=last)

                def arrived(name):
                    j = W.index[name]
                    _, k, w = weight(name)
                    W.wait_lo(pe, j, turn)
                    return [W.part(j, which, k * w).rearrange("p (k n) -> p k n", k=k) for which in range(2)]

                def read(name, ins):
                    if W.pieces[W.index[name]][2] is None:
                        ins.then_inc(W.used, 1)

                def project(stage, pieces, cols, first_k=0):
                    k0 = first_k
                    for i, name in enumerate(pieces):
                        w, last = arrived(name), i == len(pieces) - 1
                        nk = w[0].shape[1]
                        for u, c in cols:
                            for t in range(T):
                                bank = units.bank((stage, u + t)) if i else units.begin((stage, u + t))
                                for k in range(nk):
                                    ins = product(bank[:, 0:c.stop - c.start], [h[:, which, k0 + k, t * P:(t + 1) * P] for which in range(2)],
                                                  [part[:, k, c] for part in w], i == 0 and k == 0, last and k == nk - 1)
                                if last:
                                    units.finish((stage, u + t), ins)
                        read(name, ins)
                        k0 += nk
                return product, arrived, read, project

            pe.sem_inc(LU.full, LU.n)
            pe.sem_inc(LW.used, len(LW.used_order))
            with pe.Fori(0, DEPTH) as l:
                units = UnitView(LU, pe, psum, l)

                product, arrived, read, project1 = split_products(LW, units, hTp, lambda name: layer_weight(name, l), l)
                bridge(pe, units, ("tr1", 0), 18)
                xn_ready.wait(pe, T, l)
                transposes(pe, units, "tr1", xn)
                bridge(pe, units, ("proj", 0), 9)
                units.wait_emptied(*(("tr1", j) for j in range(4)))
                for b, (_, w) in enumerate(IN_BLOCKS):
                    project1("proj", [("in", b, i) for i in range(2)], [(T * b, slice(0, w))])
                idx_roped.wait(pe, 1, l)
                for t in range(T):
                    bank = units.begin(("idxT", t))
                    for c in range(2):
                        pe.transpose(bank[:, c * P:(c + 1) * P], proj[:, t, C_QI + c * P:C_QI + (c + 1) * P], ident)
                    ins = pe.transpose(bank[:, 2 * P:3 * P], ki4[:, t, :, :].rearrange("p c e -> p (c e)"), ident)
                    units.finish(("idxT", t), ins)
                bridge(pe, units, ("tr2", 0), 8)
                xn_ready.wait(pe, 2 * T, l)
                transposes(pe, units, "tr2", xn)
                units.wait_emptied(*(("idxT", t) for t in range(T)))
                for i, (t, heads) in enumerate(IDX_UNITS):
                    bank, nk = units.begin(("idxS", i)), (t + 1) * P
                    for j, h in enumerate(heads):
                        r = slice(IDX_E * (h % 4), IDX_E * (h % 4 + 1))
                        ins = pe.matmul(bank[:, j * nk:(j + 1) * nk], idxT[r, h // 4, t * P:(t + 1) * P],
                                        idxT[r, 2, 0:nk], start=True, stop=True)
                    units.finish(("idxS", i), ins)
                units.wait_emptied(*(("tr2", j) for j in range(4)))
                w = MLA_H * QK // 2
                project1("uq", [("uq", 0, i) for i in range(3)], [(T * c, slice(c * w, (c + 1) * w)) for c in range(2)])
                project1("ukv", [("ukv", 0, 0)], [(T * c, slice(c * 512, (c + 1) * 512)) for c in range(2)], Q_RANK // P)
                dsa_roped.wait(pe, 1, l)
                for t in range(T):
                    bank = units.begin(("dsaT", t))
                    for c in range(2):
                        pe.transpose(bank[:, c * P:(c + 1) * P], proj[:, t, C_AQ + c * P:C_AQ + (c + 1) * P], ident)
                    ins = pe.transpose(bank[:, 2 * P:3 * P], kd[:, t, :, :].rearrange("p c e -> p (c e)"), ident)
                    units.finish(("dsaT", t), ins)
                ret_roped.wait(pe, 1, l)
                for t in range(T):
                    bank = units.begin(("retT", t))
                    for c in range(4):
                        ins = pe.transpose(bank[:, c * P:(c + 1) * P], proj[:, t, C_RQ + c * P:C_RQ + (c + 1) * P], ident)
                    units.finish(("retT", t), ins)
                units.wait_emptied(*(("retT", t) for t in range(T)))
                for i, (t, s, h0) in enumerate(RET_UNITS):
                    bank = units.begin(("retS", i))
                    r = slice(RET_E * h0, RET_E * (h0 + 1))
                    for j, h in enumerate((h0, h0 + 2)):
                        ins = pe.matmul(bank[:, j * P:(j + 1) * P], retT[r, 2 + h // 2, s * P:(s + 1) * P],
                                        retT[r, h // 2, t * P:(t + 1) * P], start=True, stop=True)
                    units.finish(("retS", i), ins)
                q_roped.wait(pe, 1, l)
                kfull_ready.wait(pe, 1, l)
                for t in range(T):
                    for j in range(4):
                        bank = units.begin(("mlaT", 4 * t + j))
                        src = (q, kfull)[j // 2]
                        for c in range(4):
                            ins = pe.transpose(bank[0:QK, c * P:(c + 1) * P], src[:, t, 4 * (j % 2) + c, :], ident)
                        units.finish(("mlaT", 4 * t + j), ins)
                units.wait_emptied(*(("retS", i) for i in range(len(RET_UNITS))))
                for t in range(T):
                    bank = units.begin(("retO", t))
                    for h in range(RET_H):
                        mine = [i for i, u in enumerate(RET_UNITS) if (u[0], u[2]) == (t, h % 2)]
                        for i in mine:
                            s = RET_UNITS[i][1]
                            ins = pe.matmul(bank[:, h * RET_E:(h + 1) * RET_E], ret_s[i][:, h // 2 * P:(h // 2 + 1) * P],
                                            proj[:, s, C_RV + h * RET_E:C_RV + (h + 1) * RET_E],
                                            start=(i == mine[0]), stop=(i == mine[-1]))
                    units.finish(("retO", t), ins)
                units.wait_emptied(*(("dsaT", t) for t in range(T)), *(("mlaT", j) for j in range(4 * T)))

                def attend_scores(g):
                    dsa, t, heads = GROUPS[g]
                    bank, nk = units.begin(("S", g)), (t + 1) * P
                    for j, h in enumerate(heads):
                        if dsa:
                            r = slice(DSA_E * (h % 2), DSA_E * (h % 2 + 1))
                            qT, kT = dsaT[r, h // 2, t * P:(t + 1) * P], dsaT[r, 2, 0:nk]
                        else:
                            qT, kT = qTm[0:QK, h, t * P:(t + 1) * P], kTm[0:QK, h, 0:nk]
                        ins = pe.matmul(bank[:, j * nk:(j + 1) * nk], qT, kT, start=True, stop=True)
                    units.finish(("S", g), ins)

                def turn_probs(g):
                    probs_ready.wait(pe, g + 1, l)
                    bank = units.begin(("PT", g))
                    for c in range(len(GROUPS[g][2]) * (GROUPS[g][1] + 1)):
                        ins = pe.transpose(bank[:, c * P:(c + 1) * P], scores[g % 2][:, c * P:(c + 1) * P], ident)
                    units.finish(("PT", g), ins)

                def attend_values(g):
                    dsa, t, heads = GROUPS[g]
                    units.wait_emptied(("PT", g))
                    bank = units.begin(("O", g))
                    for j, h in enumerate(heads):
                        for s in range(t + 1):
                            c = j * (t + 1) + s
                            v = proj[:, s, C_AV:C_AV + DSA_E] if dsa else kv[:, s, h, NOPE:NOPE + MLA_V]
                            ins = pe.matmul(bank[:, j * MLA_V:(j + 1) * MLA_V], probsT[g % 2][:, c * P:(c + 1) * P], v,
                                            start=(s == 0), stop=(s == t))
                    units.finish(("O", g), ins)

                for i in range(NG + 2):
                    if i < NG:
                        attend_scores(i)
                    if 1 <= i <= NG:
                        turn_probs(i - 1)
                    if i >= 2:
                        attend_values(i - 2)
                units.wait_emptied(*(("O", g) for g in range(NG)))
                ret_ready.wait(pe, 1, l)
                transposes(pe, units, "mixT", mix)
                bridge(pe, units, ("wout", 0), 4)
                units.wait_emptied(*(("mixT", j) for j in range(4)))
                for c in range(2):
                    project1("wout", [("out", c, i) for i in range(2)], [(T * c, slice(0, 512))])
                bridge(pe, units, ("tr3", 0), 13)
                xn_ready.wait(pe, 3 * T, l)
                transposes(pe, units, "tr3", xn)
                bridge(pe, units, ("ff1", 0), 4)
                units.wait_emptied(*(("tr3", j) for j in range(4)))

                def ff1(b):
                    for j in range(2):
                        w = arrived(("ff1", b, j))
                        bank = units.begin(("ff1", 2 * b + j))
                        for f in range(2):
                            for k in range(KD):
                                ins = product(bank[:, f * SEQ:(f + 1) * SEQ], [part[:, k, f * P:(f + 1) * P] for part in w],
                                              [hTp[:, which, k, :] for which in range(2)], k == 0, k == KD - 1)
                        units.finish(("ff1", 2 * b + j), ins)

                def ff2(b):
                    hid_ready.wait(pe, 2 * b + 2, l)
                    for i in range(2):
                        w = arrived(("ff2", b, i))
                        for u in range(2 * T):
                            t, c = u % T, u // T
                            bank = units.begin(("ff2", u)) if b == 0 and i == 0 else units.bank(("ff2", u))
                            for f in range(2):
                                ins = product(bank, [uT[:, which, b % 2, 2 * i + f, t * P:(t + 1) * P] for which in range(2)],
                                              [part[:, f, c * 512:(c + 1) * 512] for part in w],
                                              b == 0 and i == 0 and f == 0, b == FFB - 1 and i == 1 and f == 1)
                            if b == FFB - 1 and i == 1:
                                units.finish(("ff2", u), ins)
                        read(("ff2", b, i), ins)

                for b in range(FFB):
                    ff1(b)
                    if b:
                        ff2(b - 1)
                ff2(FFB - 1)
            units = UnitView(SU, pe, psum)

            def weights(name):
                s, i = SW.where[name]
                pe.wait_ge(slot_loaded[s], 16 * i)
                return second_slot(name)

            _, _, _, project2 = split_products(PW, units, hTp2, second_piece, 0)

            def project(stage, blocks):
                for b, (_, w) in enumerate(blocks):
                    project2(stage, [(stage, b, i) for i in range(4)], [(T * b, slice(0, w))])

            bridge(pe, units, ("tr1", 0), 28)
            pe.wait_ge(xn2_ready, T)
            transposes(pe, units, "tr1", xn2)
            units.wait_emptied(*(("tr1", j) for j in range(4)))
            project("rw", RW_BLOCKS)
            pe.wait_ge(second_c_loaded, 16)
            pe.wait_ge(bias_tab_loaded, 32)
            bank, r = units.begin(("bias", 0)), slice(0, BUCKETS + ATT_H)
            units.finish(("bias", 0), pe.matmul(bank[0:ATT_H, 0:384], bias_tab[r, :], second("bucket_hot")[r, :],
                                                start=True, stop=True))
            project("qkv", QKV_BLOCKS)
            pe.wait_ge(lora_in, 1)
            for t in range(T):
                bank = units.begin(("loraT", t))
                pe.transpose(bank[:, 0:P], pf[:, t, C_XW:C_XG], ident)
                pe.transpose(bank[:, P:2 * P], pf[:, t, C_XG:C_XG + P], ident)
                units.finish(("loraT", t), pe.transpose(bank[0:LORA_G - P, 2 * P:3 * P], pf[:, t, C_XG + P:RW_IN], ident))
            pe.wait_ge(lora_loaded, 64)
            units.wait_emptied(*(("loraT", t) for t in range(T)))
            for t in range(T):
                c = slice(t * P, (t + 1) * P)
                for j, r in enumerate((slice(0, LORA_W), slice(LORA_W, P))):
                    bank = units.begin(("lora", 3 * t + j))
                    units.finish(("lora", 3 * t + j), pe.matmul(bank, loraT[r, 0, c], lora_w[r, 0, :], start=True, stop=True))
                bank, rest = units.begin(("lora", 3 * t + 2)), slice(0, LORA_G - P)
                pe.matmul(bank, loraT[:, 1, c], lora_w[:, 1, :], start=True, stop=False)
                units.finish(("lora", 3 * t + 2), pe.matmul(bank, loraT[rest, 2, c], lora_w[rest, 2, :], start=False, stop=True))
            project("gate", GATE_BLOCKS)
            pe.wait_ge(bias_loaded, 16)
            pe.wait_ge(qk_ready, 1)
            for j in range(6):
                bank = units.begin(("qkT", j))
                for c in range(2):
                    for t in range(T):
                        col = j // 3 * ATT_W + (2 * (j % 3) + c) * P
                        ins = pe.transpose(bank[:, c * SEQ + t * P:c * SEQ + (t + 1) * P], qkv[:, t, col:col + P], ident)
                units.finish(("qkT", j), ins)
            units.wait_emptied(*(("qkT", j) for j in range(6)))
            for i in range(NA + 2):
                if i < NA:
                    t, hg = ATT_UNITS[i]
                    bank, nk = units.begin(("S", i)), (t + 1) * P
                    r = slice(ATT_E * (hg % 2), ATT_E * (hg % 2 + 1))
                    per_bank = 512 // SEQ if t else GRP
                    for g0 in range(0, GRP, per_bank):
                        g1 = min(g0 + per_bank, GRP)
                        pe.matmul(bank[:, g0 * nk:g1 * nk].rearrange("p (g k) -> p g k", k=nk), second("flip"),
                                  bias_m[:, g0 * HPG + hg:(g1 - 1) * HPG + hg + 1:HPG, SEQ - nk:SEQ], start=True, stop=False)
                        for g in range(g0, g1):
                            c = (g * HPG + hg) // 2
                            ins = pe.matmul(bank[:, g * nk:(g + 1) * nk], qT[r, c, t * P:(t + 1) * P], kT[r, c, 0:nk],
                                            start=False, stop=(g == g1 - 1))
                    units.finish(("S", i), ins)
                if 1 <= i <= NA:
                    t = ATT_UNITS[i - 1][0]
                    pe.wait_ge(att_exp, i)
                    bank = units.begin(("PT", i - 1))
                    for c in range(GRP * (t + 1)):
                        ins = pe.transpose(bank[:, c * P:(c + 1) * P], att_s[(i - 1) % 2][:, c * P:(c + 1) * P], ident)
                    units.finish(("PT", i - 1), ins)
                if i >= 2:
                    t, hg = ATT_UNITS[i - 2]
                    units.wait_emptied(("PT", i - 2))
                    bank = units.begin(("O", i - 2))
                    for g in range(GRP):
                        for s in range(t + 1):
                            v = 2 * ATT_W + (g * HPG + hg) * ATT_E
                            c = g * (t + 1) + s
                            ins = pe.matmul(bank[:, 0:ATT_E], att_p[:, c * P:(c + 1) * P], qkv[:, s, v:v + ATT_E],
                                            start=(c == 0), stop=(c == GRP * (t + 1) - 1))
                    units.finish(("O", i - 2), ins)
            pe.wait_ge(wa_ready, 1)
            for t in range(T):
                for j, n in enumerate(("cum_incl", "cum_excl")):
                    bank = units.begin(("cum", 2 * t + j))
                    units.finish(("cum", 2 * t + j), pe.matmul(bank, second(n), bufR[:, t, :], start=True, stop=True))
            bank = units.begin(("sdec", 0))
            for c in range(PAIRS):
                pe.matmul(bank[:, c:c + 1], bufR[:, 0, c * P:(c + 1) * P], second("halves")[:, 1:2], start=True, stop=False)
                ins = pe.matmul(bank[:, c:c + 1], bufR[:, 1, c * P:(c + 1) * P], second("halves")[:, 0:1], start=False, stop=True)
            units.finish(("sdec", 0), ins)
            for t in range(T):
                pe.wait_ge(scaled, t + 1)
                for j, src in enumerate((bufA, bufB, bufK, bufR)):
                    bank = units.begin(("rwT", 4 * t + j))
                    for c in range(PAIRS):
                        ins = pe.transpose(bank[:, c * P:(c + 1) * P], src[:, t, c * P:(c + 1) * P], ident)
                    units.finish(("rwT", 4 * t + j), ins)
            units.wait_emptied(*(("O", i) for i in range(NA)))
            bank = units.begin(("attT", 0))
            for k in range(2):
                for t in range(T):
                    ins = pe.transpose(bank[:, k * SEQ + t * P:k * SEQ + (t + 1) * P], att[:, t, k * P:(k + 1) * P], ident)
            units.finish(("attT", 0), ins)
            w = weights(("att_out", 0))
            units.wait_emptied(("attT", 0))
            for u in range(2 * T):
                t, c = u // 2, u % 2
                token_major(pe, units, ("yatt", u), lambda k: attT[:, k, t * P:(t + 1) * P], w[:, :, c * 512:(c + 1) * 512])
            units.wait_emptied(*(("rwT", j) for j in range(8)))
            for t in range(T):
                tok = slice(t * P, (t + 1) * P)
                for par in range(2):
                    r, n = slice(RW_E * par, RW_E * (par + 1)), 2 * t + par
                    A, B, K, Rr = (rwT[j][r] for j in range(4))
                    for name, left_m, right_m in (("NT", B, A), ("N", A, B), ("Mak", K, A), ("Mrb", B, Rr), ("Mrk", K, Rr)):
                        bank = units.begin((name, n))
                        for c in range(PAIRS):
                            ins = pe.matmul(bank[:, c * P:(c + 1) * P], left_m[:, c, tok], right_m[:, c, tok],
                                            start=True, stop=True)
                        units.finish((name, n), ins)
                last = len(LEVELS) - 1
                for i in range(len(LEVELS)):
                    for par in range(2):
                        n, m = 2 * t + par, core[par]
                        if i == 0:
                            pe.wait_ge(core_start, n + 1)
                        else:
                            units.wait_emptied(("TX", 8 * n + i - 1))
                            bank = units.begin(("TT", 8 * n + i))
                            for c in range(PAIRS):
                                ins = pe.transpose(bank[:, c * P:(c + 1) * P], m["T"][:, c, :], ident)
                            units.finish(("TT", 8 * n + i), ins)
                        bank = units.begin(("X", 8 * n + i))
                        for c in range(PAIRS):
                            ins = pe.matmul(bank[:, c * P:(c + 1) * P], m["NT"][:, c, :], m["T"][:, c, :], start=True, stop=True)
                        units.finish(("X", 8 * n + i), ins)
                    for par in range(2):
                        n, m = 2 * t + par, core[par]
                        units.wait_emptied(("X", 8 * n + i), *([("TT", 8 * n + i)] if i else []))
                        key, left_m, right_m = (("TX", 8 * n + i), "TT", "X") if i < last else (("XT", 8 * n + i), "X", "TT")
                        bank = units.begin(key)
                        for c in range(PAIRS):
                            ins = pe.matmul(bank[:, c * P:(c + 1) * P], m[left_m][:, c, :], m[right_m][:, c, :], start=True, stop=True)
                        units.finish(key, ins)

                def value(c, par):
                    h = 2 * c + par
                    return pf[:, t, C_V + h * RW_E:C_V + (h + 1) * RW_E]

                if t:
                    pe.wait_ge(state_ready, 1)
                for par in range(2):
                    n, m, r = 2 * t + par, core[par], slice(RW_E * par, RW_E * (par + 1))
                    units.wait_emptied(("Mak", n), ("Mrb", n), ("Mrk", n), ("XT", 8 * n + len(LEVELS) - 1))
                    bank = units.begin(("RHS", n))
                    for c in range(PAIRS):
                        o = bank[:, c * RW_E:(c + 1) * RW_E]
                        ins = pe.matmul(o, m["Mak"][:, c, :], value(c, par), start=True, stop=(t == 0))
                        if t:
                            ins = pe.matmul(o, rwT[0][r, c, tok], minus_state[r, c, :], start=False, stop=True)
                    units.finish(("RHS", n), ins)
                for par in range(2):
                    n, m = 2 * t + par, core[par]
                    units.wait_emptied(("RHS", n))
                    bank = units.begin(("U", n))
                    for c in range(PAIRS):
                        ins = pe.matmul(bank[:, c * RW_E:(c + 1) * RW_E], m["TT"][:, c, :], rhs[par][:, c, :], start=True, stop=True)
                    units.finish(("U", n), ins)
                for par in range(2):
                    n, m, r = 2 * t + par, core[par], slice(RW_E * par, RW_E * (par + 1))
                    units.wait_emptied(("U", n))
                    bank = units.begin(("OUT", n))
                    for c in range(PAIRS):
                        o = bank[:, c * RW_E:(c + 1) * RW_E]
                        pe.matmul(o, m["Mrb"][:, c, :], rw_u[:, 2 * c + par, :], start=True, stop=False)
                        ins = pe.matmul(o, m["Mrk"][:, c, :], value(c, par), start=False, stop=(t == 0))
                        if t:
                            ins = pe.matmul(o, rwT[3][r, c, tok], state[r, c, :], start=False, stop=True)
                    units.finish(("OUT", n), ins)
                if t == 0:
                    bank = units.begin(("state", 0))
                    for c in range(PAIRS):
                        o, cols = bank[:, c * P:(c + 1) * P], slice(c * P, (c + 1) * P)
                        pe.matmul(o, bufB[:, 0, cols], rw_u[:, 2 * c:2 * c + 2, :].rearrange("p h e -> p (h e)"), start=True, stop=False)
                        ins = pe.matmul(o, bufK[:, 0, cols], pf[:, 0, C_V + c * P:C_V + (c + 1) * P], start=False, stop=True)
                    units.finish(("state", 0), ins)
            bridge(pe, units, ("oT", 0), 18)
            pe.wait_ge(o_ready, 1)
            for j in range(2):
                bank = units.begin(("oT", j))
                for kk in range(2):
                    for t in range(T):
                        k = 2 * j + kk
                        ins = pe.transpose(bank[:, kk * SEQ + t * P:kk * SEQ + (t + 1) * P], bufA[:, t, k * P:(k + 1) * P], ident)
                units.finish(("oT", j), ins)
            w = weights(("rwkv_out", 0))
            units.wait_emptied(("oT", 0), ("oT", 1))
            for u in range(2 * T):
                t, c = u // 2, u % 2
                token_major(pe, units, ("yrw", u), lambda k: oT[:, k, t * P:(t + 1) * P], w[:, :, c * 512:(c + 1) * 512])
            bridge(pe, units, ("mixT", 0), 6)
            pe.wait_ge(mixed, 1)
            transposes(pe, units, "mixT", gates[:, :, 0:D])
            units.wait_emptied(*(("mixT", j) for j in range(4)))
            for c in range(2):
                w = weights(("out", c))
                for t in range(T):
                    token_major(pe, units, ("wout", T * c + t), lambda k: hT[:, k, t * P:(t + 1) * P], w)
            bridge(pe, units, ("tr2", 0), 10)
            pe.wait_ge(xn2_ready, 2 * T)
            transposes(pe, units, "tr2", xn2)
            units.wait_emptied(*(("tr2", j) for j in range(4)))
            pe.wait_ge(route_loaded, 48)
            for t in range(T):
                token_major(pe, units, ("route", t), lambda k: hT[:, k, t * P:(t + 1) * P], w_route)
            pe.wait_ge(fills_ready, 1)
            units.wait_emptied(*(("route", t) for t in range(T)))
            final = UnitView(FU, pe, psum)
            for u in range(2 * T):
                pe.matmul(final.bank(("acc", u)), zeros, second("levels")[:, 0:512], start=True, stop=False)
            pe.wait_ge(taken_ready, 1)
            for i in range(T + 1):
                bank = units.begin(("rank", i))[:, 0:NE]
                left = [ones] * i + [second("incl")] if i < T else [ones] * T
                for s, m in enumerate(left):
                    ins = pe.matmul(bank, m, taken[:, s, :], start=(s == 0), stop=(s == len(left) - 1))
                units.finish(("rank", i), ins)
            units.wait_emptied(*(("rank", i) for i in range(T + 1)))
            pe.sem_inc(EU.full, EU.n)
            pe.wait_ge(places_ready, 1)
            with pe.Fori(0, pe.value_load(turns_i[0:1, 0:1], min_val=TURNS, max_val=TURNS * PASSES)) as turn:
                units = UnitView(EU, pe, psum, turn)

                def arrived(s, k):
                    pe.wait_ge(moe_loaded[s], turn * 16 + 16)
                    return moe_slot[s].rearrange("p (k n) -> p k n", k=k)

                take_ready.wait(pe, 1, turn)
                for i in range(2):
                    bank = units.begin(("gx", i))
                    for kk in range(4):
                        k = 4 * i + kk
                        for t in range(T):
                            ins = pe.matmul(bank[:, kk * P:(kk + 1) * P], xn2[:, t, k * P:(k + 1) * P],
                                            take[:, t, :, :].rearrange("p j n -> p (j n)"), start=(t == 0), stop=(t == T - 1))
                    units.finish(("gx", i), ins)
                bank = units.begin(("gt", 0))
                for t in range(T):
                    ins = pe.transpose(bank[:, t * P:(t + 1) * P], give[:, t, :, :].rearrange("p j n -> p (j n)"), ident)
                units.finish(("gt", 0), ins)
                units.wait_emptied(("gx", 0), ("gx", 1))
                half = lambda j: slice(j * SLOTS_E, (j + 1) * SLOTS_E)
                for i, stage in enumerate(("gate", "up")):
                    w = [arrived(EPT * i + j, KD) for j in range(EPT)]
                    bank = units.begin((stage, 0))
                    for k in range(KD):
                        for j in range(EPT):
                            ins = pe.matmul(bank[half(j), :], xe[:, k, half(j)], w[j][:, k, :], start=(k == 0), stop=(k == KD - 1))
                    units.finish((stage, 0), ins)
                units.wait_emptied(("up", 0))
                bank = units.begin(("hT", 0))
                for f in range(D_EXP // P):
                    ins = pe.transpose(bank[:, f * P:(f + 1) * P], hid[:, f * P:(f + 1) * P], ident)
                units.finish(("hT", 0), ins)
                w = [arrived(2 * EPT + j, D_EXP // P) for j in range(EPT)]
                units.wait_emptied(("hT", 0))
                for c in range(2):
                    bank = units.begin(("y", c))
                    for f in range(D_EXP // P):
                        for j in range(EPT):
                            ins = pe.matmul(bank[half(j), :], hidT[:, f, half(j)], w[j][:, f, c * 512:(c + 1) * 512],
                                            start=(f == 0), stop=(f == D_EXP // P - 1))
                    units.finish(("y", c), ins)
                units.wait_emptied(("gt", 0), ("y", 0), ("y", 1))
                for u in range(2 * T):
                    t, c = u // 2, u % 2
                    pe.matmul(final.bank(("acc", u)), giveT[:, t * P:(t + 1) * P], y_rows[:, c * 512:(c + 1) * 512],
                              start=False, stop=False)
            for u in range(2 * T):
                final.finish(("acc", u), pe.matmul(final.bank(("acc", u)), zeros, second("levels")[:, 0:512], start=False, stop=True))

        def sums_of_squares(act, parts, ready):
            for rows, scratch, c, _ in parts:
                act.activation(scratch, rows, ACT.Square, accum_out=sumsq[:, c:c + 1])
            act.drain()
            for _, _, c, width in parts:
                ins = act.activation(std[:, c:c + 1], sumsq[:, c:c + 1], ACT.Sqrt, bias=eps_c, scale=1.0 / width)
            ins.then_inc(ready, 1)

        def act_transposed(act, units, stage, gain):
            for j in range(0, 4, 2):
                bank = units.wait_full((stage, j))
                for kk in range(2):
                    k = 2 * j + kk
                    ins = act.activation(hT[:, k, :], bank[:, kk * SEQ:(kk + 1) * SEQ], ACT.Copy, scale=gain(k))
                units.emptied_by((stage, j), ins, "A")

        def dve_transposed(dve, units, stage, gain):
            for j in range(1, 4, 2):
                bank = units.wait_full((stage, j))
                for kk in range(2):
                    k = 2 * j + kk
                    ins = dve.tensor_scalar(hT[:, k, :], bank[:, kk * SEQ:(kk + 1) * SEQ], gain(k), None, ALU.mult)
                units.emptied_by((stage, j), ins, "V")

        def high_transposed(act, units, stage, gain, h, ready):
            for j in range(4):
                bank = units.wait_full((stage, j))
                for kk in range(2):
                    k, g = 2 * j + kk, gain(2 * j + kk)
                    src = bank[:, kk * SEQ:(kk + 1) * SEQ]
                    ins = act.activation(h[:, 0, k, :], src, ACT.Copy, **({} if g is None else {"scale": g}))
                ins.then_inc(ready.sem, 1)

        def low_transposed(dve, units, stage, nth, gain, h, ready, turn):
            for j in range(4):
                bank = units.wait_full((stage, j))
                ready.wait(dve, 4 * nth + j + 1, turn)
                for kk in range(2):
                    k, g = 2 * j + kk, gain(2 * j + kk)
                    src, hi, lo = bank[:, kk * SEQ:(kk + 1) * SEQ], h[:, 0, k, :].bitcast(F32), h[:, 1, k, :]
                    if g is None:
                        ins = dve.tensor_tensor(lo, src, hi, ALU.subtract)
                    else:
                        ins = dve.scalar_tensor_tensor(lo, src, g, hi, ALU.mult, ALU.subtract)
                units.emptied_by((stage, j), ins, "V")

        def high_parts(act, W, units, turn):
            done = [0]

            def split_high(n):
                for j in range(done[0], min(n + 1, W.n)):
                    w = piece_words(W, j)
                    W.wait_loaded(act, j, turn)
                    W.wait_split_free(units, j, turn)
                    act.activation(W.part(j, 0, w), W.raw(j, w), ACT.Copy).then_inc(W.hi, 1)
                done[0] = max(done[0], n + 1)

            return split_high

        @block.scalar
        def _(act):
            act.wait_ge(x_loaded, 16)
            act.wait_ge(consts_set, 1)
            with act.Fori(0, DEPTH) as l:
                units = UnitView(LU, act, psum, l)

                def gain(first_col):
                    return lambda k: gains[:, first_col + k:first_col + k + 1]

                split_high = high_parts(act, LW, units, l)

                def copy_out(key, dst, n):
                    bank = units.wait_full(key)
                    units.emptied_by(key, act.activation(dst, bank[:, 0:n], ACT.Copy), "A")

                x_done.wait(act, 1, l)
                act.dma_start(gains[:], io["gains"][l]).then_inc(gains_loaded, 16)
                sums_of_squares(act, [(x[:, t, :], xn[:, t, :], t, D) for t in range(T)], std_ready.sem)
                split_high(SPLITS - 1)
                act.wait_ge(gains_loaded, l * 16 + 16)
                high_transposed(act, units, "tr1", gain(G_MIX), hTp, hT_hi)
                for b, (c, w) in enumerate(IN_BLOCKS):
                    split_high(2 * b + SPLITS)
                    copy_out(("proj", T * b + 1), proj[:, 1, c:c + w], w)
                    split_high(2 * b + 1 + SPLITS)
                units.wait_emptied(*(("proj", T * b + t) for t in range(T) for b in range(2)))
                sums_of_squares(act, [(proj[:, t, C_CQ:C_CKV], xn[:, t, C_CQ:C_CKV], t, Q_RANK) for t in range(T)] +
                                [(proj[:, t, C_CKV:C_KR], xn[:, t, C_CKV:C_KR], T + t, KV_RANK) for t in range(T)], std_ready.sem)
                high_transposed(act, units, "tr2", gain(G_QKV), hTp, hT_hi)
                for i, (t, heads) in enumerate(IDX_UNITS):
                    bank, n = units.wait_full(("idxS", i)), len(heads) * (t + 1) * P
                    if i >= 2:
                        rel_read.wait(act, i - 1, l)
                    else:
                        idx_roped.wait(act, 1, l)
                        kr_roped.wait(act, 1, l)
                    units.emptied_by(("idxS", i), act.activation(rel[:, i % 2, 0:n], bank[:, 0:n], ACT.Relu), "A")
                split_high(LW.index["ukv", 0, 0])
                w = MLA_H * QK // 2
                for c in range(2):
                    for t in range(T):
                        copy_out(("uq", T * c + t),
                                 q[:, t, :, :].rearrange("p h e -> p (h e)")[:, c * w:(c + 1) * w], w)
                for c in range(2):
                    for t in range(T):
                        copy_out(("ukv", T * c + t),
                                 kv[:, t, 4 * c:4 * c + 4, :].rearrange("p h e -> p (h e)"), 512)
                units.wait_emptied(*(("ukv", j) for j in range(2 * T)))
                kr_roped.wait(act, 1, l)
                for t in range(T):
                    act.activation(kfull[:, t, :, 0:NOPE], kv[:, t, :, 0:NOPE], ACT.Copy)
                    ins = act.activation(kfull[:, t, :, NOPE:QK],
                                         proj[:, t, None, C_KR:C_AQ].to_broadcast([P, MLA_H, ROPE]), ACT.Copy)
                ins.then_inc(kfull_ready.sem, 1)
                for t in range(T):
                    split_high(LW.index["ukv", 0, 0] + 1 + t)
                    for j in range(4):
                        bank = units.wait_full(("mlaT", 4 * t + j))
                        dst = (qTm, kTm)[j // 2][0:QK, 4 * (j % 2):4 * (j % 2) + 4, t * P:(t + 1) * P]
                        units.emptied_by(("mlaT", 4 * t + j), act.activation(
                            dst, bank[0:QK, :].rearrange("p (c s) -> p c s", c=4), ACT.Copy), "A")
                split_high(LW.index["ukv", 0, 0] + SPLITS)
                width = lambda g: len(GROUPS[g][2]) * (GROUPS[g][1] + 1) * P
                for i in range(NG + 1):
                    if i < NG:
                        shifted.wait(act, i + 1, l)
                        act.activation(scores[i % 2][:, 0:width(i)], scores[i % 2][:, 0:width(i)], ACT.Exp).then_inc(probs_ready.sem, 1)
                    if i >= 1:
                        g = i - 1
                        bank = units.wait_full(("PT", g))
                        units.emptied_by(("PT", g), act.activation(probsT[g % 2][:, 0:width(g)], bank[:, 0:width(g)], ACT.Copy), "A")
                    if i == 3:
                        act.activation(proj[:, :, C_RG:IN_W], proj[:, :, C_RG:IN_W], ACT.Silu).then_inc(silu_ready.sem, 1)
                        ret_var_ready.wait(act, 1, l)
                        act.activation(ret_rstd, ret_var, ACT.Sqrt, bias=eps_c, scale=1.0 / RET_E).then_inc(ret_std_ready.sem, 1)
                high_transposed(act, units, "mixT", lambda k: gain(G_RET)(k - (KD - 2)) if k >= KD - 2 else None, hTp, hT_hi)
                split_high(LW.index["out", 1, 0] + SPLITS)
                units.wait_emptied(("wout", 2 * T - 1))
                sums_of_squares(act, [(x[:, t, :], xn[:, t, :], t, D) for t in range(T)], std_ready.sem)
                split_high(LW.index["out", 1, 1] + SPLITS)
                high_transposed(act, units, "tr3", gain(G_MLP), hTp, hT_hi)
                for b in range(FFB + 1):
                    for j in range(2 if b < FFB else 0):
                        i = 2 * b + j
                        split_high(LW.index["ff1", b, j] + SPLITS)
                        hid_sq_ready.wait(act, i + 1, l)
                        act.activation(uT[:, 0, b % 2, 2 * j:2 * j + 2, :].rearrange("p f s -> p (f s)"),
                                       hid_sq[i % 4], ACT.Copy).then_inc(hid_hi.sem, 1)
                    if b:
                        split_high(LW.index["ff2", b - 1, 1] + SPLITS)
            units = UnitView(SU, act, psum)

            def gain2(first_col):
                return lambda k: gains[:, first_col + k:first_col + k + 1]

            def empty(key, dst, n, func=ACT.Copy):
                bank = units.wait_full(key)
                units.emptied_by(key, act.activation(dst, bank[:, 0:n], func), "A")

            x_rows = lambda: [(x[:, t, :], xn2[:, t, :], t, D) for t in range(T)]
            x_done.wait(act, DEPTH + 1)
            act.dma_start(gains[:, 0:2 * KD], io["gains2"]).then_inc(gains2_loaded, 16)
            act.dma_start(phase_c[:], io["second_c"]).then_inc(second_c_loaded, 16)
            sums_of_squares(act, x_rows(), std2_ready)
            split_high = high_parts(act, PW, units, 0)
            split_high(SPLITS2 - 1)

            def while_projecting(stage, b, emptyings):
                split_high(PW.index[stage, b, 2] + SPLITS2)
                emptyings()
                split_high(PW.index[stage, b, 3] + SPLITS2)

            act.wait_ge(x_normed, 1)
            sums_of_squares(act, x_rows(), std2_ready)
            act.wait_ge(gains2_loaded, 16)
            high_transposed(act, units, "tr1", gain2(0), hTp2, hT2_hi)
            for b, (c, w) in enumerate(RW_BLOCKS):
                while_projecting("rw", b, lambda: empty(("rw", T * b + 1), pf[:, 1, c:c + w], w))
            for b, (c, w) in enumerate(QKV_BLOCKS):
                while_projecting("qkv", b, lambda: empty(("qkv", T * b + 1), qkv[:, 1, c:c + w], w))
            act.wait_ge(pm_ready, 1)
            act.activation(pf[:, :, C_XG:RW_IN], pf[:, :, C_XG:RW_IN], ACT.Sigmoid)
            act.activation(pf[:, :, C_XW:C_XA], pf[:, :, C_XW:C_XA], ACT.Tanh).then_inc(lora_in, 1)
            for t in range(T):
                bank = units.wait_full(("loraT", t))
                act.activation(loraT[:, 0:2, t * P:(t + 1) * P], bank[:, 0:2 * P].rearrange("p (j s) -> p j s", j=2), ACT.Copy)
                units.emptied_by(("loraT", t), act.activation(
                    loraT[0:LORA_G - P, 2, t * P:(t + 1) * P], bank[0:LORA_G - P, 2 * P:3 * P], ACT.Copy), "A")
            for t in range(T):
                empty(("lora", 3 * t + 2), rw_g[:, t, :], RW_W)
            act.wait_ge(wa_in, 1)
            act.activation(bufB, bufB, ACT.Sigmoid)
            act.activation(bufR, bufR, ACT.Sigmoid).then_inc(wa_ready, 1)
            for b, (c, w) in enumerate(GATE_BLOCKS):
                while_projecting("gate", b, lambda: [empty(("gate", T * b + t), gates[:, t, c:c + w], w, ACT.Sigmoid) for t in range(T)])
                if b == 0:
                    act.wait_ge(kk_ss, 1)
                    act.activation(kk_n, kk_n, ACT.Sqrt).then_inc(kk_std, 1)
                    act.wait_ge(qk_ss_ready, 1)
                    act.activation(stat2[:, 0:48], stat2[:, 0:48], ACT.Sqrt, bias=eps_c, scale=1.0 / ATT_E).then_inc(qk_std, 1)
            for j in range(6):
                dst = (qT, kT)[j // 3][:, 2 * (j % 3):2 * (j % 3) + 2, :].rearrange("p c s -> p (c s)")
                empty(("qkT", j), dst, 512)
            for i in range(NA + 1):
                if i < NA:
                    n = GRP * (ATT_UNITS[i][0] + 1) * P
                    act.wait_ge(att_max, i + 1)
                    act.activation(att_s[i % 2][:, 0:n], units.wait_full(("S", i))[:, 0:n], ACT.Exp,
                                   bias=rowmax[:, i % 2:i % 2 + 1], accum_out=rowsum[:, i % 2:i % 2 + 1])
                    act.drain()
                    units.emptied_by(("S", i), act.activation(stat[:, 91:92], stat[:, 91:92], ACT.Copy), "A")
                    act.sem_inc(att_exp, 1)
                if i >= 1:
                    n = GRP * (ATT_UNITS[i - 1][0] + 1) * P
                    if i >= 2:
                        units.wait_full(("O", i - 2))
                    empty(("PT", i - 1), att_p[:, 0:n], n)
            for t in range(T):
                incl, excl = units.wait_full(("cum", 2 * t)), units.wait_full(("cum", 2 * t + 1))
                act.wait_ge(preproc_done, 1)
                if t:
                    units.wait_full(("sdec", 0))
                act.activation(bufK[:, t, :], incl, ACT.Exp, scale=-1.0)
                act.activation(excl, excl, ACT.Exp).then_inc(exp_excl, 1)
                if t == 0:
                    units.wait_full(("sdec", 0))
                act.activation(bufR[:, t, :], incl, ACT.Exp)
                act.drain()
                units.emptied_by(("cum", 2 * t), act.activation(stat[:, 90:91], stat[:, 90:91], ACT.Copy), "A")
                act.sem_inc(exp_incl, 1)
            empty(("sdec", 0), sdec, PAIRS, ACT.Exp)
            for t in range(T):
                for j in range(4):
                    bank = units.wait_full(("rwT", 4 * t + j))
                    units.emptied_by(("rwT", 4 * t + j), act.activation(
                        rwT[j][:, :, t * P:(t + 1) * P], bank.rearrange("p (c s) -> p c s", c=PAIRS), ACT.Copy), "A")
            empty(("attT", 0), hTs[:, 512:1024], 512)
            for t in range(T):
                for i in range(1, len(LEVELS)):
                    for par in range(2):
                        empty(("TT", 8 * (2 * t + par) + i), core[par]["TT"].rearrange("p c s -> p (c s)"), 512)
                    if t == 1 and i == 3:
                        act.wait_ge(gn_ss, 1)
                        act.activation(head_rows(rw_var, 0), head_rows(rw_var, 0), ACT.Sqrt, bias=gn_eps_c, scale=1.0 / RW_E).then_inc(gn_std, 1)
                for par in range(2):
                    empty(("RHS", 2 * t + par), rhs[par].rearrange("p c e -> p (c e)"), PAIRS * RW_E)
                for par in range(2):
                    bank = units.wait_full(("U", 2 * t + par))
                    units.emptied_by(("U", 2 * t + par), act.activation(
                        rw_u[:, par:RW_H:2, :], bank[:, 0:PAIRS * RW_E].rearrange("p (c e) -> p c e", c=PAIRS), ACT.Copy), "A")
            act.wait_ge(gn_ss, 2)
            act.activation(head_rows(rw_var, 1), head_rows(rw_var, 1), ACT.Sqrt, bias=gn_eps_c, scale=1.0 / RW_E).then_inc(gn_std, 1)
            for j in range(2):
                empty(("oT", j), oT[:, 2 * j:2 * j + 2, :].rearrange("p k s -> p (k s)"), 512)
            for j in range(4):
                empty(("mixT", j), hT[:, 2 * j:2 * j + 2, :].rearrange("p k s -> p (k s)"), 512)
            units.wait_emptied(("wout", 2 * T - 1))
            sums_of_squares(act, x_rows(), std2_ready)
            act_transposed(act, units, "tr2", gain2(KD))
            act.wait_ge(route_max, 1)
            act.activation(ra[0][:, 0:T * EG], ra[0][:, 0:T * EG], ACT.Exp).then_inc(route_exp, 1)
            act.wait_ge(pair_diff, 1)
            act.activation(ra[5][:, 0:T], ra[5][:, 0:T], ACT.Exp).then_inc(pair_exp, 1)
            act.wait_ge(places_ready, 1)
            with act.Fori(0, act.value_load(turns_i[0:1, 0:1], min_val=TURNS, max_val=TURNS * PASSES)) as turn:
                units = UnitView(EU, act, psum, turn)
                bank = units.wait_full(("gt", 0))
                units.emptied_by(("gt", 0), act.activation(giveT, bank[:, 0:SEQ], ACT.Copy), "A")
                bank = units.wait_full(("gate", 0))
                units.emptied_by(("gate", 0), act.activation(silu_g, bank, ACT.Silu), "A")
                bank = units.wait_full(("hT", 0))
                units.emptied_by(("hT", 0), act.activation(hidT.rearrange("p f n -> p (f n)"), bank, ACT.Copy), "A")
                bank = units.wait_full(("y", 0))
                units.emptied_by(("y", 0), act.activation(y_rows[:, 0:512], bank, ACT.Copy), "A")

        def rotate(e, x1, x2, cos, sin, tmp):
            shape = x1.shape
            cos, sin = (a.unsqueeze(2).to_broadcast(shape) for a in (cos, sin))
            m1, m2 = (b[:, 0:int(np.prod(shape[1:]))].rearrange("p (t h e) -> p t h e", t=shape[1], h=shape[2]) for b in tmp)
            e.tensor_tensor(m1, x1, sin, ALU.mult)
            e.tensor_tensor(m2, x2, sin, ALU.mult)
            e.drain()
            e.tensor_tensor(x1, x1, cos, ALU.mult)
            e.tensor_tensor(x2, x2, cos, ALU.mult)
            e.drain()
            e.tensor_tensor(x1, x1, m2, ALU.subtract)
            return e.tensor_tensor(x2, x2, m1, ALU.add)

        def angles(dim):
            return (first(f"{n}{dim}").rearrange("p (t e) -> p t e", t=T) for n in ("cos", "sin"))

        def halves(a):
            e = a.shape[3] // 2
            return a[:, :, :, 0:e], a[:, :, :, e:2 * e]

        def heads_of(c0, c1, e):
            return proj[:, :, c0:c1].rearrange("p t (h e) -> p t h e", e=e)

        @block.gpsimd
        def _(pool):
            pool.wait_ge(consts_loaded, 32)
            pool.sem_inc(LW.lo["P"], len(LW.lo_order["P"]))
            with pool.Fori(0, DEPTH) as l:
                units = UnitView(LU, pool, psum, l)

                def split_rest(first, last):
                    for j in LW.lo_order["P"]:
                        if LW.index[first] <= j <= LW.index[last]:
                            split_low(LW, pool, j, l)

                def wait_columns(c0, c1):
                    units.wait_emptied(*(("proj", T * b + t) for t in range(T)
                                         for b, (c, w) in enumerate(IN_BLOCKS) if c < c1 and c0 < c + w))

                split_rest(("in", 0, 0), ("uq", 0, 2))
                wait_columns(C_AQ, C_AV)
                rotate(pool, *halves(heads_of(C_AQ, C_AV, DSA_E)), *angles(DSA_E), pool_tmp)
                pool.drain()
                for t in range(T):
                    ins = pool.tensor_copy(kd[:, t, :, :], proj[:, t, None, C_AK:C_AV].to_broadcast([P, 2, DSA_E]))
                ins.then_inc(dsa_roped.sem, 1)
                split_rest(("ukv", 0, 0), ("ukv", 0, 0))
                wait_columns(C_RQ, C_RV)
                rotate(pool, *halves(heads_of(C_RQ, C_RV, RET_E)), *angles(RET_E), pool_tmp).then_inc(ret_roped.sem, 1)
                split_rest(("out", 0, 0), ("out", 0, 1))
                for g, (_, t, heads) in enumerate(GROUPS):
                    nk, nh = (t + 1) * P, len(heads)
                    s = scores[g % 2][:, 0:nh * nk].rearrange("p (h k) -> p h k", h=nh)
                    rowmax_ready.wait(pool, g + 1, l)
                    pool.tensor_tensor(s, s, rowmax2[g % 2][:, 0:nh].unsqueeze(2).to_broadcast([P, nh, nk]),
                                       ALU.subtract).then_inc(shifted.sem, 1)
                split_rest(("out", 1, 0), ("ff2", FFB - 1, 1))
            units = UnitView(SU, pool, psum)

            pool.wait_ge(x_done.sem, DEPTH + 1)
            pool.memset(prev[0:1, 0, :], 0.0).then_inc(prev_zero, 1)
            for j in range(PW.n):
                split_low(PW, pool, j, 0)
            pool.wait_ge(bonus_ready, 1)
            pool.wait_ge(scaled, T)
            pool.dma_start(w_route[:, :, 0:EG], io["w_group_router_2"][0].rearrange("(k p) n -> p k n", p=P)).then_inc(route_loaded, 16)
            pool.dma_start(w_route[:, :, EG:], io["w_expert_router_2"][0].rearrange("(k p) n -> p k n", p=P)).then_inc(route_loaded, 16)
            pool.dma_start(b_route, row("b_route")).then_inc(route_loaded, 16)
            pool.tensor_tensor(pf[:, :, C_R:C_K].rearrange("p t (h e) -> p t h e", e=RW_E),
                               pf[:, :, C_V:C_XW].rearrange("p t (h e) -> p t h e", e=RW_E),
                               bonus.rearrange("p (t h) -> p t h", t=T).unsqueeze(3).to_broadcast([P, T, RW_H, RW_E]),
                               ALU.mult).then_inc(bonus_v, 1)
            pool.memset(zeros, 0.0)
            pool.memset(ones, 1.0).then_inc(fills_ready, 1)
            eye = ident.unsqueeze(1).to_broadcast([P, PAIRS, P])
            for n, (t, par) in enumerate(CORE):
                m = core[par]
                pool.wait_ge(core_masked, n + 1)
                pool.tensor_tensor(m["TT"], m["NT"], second("level1T").unsqueeze(1).to_broadcast([P, PAIRS, P]), ALU.mult)
                pool.tensor_tensor(m["T"], m["T"], eye, ALU.add)
                pool.drain()
                pool.tensor_tensor(m["TT"], m["TT"], eye, ALU.add).then_inc(core_start, 1)

        def scale_rows(dve, parts):
            dve.reciprocal(rstd, std)
            dve.drain()
            for rows, scaled, c in parts:
                ins = dve.tensor_scalar(scaled, rows, rstd[:, c:c + 1], None, ALU.mult)
            return ins

        @block.vector
        def _(dve):
            dve.memset(stat[:], 1.0)
            dve.drain()
            dve.memset(eps_c, EPS).then_inc(consts_set, 1)
            dve.wait_ge(consts_loaded, 32)
            dve.wait_ge(x_loaded, 16)
            dve.sem_inc(x_done.sem, 1)
            dve.sem_inc(LW.lo["V"], len(LW.lo_order["V"]))
            with dve.Fori(0, DEPTH) as l:
                units = UnitView(LU, dve, psum, l)

                def gain(first_col):
                    return lambda k: gains[:, first_col + k:first_col + k + 1]

                def norm(k):
                    std_ready.wait(dve, k, l)
                    scale_rows(dve, [(x[:, t, :], xn[:, t, :], t) for t in range(T)]).then_inc(xn_ready.sem, T)

                def wait_columns(c0, c1):
                    units.wait_emptied(*(("proj", T * b + t) for t in range(T)
                                         for b, (c, w) in enumerate(IN_BLOCKS) if c < c1 and c0 < c + w))

                norm(1)
                dve.wait_ge(gains_loaded, l * 16 + 16)
                low_transposed(dve, units, "tr1", 0, gain(G_MIX), hTp, hT_hi, l)
                for b, (c, w) in enumerate(IN_BLOCKS):
                    bank = units.wait_full(("proj", T * b))
                    units.emptied_by(("proj", T * b), dve.tensor_copy(proj[:, 0, c:c + w], bank[:, 0:w]), "V")
                wait_columns(C_QI, C_RQ)
                rotate(dve, *halves(heads_of(C_QI, C_WI, IDX_E)), *angles(IDX_E), dve_tmp)
                dve.drain()
                dve.tensor_scalar(wi, proj[:, :, C_WI:C_RQ], IDX_H ** -0.5 * IDX_E ** -0.5, None, ALU.mult)
                for t in range(T):
                    ins = dve.tensor_copy(ki4[:, t, :, :], proj[:, t, None, C_KI:C_WI].to_broadcast([P, 4, IDX_E]))
                ins.then_inc(idx_roped.sem, 1)
                std_ready.wait(dve, 2, l)
                scale_rows(dve, [(proj[:, t, C_CQ:C_CKV], xn[:, t, C_CQ:C_CKV], t) for t in range(T)] +
                           [(proj[:, t, C_CKV:C_KR], xn[:, t, C_CKV:C_KR], T + t) for t in range(T)]
                           ).then_inc(xn_ready.sem, T)
                wait_columns(C_KR, C_AQ)
                rotate(dve, *halves(heads_of(C_KR, C_AQ, ROPE)), *angles(ROPE), dve_tmp).then_inc(kr_roped.sem, 1)
                for t in range(T):
                    bank = units.wait_full(("idxT", t))
                    units.emptied_by(("idxT", t), dve.tensor_copy(
                        idxT[:, :, t * P:(t + 1) * P], bank[:, 0:3 * P].rearrange("p (c s) -> p c s", c=3)), "V")
                low_transposed(dve, units, "tr2", 1, gain(G_QKV), hTp, hT_hi, l)
                for t in range(T):
                    nk = (t + 1) * P
                    s, r = score[:, 0:nk], left[:, 0:nk]
                    for i, (ti, heads) in enumerate(IDX_UNITS):
                        if ti != t:
                            continue
                        if heads[0]:
                            dve.drain()
                        units.wait_emptied(("idxS", i))
                        for j, h in enumerate(heads):
                            rel_h = rel[:, i % 2, j * nk:(j + 1) * nk]
                            if h == 0:
                                ins = dve.tensor_scalar(s, rel_h, wi[:, t, h:h + 1], None, ALU.mult)
                            else:
                                if j:
                                    dve.drain()
                                ins = dve.scalar_tensor_tensor(s, rel_h, wi[:, t, h:h + 1], s, ALU.mult, ALU.add)
                        ins.then_inc(rel_read.sem, 1)
                    dve.drain()
                    hidden = causal[:, T * P - nk:T * P]
                    dve.tensor_tensor(s, s, hidden, ALU.add)
                    dve.drain()
                    for i in range(TOPK // 8):
                        dve.max(top8, r if i else s)
                        dve.drain()
                        dve.match_replace(r, top8, r if i else s, TAKEN)
                        dve.drain()
                    dve.tensor_scalar(r, r, TAKEN, -MASKED, ALU.is_equal, ALU.mult)
                    dve.drain()
                    dve.scalar_tensor_tensor(dsa_mask[:, t, 0:nk], r, MASKED, hidden, ALU.add, ALU.add)
                units.wait_emptied(*(("uq", j) for j in range(2 * T)))
                rotate(dve, *halves(q[:, :, :, NOPE:QK]), *angles(ROPE), dve_tmp).then_inc(q_roped.sem, 1)
                for t in range(T):
                    bank = units.wait_full(("dsaT", t))
                    units.emptied_by(("dsaT", t), dve.tensor_copy(
                        dsaT[:, :, t * P:(t + 1) * P], bank[:, 0:3 * P].rearrange("p (c s) -> p c s", c=3)), "V")
                for t in range(T):
                    bank = units.wait_full(("retT", t))
                    units.emptied_by(("retT", t), dve.tensor_copy(
                        retT[:, :, t * P:(t + 1) * P], bank.rearrange("p (c s) -> p c s", c=4)), "V")
                decay = first("decay").rearrange("p (d h s) -> p d h s", d=T, h=RET_H)
                for i, (t, s, h0) in enumerate(RET_UNITS):
                    bank = units.wait_full(("retS", i))
                    units.emptied_by(("retS", i), dve.tensor_tensor(
                        ret_s[i].rearrange("p (h s) -> p h s", h=2), bank[:, 0:2 * P].rearrange("p (h s) -> p h s", h=2),
                        decay[:, t - s, h0:RET_H:2, :], ALU.mult), "V")

                for t in range(T):
                    g = slice(t * RET_H, (t + 1) * RET_H)
                    bank = units.wait_full(("retO", t))[:, 0:RET_H * RET_E].rearrange("p (h e) -> p h e", h=RET_H)
                    dve.tensor_reduce(ret_mean[:, g], bank, AX.X, ALU.add)
                    dve.drain()
                    dve.tensor_scalar(ret_mean[:, g], ret_mean[:, g], 1.0 / RET_E, None, ALU.mult)
                    dve.drain()
                    units.emptied_by(("retO", t), dve.tensor_tensor(
                        ret_o[:, g, :], bank, ret_mean[:, g].unsqueeze(2).to_broadcast([P, RET_H, RET_E]), ALU.subtract), "V")
                def mask_and_max(g):
                    dsa, t, heads = GROUPS[g]
                    nk, nh = (t + 1) * P, len(heads)
                    bank = units.wait_full(("S", g))[:, 0:nh * nk].rearrange("p (h k) -> p h k", h=nh)
                    s = scores[g % 2][:, 0:nh * nk].rearrange("p (h k) -> p h k", h=nh)
                    mask = dsa_mask[:, t, 0:nk] if dsa else causal[:, T * P - nk:T * P]
                    scale = DSA_E ** -0.5 if dsa else QK ** -0.5
                    units.emptied_by(("S", g), dve.scalar_tensor_tensor(
                        s, bank, scale, mask.unsqueeze(1).to_broadcast([P, nh, nk]), ALU.mult, ALU.add), "V")
                    dve.drain()
                    dve.tensor_reduce(rowmax2[g % 2][:, 0:nh], s, AX.X, ALU.max).then_inc(rowmax_ready.sem, 1)

                def row_sums(g):
                    nh, n = len(GROUPS[g][2]), len(GROUPS[g][2]) * (GROUPS[g][1] + 1) * P
                    probs_ready.wait(dve, g + 1, l)
                    dve.tensor_reduce(rowsum[:, 0:nh], scores[g % 2][:, 0:n].rearrange("p (h k) -> p h k", h=nh), AX.X, ALU.add)
                    dve.drain()
                    dve.reciprocal(rinv[g % 3][:, 0:nh], rowsum[:, 0:nh])
                    dve.drain()

                def attend_out(g):
                    dsa, t, heads = GROUPS[g]
                    bank, nh = units.wait_full(("O", g)), len(heads)
                    first_head = heads[0] + (MLA_H if dsa else 0)
                    step = heads[1] - heads[0]
                    units.emptied_by(("O", g), dve.tensor_tensor(
                        mix[:, t, :].rearrange("p (h e) -> p h e", e=MLA_V)[:, first_head:first_head + step * (nh - 1) + 1:step, :],
                        bank[:, 0:nh * MLA_V].rearrange("p (h e) -> p h e", h=nh),
                        rinv[g % 3][:, 0:nh].unsqueeze(2).to_broadcast([P, nh, MLA_V]), ALU.mult), "V")

                def retention_variance():
                    dve.drain()
                    dve.tensor_tensor(ret_sq, ret_o, ret_o, ALU.mult)
                    dve.drain()
                    dve.tensor_reduce(ret_var, ret_sq, AX.X, ALU.add).then_inc(ret_var_ready.sem, 1)

                def gate_retention():
                    ret_std_ready.wait(dve, 1, l)
                    dve.reciprocal(ret_rstd, ret_rstd)
                    dve.drain()
                    dve.tensor_tensor(ret_o, ret_o, ret_rstd.unsqueeze(2).to_broadcast([P, T * RET_H, RET_E]), ALU.mult)
                    dve.drain()
                    silu_ready.wait(dve, 1, l)
                    dve.tensor_tensor(mix[:, :, D - RET_H * RET_E:D],
                                      ret_o.rearrange("p (t h) e -> p t (h e)", t=T), proj[:, :, C_RG:IN_W],
                                      ALU.mult).then_inc(ret_ready.sem, 1)

                dve.drain()
                for i in range(NG + 2):
                    if i < NG:
                        mask_and_max(i)
                    if 1 <= i <= NG:
                        row_sums(i - 1)
                    if i >= 2:
                        attend_out(i - 2)
                    if i == 1:
                        retention_variance()
                    if i == 5:
                        gate_retention()
                low_transposed(dve, units, "mixT", 2, lambda k: gain(G_RET)(k - (KD - 2)) if k >= KD - 2 else None, hTp, hT_hi, l)
                for c in range(2):
                    for t in range(T):
                        bank = units.wait_full(("wout", T * c + t))
                        xc = x[:, t, c * 512:(c + 1) * 512]
                        units.emptied_by(("wout", T * c + t), dve.tensor_tensor(xc, bank, xc, ALU.add), "V")
                split_low(LW, dve, LW.index["ff1", 0, 1], l)
                norm(3)
                low_transposed(dve, units, "tr3", 3, gain(G_MLP), hTp, hT_hi, l)
                split_low_at = {LW.index[name] for name, e, _ in LW.pieces if e == "V"} - {LW.index["ff1", 0, 1]}

                def split_after(name):
                    if LW.index[name] + SPLITS in split_low_at:
                        split_low(LW, dve, LW.index[name] + SPLITS, l)

                for b in range(FFB + 1):
                    for j in range(2 if b < FFB else 0):
                        i = 2 * b + j
                        bank = units.wait_full(("ff1", i))
                        units.emptied_by(("ff1", i), dve.tensor_scalar(hid_sq[i % 4], bank, 0.0, None, ALU.max), "V")
                        dve.drain()
                        dve.tensor_tensor(hid_sq[i % 4], hid_sq[i % 4], hid_sq[i % 4], ALU.mult)
                        dve.drain()
                        dve.sem_inc(hid_sq_ready.sem, 1)
                        split_after(("ff1", b, j))
                        hid_hi.wait(dve, i + 1, l)
                        part = [uT[:, which, b % 2, 2 * j:2 * j + 2, :].rearrange("p f s -> p (f s)") for which in range(2)]
                        dve.tensor_tensor(part[1], hid_sq[i % 4], part[0].bitcast(F32), ALU.subtract).then_inc(hid_ready.sem, 1)
                    if b:
                        for i in range(2):
                            split_after(("ff2", b - 1, i))
                for u in range(2 * T):
                    t, c = u % T, u // T
                    bank = units.wait_full(("ff2", u))
                    xc = x[:, t, c * 512:(c + 1) * 512]
                    units.emptied_by(("ff2", u), dve.tensor_tensor(xc, bank, xc, ALU.add), "V")
                dve.drain()
                dve.sem_inc(x_done.sem, 1)
            units = UnitView(SU, dve, psum)

            def gain2(first_col):
                return lambda k: gains[:, first_col + k:first_col + k + 1]

            def per_head(a, shape):
                return a.unsqueeze(len(shape) - 1).to_broadcast(shape)

            def channels(name):
                return vec[name].unsqueeze(1).to_broadcast([P, T, RW_W])

            def done(ins):
                dve.drain()

            mul, add, sub = ALU.mult, ALU.add, ALU.subtract
            dve.memset(gn_eps_c, GN_EPS)
            dve.wait_ge(g_final_loaded, 16)
            dve.wait_ge(std2_ready, 1)
            dve.reciprocal(rstd, std)
            dve.drain()
            for t in range(T):
                ins = dve.scalar_tensor_tensor(x[:, t, :], x[:, t, :], rstd[:, t:t + 1], g_final, mul, mul)
            ins.then_inc(x_normed, 1)
            dve.wait_ge(std2_ready, 2)
            scale_rows(dve, [(x[:, t, :], xn2[:, t, :], t) for t in range(T)]).then_inc(xn2_ready, T)
            dve.wait_ge(gains2_loaded, 16)
            low_transposed(dve, units, "tr1", 0, gain2(0), hTp2, hT2_hi, None)
            for b, (c, w) in enumerate(RW_BLOCKS):
                bank = units.wait_full(("rw", T * b))
                units.emptied_by(("rw", T * b), dve.tensor_copy(pf[:, 0, c:c + w], bank[:, 0:w]), "V")
            bank = units.wait_full(("bias", 0))
            units.emptied_by(("bias", 0), dve.tensor_copy(bias_row[0:ATT_H, :], bank[0:ATT_H, 0:384]), "V")
            dve.drain()
            dve.sem_inc(bias_done, 1)
            dve.wait_ge(mu_loaded, 16)
            dve.wait_ge(prev_zero, 1)
            dve.wait_ge(prev_loaded, 48)
            dve.tensor_tensor(prev, prev, pf, sub)
            dve.drain()
            dve.tensor_tensor(prev, prev, mu.unsqueeze(1).to_broadcast([P, T, RW_IN]), mul)
            dve.drain()
            dve.tensor_tensor(pf, pf, prev, add).then_inc(pm_ready, 1)
            for b, (c, w) in enumerate(QKV_BLOCKS):
                bank = units.wait_full(("qkv", T * b))
                units.emptied_by(("qkv", T * b), dve.tensor_copy(qkv[:, 0, c:c + w], bank[:, 0:w]), "V")
            dve.wait_ge(vec_loaded, 16 * len(vec))
            for t in range(T):
                for j, (dst, n) in enumerate(((bufR, "w0"), (bufB, "a0"))):
                    bank = units.wait_full(("lora", 3 * t + j))
                    ins = dve.tensor_tensor(dst[:, t, :], bank, vec[n], add)
                    units.emptied_by(("lora", 3 * t + j), ins, "V")
            dve.drain()
            dve.sem_inc(wa_in, 1)
            r_, k_, v_ = (pf[:, :, c:c + RW_W] for c in (C_R, C_K, C_V))
            heads = lambda a: a.rearrange("p t (h e) -> p t h e", e=RW_E)
            hshape = [P, T, RW_H, RW_E]
            th = lambda a: a.rearrange("p (t h) -> p t h", t=T)
            dve.tensor_tensor(bufA, k_, channels("k_k"), mul)
            dve.drain()
            dve.tensor_tensor(bufK, bufA, bufA, mul)
            dve.drain()
            dve.tensor_reduce(th(kk_n), heads(bufK), AX.X, add).then_inc(kk_ss, 1)
            units.wait_emptied(*(("qkv", j) for j in range(PROJ_QKV)))
            qk = [qkv[:, :, j * ATT_W:(j + 1) * ATT_W].rearrange("p t (h e) -> p t h e", e=ATT_E) for j in range(2)]
            sq = qk_sq.rearrange("p t (h e) -> p t h e", e=ATT_E)
            for j in range(2):
                dve.tensor_tensor(sq, qk[j], qk[j], mul)
                dve.drain()
                ins = dve.tensor_reduce(qk_ss[:, j, :, :], sq, AX.X, add)
                if j == 0:
                    dve.drain()
            ins.then_inc(qk_ss_ready, 1)
            dve.wait_ge(qk_gain_loaded, 32)
            dve.wait_ge(qk_std, 1)
            dve.reciprocal(stat2[:, 0:48], stat2[:, 0:48])
            dve.drain()
            dve.tensor_scalar(qk_ss[:, 0, :, :], qk_ss[:, 0, :, :], ATT_E ** -0.5, None, mul)
            dve.drain()
            for j in range(2):
                dve.tensor_tensor(qk[j], qk[j], per_head(qk_ss[:, j, :, :], [P, T, ATT_H, ATT_E]), mul)
            dve.drain()
            for j in range(2):
                for t in range(T):
                    a = qk[j][:, t, :, :].rearrange("p (g h) e -> p g h e", g=GRP)
                    ins = dve.tensor_tensor(a, a, qk_gain[:, j, :, :].unsqueeze(2).to_broadcast([P, GRP, HPG, ATT_E]), mul)
            ins.then_inc(qk_ready, 1)
            dve.wait_ge(kk_std, 1)
            dve.wait_ge(wa_ready, 1)
            dve.tensor_scalar(kk_n, kk_n, 1e-12, None, ALU.max)
            dve.drain()
            dve.reciprocal(kk_n, kk_n)
            dve.drain()
            dve.tensor_tensor(heads(bufA), heads(bufA), per_head(th(kk_n), hshape), mul)
            for t in range(T):
                dve.scalar_tensor_tensor(bufK[:, t, :], bufB[:, t, :], -1.0, vec["k_a"], add, mul)
            dve.drain()
            for t in range(T):
                dve.scalar_tensor_tensor(k_[:, t, :], bufK[:, t, :], 1.0, k_[:, t, :], add, mul)
            dve.tensor_tensor(bufB, bufB, bufA, mul)
            dve.drain()
            dve.tensor_tensor(bufK, r_, k_, mul)
            dve.drain()
            dve.tensor_tensor(bufK, bufK, channels("r_k"), mul)
            dve.drain()
            dve.tensor_reduce(th(bonus), heads(bufK), AX.X, add).then_inc(bonus_ready, 1)
            dve.drain()
            dve.sem_inc(preproc_done, 1)
            for i in range(NA + 2):
                if i < NA:
                    t, hg = ATT_UNITS[i]
                    nk = (t + 1) * P
                    m = rowmax[:, i % 2:i % 2 + 1]
                    dve.tensor_reduce(m, units.wait_full(("S", i))[:, 0:GRP * nk], AX.X, ALU.max)
                    dve.drain()
                    dve.tensor_scalar(m, m, -1.0, None, mul).then_inc(att_max, 1)
                if 1 <= i <= NA:
                    dve.wait_ge(att_exp, i)
                    dve.reciprocal(rinv[(i - 1) % 3][:, 0:1], rowsum[:, (i - 1) % 2:(i - 1) % 2 + 1])
                    dve.drain()
                if i >= 2:
                    t, hg = ATT_UNITS[i - 2]
                    bank = units.wait_full(("O", i - 2))
                    units.emptied_by(("O", i - 2), dve.tensor_scalar(
                        att[:, t, hg * ATT_E:(hg + 1) * ATT_E], bank[:, 0:ATT_E], rinv[(i - 2) % 3][:, 0:1], None, mul), "V")
            for t in range(T):
                dve.wait_ge(exp_excl, t + 1)
                excl = units.bank(("cum", 2 * t + 1))
                units.emptied_by(("cum", 2 * t + 1), dve.tensor_tensor(bufA[:, t, :], excl, bufA[:, t, :], mul), "V")
                dve.wait_ge(exp_incl, t + 1)
                dve.tensor_tensor(bufB[:, t, :], bufB[:, t, :], bufK[:, t, :], mul)
                dve.tensor_tensor(bufR[:, t, :], bufR[:, t, :], r_[:, t, :], mul)
                dve.drain()
                dve.tensor_tensor(bufK[:, t, :], bufK[:, t, :], k_[:, t, :], mul)
                dve.drain()
                dve.sem_inc(scaled, 1)
            for u in range(2 * T):
                t, c = u // 2, u % 2
                bank = units.wait_full(("yatt", u))
                g = gates[:, t, c * 512:(c + 1) * 512]
                units.emptied_by(("yatt", u), dve.tensor_tensor(g, bank, g, mul), "V")
            def head_norm(t, step):
                o, sq = rw_o[:, t * RW_H:(t + 1) * RW_H, :], rw_sq[:, t * RW_H:(t + 1) * RW_H, :]
                mean, var, flat = head_rows(rw_mean, t), head_rows(rw_var, t), bufA[:, t, :]
                spread = lambda a: a.unsqueeze(2).to_broadcast([P, RW_H, RW_E])
                dve.drain()
                if step == 0:
                    dve.tensor_reduce(mean, o, AX.X, add)
                    dve.drain()
                    dve.tensor_scalar(mean, mean, 1.0 / RW_E, None, mul)
                elif step == 1:
                    dve.tensor_tensor(o, o, spread(mean), sub)
                    dve.drain()
                    dve.tensor_tensor(sq, o, o, mul)
                elif step == 2:
                    dve.tensor_reduce(var, sq, AX.X, add).then_inc(gn_ss, 1)
                elif step == 3:
                    dve.wait_ge(gn_std, t + 1)
                    dve.reciprocal(var, var)
                    dve.drain()
                    dve.tensor_tensor(o, o, spread(var), mul)
                elif step == 4:
                    dve.tensor_tensor(flat, flat, vec["ln_w"], mul)
                    dve.drain()
                    dve.tensor_tensor(flat, flat, vec["ln_b"], add)
                else:
                    dve.wait_ge(bonus_v, 1)
                    dve.tensor_tensor(flat, flat, r_[:, t, :], add)
                    dve.drain()
                    dve.tensor_tensor(flat, flat, rw_g[:, t, :], mul)
                dve.drain()

            every = lambda name: second(name).unsqueeze(1).to_broadcast([P, PAIRS, P])
            for t in range(T):
                for par in range(2):
                    n, m = 2 * t + par, core[par]
                    four = lambda key: units.wait_full(key).rearrange("p (c s) -> p c s", c=PAIRS)
                    for name, dst, mask in (("NT", "NT", "minus_strict"), ("N", "T", "minus_level1"), ("Mak", "Mak", "minus_strict"),
                                            ("Mrb", "Mrb", "incl"), ("Mrk", "Mrk", "incl")):
                        bank = four((name, n))
                        units.emptied_by((name, n), dve.tensor_tensor(m[dst], bank, every(mask), mul), "V")
                        if name == "N":
                            dve.drain()
                            dve.sem_inc(core_masked, 1)
                for i in range(len(LEVELS)):
                    level = second("levels")[:, i * P:(i + 1) * P].unsqueeze(1).to_broadcast([P, PAIRS, P])
                    for par in range(2):
                        key = ("X", 8 * (2 * t + par) + i)
                        bank = units.wait_full(key).rearrange("p (c s) -> p c s", c=PAIRS)
                        units.emptied_by(key, dve.tensor_tensor(core[par]["X"], bank, level, mul), "V")
                    for par in range(2):
                        stage, name = ("TX", "T") if i < len(LEVELS) - 1 else ("XT", "TT")
                        key, a = (stage, 8 * (2 * t + par) + i), core[par][name]
                        bank = units.wait_full(key).rearrange("p (c s) -> p c s", c=PAIRS)
                        if stage == "XT":
                            units.wait_emptied(("TT", key[1]))
                        units.emptied_by(key, dve.tensor_tensor(a, bank, a, add), "V")
                    if t == 1:
                        head_norm(0, i)
                for par in range(2):
                    key = ("OUT", 2 * t + par)
                    bank = units.wait_full(key)[:, 0:PAIRS * RW_E].rearrange("p (c e) -> p c e", c=PAIRS)
                    units.emptied_by(key, dve.tensor_copy(rw_o[:, t * RW_H + par:(t + 1) * RW_H:2, :], bank), "V")
                if t == 0:
                    bank = units.wait_full(("state", 0)).rearrange("p (c e) -> p c e", c=PAIRS)
                    units.wait_emptied(("sdec", 0))
                    for par in range(2):
                        r = slice(RW_E * par, RW_E * (par + 1))
                        ins = dve.tensor_tensor(state[r], bank[r, :, RW_E * par:RW_E * (par + 1)],
                                                sdec[r].unsqueeze(2).to_broadcast([RW_E, PAIRS, RW_E]), mul)
                    units.emptied_by(("state", 0), ins, "V")
                    dve.drain()
                    dve.tensor_scalar(minus_state, state, -1.0, None, mul).then_inc(state_ready, 1)
            for step in range(len(LEVELS)):
                head_norm(1, step)
            dve.sem_inc(o_ready, 1)
            for u in range(2 * T):
                t, c = u // 2, u % 2
                bank = units.wait_full(("yrw", u))
                g = gates[:, t, D + c * 512:D + (c + 1) * 512]
                units.emptied_by(("yrw", u), dve.tensor_tensor(g, bank, g, mul), "V")
            dve.drain()
            dve.tensor_tensor(gates[:, :, 0:D], gates[:, :, 0:D], gates[:, :, D:2 * D], add).then_inc(mixed, 1)
            for c in range(2):
                for t in range(T):
                    bank = units.wait_full(("wout", T * c + t))
                    xc = x[:, t, c * 512:(c + 1) * 512]
                    units.emptied_by(("wout", T * c + t), dve.tensor_tensor(xc, bank, xc, add), "V")
            dve.wait_ge(std2_ready, 3)
            scale_rows(dve, [(x[:, t, :], xn2[:, t, :], t) for t in range(T)]).then_inc(xn2_ready, T)
            dve_transposed(dve, units, "tr2", gain2(KD))
            dve.wait_ge(route_loaded, 48)
            for t in range(T):
                bank = units.wait_full(("route", t))
                units.emptied_by(("route", t), dve.tensor_tensor(logits[:, t, :], bank[:, 0:EG + NE], b_route, add), "V")
            dve.drain()
            small = stat[:, 12:36]
            best, total, first1, second1 = (small[:, T * j:T * j + T] for j in range(4))
            pick = small[:, 8:8 + T]

            def first_of(values, n, m, hot, tmp):
                rank = second("rank")[:, EPG - n:EPG].unsqueeze(1).to_broadcast([P, T, n])
                dve.tensor_reduce(m, values, AX.X, ALU.max)
                dve.drain()
                dve.tensor_tensor(tmp, values, m.unsqueeze(2).to_broadcast([P, T, n]), ALU.is_equal)
                dve.drain()
                dve.tensor_tensor(tmp, tmp, rank, mul)
                dve.drain()
                dve.tensor_reduce(pick, tmp, AX.X, ALU.max)
                dve.drain()
                dve.tensor_tensor(hot, tmp, pick.unsqueeze(2).to_broadcast([P, T, n]), ALU.is_equal)
                dve.drain()

            tn = lambda a, n: a[:, 0:T * n].rearrange("p (t n) -> p t n", t=T)
            shifted_g, hot_g, tmp_g = tn(ra[0], EG), tn(ra[1], EG), tn(ra[7], EG)
            glog, elog = logits[:, :, 0:EG], logits[:, :, EG:].rearrange("p t (g e) -> p t g e", g=EG)
            first_of(glog, EG, best, hot_g, tmp_g)
            dve.tensor_tensor(shifted_g, glog, best.unsqueeze(2).to_broadcast([P, T, EG]), sub).then_inc(route_max, 1)
            full = ra[2].rearrange("p (t g e) -> p t g e", t=T, g=EG)
            dve.tensor_tensor(full, elog, hot_g.unsqueeze(3).to_broadcast([P, T, EG, EPG]), mul)
            dve.drain()
            chosen, hot1, hot2, tmp_e = tn(ra[3], EPG), tn(ra[4], EPG), tn(ra[6], EPG), tn(ra[7], EPG)
            dve.tensor_reduce(chosen, full.rearrange("p t g e -> p t e g"), AX.X, add)
            dve.drain()
            first_of(chosen, EPG, first1, hot1, tmp_e)
            dve.tensor_scalar(tmp_e, hot1, MASKED, None, mul)
            dve.drain()
            dve.tensor_tensor(chosen, chosen, tmp_e, add)
            dve.drain()
            first_of(chosen, EPG, second1, hot2, tmp_e)
            diff = ra[5][:, 0:T]
            dve.tensor_tensor(diff, second1, first1, sub).then_inc(pair_diff, 1)
            dve.wait_ge(route_exp, 1)
            dve.tensor_reduce(total, shifted_g, AX.X, add)
            dve.wait_ge(pair_exp, 1)
            dve.tensor_scalar(best, diff, 1.0, None, add)
            dve.drain()
            dve.tensor_tensor(total, total, best, mul)
            dve.drain()
            dve.reciprocal(first1, total)
            dve.drain()
            dve.tensor_tensor(second1, first1, diff, mul)
            dve.drain()
            dve.tensor_tensor(tmp_e, hot1, hot2, add)
            dve.drain()
            spread_e = lambda a, t: a[:, t, :].unsqueeze(1).to_broadcast([P, EG, EPG])
            spread_g = lambda t: hot_g[:, t, :].unsqueeze(2).to_broadcast([P, EG, EPG])
            for t in range(T):
                ins = dve.tensor_tensor(taken[:, t, :].rearrange("p (g e) -> p g e", g=EG), spread_g(t), spread_e(tmp_e, t), mul)
            ins.then_inc(taken_ready, 1)
            dve.tensor_tensor(hot1, hot1, first1.unsqueeze(2).to_broadcast([P, T, EPG]), mul)
            dve.tensor_tensor(hot2, hot2, second1.unsqueeze(2).to_broadcast([P, T, EPG]), mul)
            dve.drain()
            dve.tensor_tensor(hot1, hot1, hot2, add)
            dve.drain()
            for t in range(T):
                for q_ in range(PASSES):
                    dve.tensor_tensor(gate_tab[:, q_, :, t].rearrange("p (g e) -> p g e", g=EG), spread_g(t), spread_e(hot1, t), mul)
            units.wait_full(("rank", T))
            for t in range(T):
                bank = units.wait_full(("rank", t))
                units.emptied_by(("rank", t), dve.tensor_tensor(taken[:, t, :], bank[:, 0:NE], taken[:, t, :], mul), "V")
            bank = units.wait_full(("rank", T))
            units.emptied_by(("rank", T), dve.tensor_reduce(fullest[:, 0:1], bank[:, 0:NE], AX.X, ALU.max), "V")
            dve.drain()
            for t in range(T):
                for q_ in range(PASSES):
                    dve.tensor_scalar(place[:, q_, :, t], taken[:, t, :], -1.0 - q_ * SLOTS_E, None, add)
            for q_ in range(1, PASSES):
                dve.tensor_scalar(fullest[:, q_:q_ + 1], fullest[:, 0:1], q_ * SLOTS_E + 0.5, float(TURNS), ALU.is_gt, mul)
            dve.drain()
            dve.tensor_reduce(turns_f, fullest[:, 1:PASSES], AX.X, add)
            dve.drain()
            dve.tensor_scalar(turns_i[:], turns_f, float(TURNS), None, add)
            dve.drain()
            dve.sem_inc(places_ready, 1)
            dve.wait_ge(places_ready, 1)
            places = second("places")
            table = lambda a, turn: a.rearrange("p q e t -> p (q e) t")[:, bass.ds(turn * EPT, EPT), :]
            with dve.Fori(0, dve.value_load(turns_i[0:1, 0:1], min_val=TURNS, max_val=TURNS * PASSES)) as turn:
                units = UnitView(EU, dve, psum, turn)
                dve.tensor_copy(place_now, table(place, turn))
                dve.tensor_copy(gate_now, table(gate_tab, turn))
                dve.drain()
                for t in range(T):
                    for j in range(EPT):
                        at, g = place_now[:, j, t:t + 1], gate_now[:, j, t:t + 1]
                        dve.tensor_scalar(take[:, t, j, :], places, at, None, ALU.is_equal)
                        ins = dve.tensor_scalar(give[:, t, j, :], places, at, g, ALU.is_equal, mul)
                ins.then_inc(take_ready.sem, 1)
                for i in range(2):
                    bank = units.wait_full(("gx", i)).rearrange("p (k n) -> p k n", k=4)
                    norm2 = gains[:, KD + 4 * i:KD + 4 * i + 4].unsqueeze(2).to_broadcast([P, 4, P])
                    units.emptied_by(("gx", i), dve.tensor_tensor(xe[:, 4 * i:4 * i + 4, :], bank, norm2, mul), "V")
                bank = units.wait_full(("up", 0))
                units.wait_emptied(("gate", 0))
                units.emptied_by(("up", 0), dve.tensor_tensor(hid, bank, silu_g, mul), "V")
                bank = units.wait_full(("y", 1))
                units.emptied_by(("y", 1), dve.tensor_copy(y_rows[:, 512:D], bank), "V")
                dve.drain()
            final = UnitView(FU, dve, psum)
            for u in range(2 * T):
                t, c = u // 2, u % 2
                bank = final.wait_full(("acc", u))
                xc = x[:, t, c * 512:(c + 1) * 512]
                final.emptied_by(("acc", u), dve.tensor_tensor(xc, bank, xc, add), "V")
            dve.drain()
            dve.sem_inc(moe_done, 1)


def kernel(**inputs):
    import concourse.bacc as bacc
    from concourse.bass_utils import run_bass_kernel_spmd as run

    nc = bacc.Bacc("TRN2", target_bir_lowering=False, num_devices=1)
    tables = shape_tables()
    arrays = {name: np.ascontiguousarray(a) for name, a in inputs.items() if name not in SMALL}
    cols = lambda a: np.asarray(a).reshape(DEPTH, -1, P).transpose(0, 2, 1)
    arrays["gains"] = np.ascontiguousarray(np.concatenate(
        [cols(inputs[n]) for n in ("g_mix", "g_q", "g_kv", "g_mlp", "g_ret")], axis=2))
    arrays["gains2"] = np.ascontiguousarray(np.concatenate(
        [np.asarray(inputs[n]).reshape(-1, P).T for n in ("norm1_gain_2", "norm2_gain_2")], axis=1))
    arrays["rows2"] = np.concatenate([np.asarray(inputs[n]).reshape(-1) for n in ROW_INPUTS])[None]
    for name, names in (("shared_c", SHARED), ("first_c", FIRST), ("second_c", SECOND)):
        arrays[name] = pack(tables, names)
    io = {n: nc.dram_tensor(f"in_{n}", a.shape, F32, kind="ExternalInput").ap() for n, a in arrays.items()}
    out = nc.dram_tensor("out", (1, SEQ, D), F32, kind="ExternalOutput").ap()
    program(nc, io, out)
    return run(nc, [{f"in_{n}": a for n, a in arrays.items()}], core_ids=[0]).results[0]["out"]


ROW_INPUTS = ("rwkv_shift_mu_2", "rwkv_w0_2", "rwkv_a0_2", "rwkv_k_k_2", "rwkv_k_a_2", "rwkv_r_k_2", "rwkv_ln_w_2",
              "rwkv_ln_b_2", "q_norm_gain_2", "k_norm_gain_2", "g_final", "b_group_router_2", "b_expert_router_2")
SMALL = ("g_mix", "g_q", "g_kv", "g_mlp", "g_ret", "norm1_gain_2", "norm2_gain_2") + ROW_INPUTS
```
